# Optimizing a Trainium2 kernel written in Bass

```python
import math
import jax, jax.numpy as jnp
from jax import lax
import numpy as np

D_MODEL = 1024
BATCH = 1
SEQ = 512
DEPTH = 2

GRID_W = 64
Q_BLOCK = 128
NORM_EPS = 1e-6
ROPE_THETA = 10000.0

HY_D = 256
HY_ORDER = 2
HY_EMB = 33
HY_BANDS = (HY_EMB - 1) // 2
HY_FILTER_HIDDEN = 64
HY_DECAY_TARGET = 1e-2
HY_FAST_DECAY_PCT = 0.3
HY_SLOW_DECAY_PCT = 1.5

GQA_HEADS = 8
GQA_KV_HEADS = 2
GQA_HEAD_DIM = 64

MLA_HEADS = 4
MLA_Q_RANK = 256
MLA_KV_RANK = 128
MLA_NOPE_DIM = 64
MLA_ROPE_DIM = 32
MLA_V_DIM = 64

D_MIX = HY_D + GQA_HEADS * GQA_HEAD_DIM + MLA_HEADS * MLA_V_DIM

D_FF = 2816

IN_SPLITS = ((HY_ORDER + 1) * HY_D, GQA_HEADS * GQA_HEAD_DIM, GQA_KV_HEADS * GQA_HEAD_DIM,
             GQA_KV_HEADS * GQA_HEAD_DIM, MLA_Q_RANK, MLA_KV_RANK, MLA_ROPE_DIM)
D_IN = 1952

kernel_name = 'hybrid_hyena_gqa_mla_encoder'

F32 = jnp.float32

def rms_norm(x, g):
    xf = x.astype(F32)
    y = xf * lax.rsqrt(jnp.mean(xf * xf, axis=-1, keepdims=True) + NORM_EPS)
    return (y * g.astype(F32)).astype(x.dtype)

def dwconv3(x, w, b):
    xp = jnp.pad(x, ((0, 0), (1, 1), (0, 0)))
    return xp[:, :-2] * w[0] + xp[:, 1:-1] * w[1] + xp[:, 2:] * w[2] + b

def axial_rope_tables(row_idx, col_idx, rot_dim):
    n_axis = rot_dim // 4
    inv = ROPE_THETA ** (-jnp.arange(n_axis, dtype=F32) / n_axis)
    ang = jnp.concatenate([row_idx[:, None].astype(F32) * inv,
                           col_idx[:, None].astype(F32) * inv], axis=-1)
    return jnp.cos(ang), jnp.sin(ang)

def apply_rope(x, cos, sin):
    x1, x2 = jnp.split(x.astype(F32), 2, axis=-1)
    return jnp.concatenate([x1 * cos - x2 * sin, x1 * sin + x2 * cos], axis=-1).astype(x.dtype)

def hyena_position_features(L):
    t = jnp.linspace(0.0, 1.0, L, dtype=F32)[:, None]
    w = 2.0 * math.pi * jnp.arange(L, dtype=F32)[:, None] / L
    f = jnp.linspace(1e-4, HY_BANDS - 1, HY_BANDS, dtype=F32)[None, :]
    z = jnp.concatenate([t, jnp.cos(f * w), -jnp.sin(f * w)], axis=-1)
    max_decay = math.log(HY_DECAY_TARGET) / HY_FAST_DECAY_PCT
    min_decay = math.log(HY_DECAY_TARGET) / HY_SLOW_DECAY_PCT
    deltas = jnp.linspace(min_decay, max_decay, HY_D, dtype=F32)
    window = jnp.exp(-t * jnp.abs(deltas)[None, :])
    return z, window

def hyena_filters(z, window, w1, b1, f1, w2, b2, f2, w3):
    h = jnp.sin(f1.astype(F32) * (z @ w1.astype(F32) + b1.astype(F32)))
    h = jnp.sin(f2.astype(F32) * (h @ w2.astype(F32) + b2.astype(F32)))
    h = (h @ w3.astype(F32)).reshape(-1, HY_ORDER, 2, HY_D)
    return h * window[:, None, None, :]

def bidir_fftconv(u, h_fwd, h_bwd, skip):
    L = u.shape[1]
    k = jnp.concatenate([h_fwd, h_bwd[::-1]], axis=0)
    uf = jnp.fft.rfft(u.astype(F32), n=2 * L, axis=1)
    kf = jnp.fft.rfft(k, axis=0)
    y = jnp.fft.irfft(uf * kf[None], n=2 * L, axis=1)[:, :L]
    return (y + u.astype(F32) * skip.astype(F32)).astype(u.dtype)

def hyena_mixer(u, conv_w, conv_b, filters, skip):
    uc = dwconv3(u, conv_w, conv_b)
    v, x1, x2 = jnp.split(uc, 3, axis=-1)
    z = v
    for i, gate in enumerate((x1, x2)):
        z = gate * bidir_fftconv(z, filters[:, i, 0], filters[:, i, 1], skip[i])
    return z

def gqa_attention(q, k, v, scale):
    B, L, Hq, d = q.shape
    Hkv = k.shape[2]
    G = Hq // Hkv
    nb = L // Q_BLOCK
    qb = q.reshape(B, nb, Q_BLOCK, Hkv, G, d).transpose(1, 0, 3, 4, 2, 5)

    def one_block(qi):
        s = jnp.einsum('bkgqd,bskd->bkgqs', qi, k, preferred_element_type=F32) * scale
        p = jax.nn.softmax(s, axis=-1).astype(v.dtype)
        return jnp.einsum('bkgqs,bskd->bkgqd', p, v)

    o = lax.map(one_block, qb)
    return o.transpose(1, 0, 4, 2, 3, 5).reshape(B, L, Hq * d)

def mla_attention(q_nope, q_pe, k_nope, k_pe, v, scale):
    B, L, H, dn = q_nope.shape
    dr = q_pe.shape[-1]
    dv = v.shape[-1]
    nb = L // Q_BLOCK
    qn = q_nope.reshape(B, nb, Q_BLOCK, H, dn).transpose(1, 0, 3, 2, 4)
    qr = q_pe.reshape(B, nb, Q_BLOCK, H, dr).transpose(1, 0, 3, 2, 4)

    def one_block(args):
        qn_i, qr_i = args
        s = (jnp.einsum('bhqd,bshd->bhqs', qn_i, k_nope, preferred_element_type=F32)
             + jnp.einsum('bhqr,bsr->bhqs', qr_i, k_pe, preferred_element_type=F32)) * scale
        p = jax.nn.softmax(s, axis=-1).astype(v.dtype)
        return jnp.einsum('bhqs,bshd->bhqd', p, v)

    o = lax.map(one_block, (qn, qr))
    return o.transpose(1, 0, 3, 2, 4).reshape(B, L, H * dv)

def setup_inputs(seed: int = 0) -> dict:
    key = jax.random.key(seed)
    ks = jax.random.split(key, 30)

    def nrm(k, shape, scale):
        return jax.random.normal(k, shape, F32) * scale

    def gain(k, n):
        return 1.0 + 0.05 * jax.random.normal(k, (DEPTH, n), F32)

    hy_cols = (HY_ORDER + 1) * HY_D
    return {
        'x': nrm(ks[0], (BATCH, SEQ, D_MODEL), 1.0),
        'mix_pre_norm': gain(ks[1], D_MODEL),
        'w_in': nrm(ks[2], (DEPTH, D_MODEL, D_IN), D_MODEL ** -0.5),
        'hy_conv_w': nrm(ks[3], (DEPTH, 3, hy_cols), 3 ** -0.5),
        'hy_conv_b': nrm(ks[4], (DEPTH, hy_cols), 0.01),
        'hy_filt_w1': nrm(ks[5], (DEPTH, HY_EMB, HY_FILTER_HIDDEN), HY_EMB ** -0.5),
        'hy_filt_b1': nrm(ks[6], (DEPTH, HY_FILTER_HIDDEN), 0.1),
        'hy_filt_freq1': gain(ks[7], HY_FILTER_HIDDEN),
        'hy_filt_w2': nrm(ks[8], (DEPTH, HY_FILTER_HIDDEN, HY_FILTER_HIDDEN), HY_FILTER_HIDDEN ** -0.5),
        'hy_filt_b2': nrm(ks[9], (DEPTH, HY_FILTER_HIDDEN), 0.1),
        'hy_filt_freq2': gain(ks[10], HY_FILTER_HIDDEN),
        'hy_filt_w3': nrm(ks[11], (DEPTH, HY_FILTER_HIDDEN, HY_ORDER * 2 * HY_D), HY_FILTER_HIDDEN ** -0.5),
        'hy_skip': nrm(ks[12], (DEPTH, HY_ORDER, HY_D), 0.5),
        'gqa_q_norm': gain(ks[13], GQA_HEAD_DIM),
        'gqa_k_norm': gain(ks[14], GQA_HEAD_DIM),
        'mla_q_a_norm': gain(ks[15], MLA_Q_RANK),
        'mla_w_uq': nrm(ks[16], (DEPTH, MLA_Q_RANK, MLA_HEADS * (MLA_NOPE_DIM + MLA_ROPE_DIM)), MLA_Q_RANK ** -0.5),
        'mla_kv_a_norm': gain(ks[17], MLA_KV_RANK),
        'mla_w_ukv': nrm(ks[18], (DEPTH, MLA_KV_RANK, MLA_HEADS * (MLA_NOPE_DIM + MLA_V_DIM)), MLA_KV_RANK ** -0.5),
        'hy_out_norm': gain(ks[19], HY_D),
        'gqa_out_norm': gain(ks[20], GQA_HEADS * GQA_HEAD_DIM),
        'mla_out_norm': gain(ks[21], MLA_HEADS * MLA_V_DIM),
        'w_out': nrm(ks[22], (DEPTH, D_MIX, D_MODEL), D_MIX ** -0.5),
        'mix_post_norm': gain(ks[23], D_MODEL),
        'ffn_pre_norm': gain(ks[24], D_MODEL),
        'w_up': nrm(ks[25], (DEPTH, D_MODEL, 2 * D_FF), D_MODEL ** -0.5),
        'ffn_conv_w': nrm(ks[26], (DEPTH, 3, 2 * D_FF), 3 ** -0.5),
        'ffn_conv_b': nrm(ks[27], (DEPTH, 2 * D_FF), 0.01),
        'w_down': nrm(ks[28], (DEPTH, D_FF, D_MODEL), D_FF ** -0.5),
        'ffn_post_norm': gain(ks[29], D_MODEL),
    }

def reference(x, mix_pre_norm, w_in, hy_conv_w, hy_conv_b, hy_filt_w1, hy_filt_b1, hy_filt_freq1,
              hy_filt_w2, hy_filt_b2, hy_filt_freq2, hy_filt_w3, hy_skip, gqa_q_norm, gqa_k_norm,
              mla_q_a_norm, mla_w_uq, mla_kv_a_norm, mla_w_ukv, hy_out_norm, gqa_out_norm,
              mla_out_norm, w_out, mix_post_norm, ffn_pre_norm, w_up, ffn_conv_w, ffn_conv_b,
              w_down, ffn_post_norm):
    B, L, _ = x.shape
    rows = L // GRID_W
    row_idx = jnp.broadcast_to(jnp.arange(rows)[:, None], (rows, GRID_W)).reshape(L)
    col_idx = jnp.broadcast_to(jnp.arange(GRID_W)[None, :], (rows, GRID_W)).reshape(L)

    cos_g, sin_g = axial_rope_tables(row_idx, col_idx, GQA_HEAD_DIM)
    cos_m, sin_m = axial_rope_tables(row_idx, col_idx, MLA_ROPE_DIM)
    z_pos, window = hyena_position_features(L)
    offsets = [int(o) for o in np.cumsum(IN_SPLITS)[:-1]]

    for l in range(DEPTH):
        h = rms_norm(x, mix_pre_norm[l])
        proj = h @ w_in[l]
        hy_in, gq, gk, gv, mq, mkv, mkr = jnp.split(proj, offsets, axis=-1)

        filters = hyena_filters(z_pos, window, hy_filt_w1[l], hy_filt_b1[l], hy_filt_freq1[l],
                                hy_filt_w2[l], hy_filt_b2[l], hy_filt_freq2[l], hy_filt_w3[l])
        y_hy = hyena_mixer(hy_in, hy_conv_w[l], hy_conv_b[l], filters, hy_skip[l])

        q = rms_norm(gq.reshape(B, L, GQA_HEADS, GQA_HEAD_DIM), gqa_q_norm[l])
        k = rms_norm(gk.reshape(B, L, GQA_KV_HEADS, GQA_HEAD_DIM), gqa_k_norm[l])
        q = apply_rope(q, cos_g[:, None, :], sin_g[:, None, :])
        k = apply_rope(k, cos_g[:, None, :], sin_g[:, None, :])
        v = gv.reshape(B, L, GQA_KV_HEADS, GQA_HEAD_DIM)
        y_gqa = gqa_attention(q, k, v, GQA_HEAD_DIM ** -0.5)

        cq = rms_norm(mq, mla_q_a_norm[l])
        qm = (cq @ mla_w_uq[l]).reshape(B, L, MLA_HEADS, MLA_NOPE_DIM + MLA_ROPE_DIM)
        q_nope, q_pe = jnp.split(qm, [MLA_NOPE_DIM], axis=-1)
        q_pe = apply_rope(q_pe, cos_m[:, None, :], sin_m[:, None, :])
        ckv = rms_norm(mkv, mla_kv_a_norm[l])
        kv = (ckv @ mla_w_ukv[l]).reshape(B, L, MLA_HEADS, MLA_NOPE_DIM + MLA_V_DIM)
        k_nope, v_m = jnp.split(kv, [MLA_NOPE_DIM], axis=-1)
        k_pe = apply_rope(mkr, cos_m, sin_m)
        y_mla = mla_attention(q_nope, q_pe, k_nope, k_pe, v_m,
                              (MLA_NOPE_DIM + MLA_ROPE_DIM) ** -0.5)

        groups = jnp.concatenate([rms_norm(y_hy, hy_out_norm[l]),
                                  rms_norm(y_gqa, gqa_out_norm[l]),
                                  rms_norm(y_mla, mla_out_norm[l])], axis=-1)
        x = x + rms_norm(groups @ w_out[l], mix_post_norm[l])

        h = rms_norm(x, ffn_pre_norm[l])
        up = dwconv3(h @ w_up[l], ffn_conv_w[l], ffn_conv_b[l])
        gate, val = jnp.split(up, 2, axis=-1)
        f = (jax.nn.gelu(gate, approximate=True) * val) @ w_down[l]
        x = x + rms_norm(f, ffn_post_norm[l])
    return x


_drawn_inputs = setup_inputs


def setup_inputs(seed=0):
    import zlib

    import numpy as np

    out = dict(_drawn_inputs(seed))
    spreads = {}
    factors = {'ffn_conv_b': 4.513}
    for name, (base, spread) in spreads.items():
        noise = np.random.default_rng([zlib.crc32(name.encode()), seed]).standard_normal(out[name].shape)
        drawn = base * np.exp(spread * noise) if base else spread * noise
        out[name] = __import__('jax').numpy.asarray(drawn.astype(out[name].dtype))
    for name, factor in factors.items():
        out[name] = (out[name] * factor).astype(out[name].dtype)
    return out
```

```python
from contextlib import ExitStack

import concourse.bass as bass
import numpy as np
from concourse import mybir

F32 = mybir.dt.float32
F32R = mybir.dt.float32r
ACT = mybir.ActivationFunctionType
ALU = mybir.AluOpType
AX = mybir.AxisListType

P = 128
DM, T, DEPTH = 1024, 512, 2
DC = DM // P
TC = T // P
GRID_W = 64
EPS = 1e-6
HD, HEMB, HHID = 256, 33, 64
GH, GKV, GD = 8, 2, 64
MH, MQR, MKVR, MN, MR, MV = 4, 256, 128, 64, 32, 64
MD = MN + MR
DFF = 2816
FC = DFF // P
D_IN = 3 * HD + GH * GD + 2 * GKV * GD + MQR + MKVR + MR
NF = T // 2

WIN = -(-D_IN // P)
C_Q = 3 * HD // P
C_K = C_Q + GH * GD // P
C_V = C_K + 1
C_MQ = C_V + 1
C_MKV = C_MQ + MQR // P
C_MKR = C_MKV + 1
assert C_MKR == WIN - 1 and D_IN - C_MKR * P == MR

ITEM = 8
I_OUT = WIN
I_UP = I_OUT + DC
I_DOWN = I_UP + 2 * FC
DOWN_PARTS = [(k, min(ITEM, FC - k)) for k in range(0, FC, ITEM)]
ITEMS = I_DOWN + DC * len(DOWN_PARTS)
assert I_OUT % 2 == 0 and I_UP % 2 == 0 and I_DOWN % 2 == 0 and ITEMS % 2 == 0

PM = {}
_at = 0
for _name, _n in (("mix_pre", DC), ("hy_w", 18), ("hy_b", 6), ("skip", 4), ("mqa", 2), ("mkva", 1),
                  ("g_out", DC), ("mix_post", DC), ("ffn_pre", DC), ("ffn_post", DC), ("gq", 1), ("gk", 1)):
    PM[_name] = _at
    _at += _n
PM_A = _at
PM["ffn_w0"], PM["ffn_w1"], PM["ffn_w2"], PM["ffn_b"] = P, P + 2 * FC, 2 * P, 2 * P + 2 * FC
PM_ROWS = [PM_A, 4 * FC, 4 * FC]
PML = 3 * P

MAGIC = 1.5 * 2.0 ** 23
PI2 = (6.28125, 0.0019350051879882812, 3.019916e-07)
PI = 3.1415925


class Chain:

    def __init__(self, eng, sem):
        self.eng, self.sem, self.n = eng, sem, 0

    def do(self, ins):
        ins.then_inc(self.sem, 1)
        self.n += 1

    def join(self):
        self.eng.wait_ge(self.sem, self.n)

    def restart(self):
        self.eng.sem_clear(self.sem)
        self.n = 0


def build(nc, a, out):
    ctx = ExitStack()
    with ctx:
        def sb(name, shape, dt=F32, scope=ctx):
            return scope.enter_context(nc.sbuf_tensor(name, shape, dt))

        def sem(name):
            return ctx.enter_context(nc.semaphore(name))

        xT = sb("xT", [P, DC, T])
        raw = sb("raw", [P, 2, ITEM * P])
        wh = sb("wh", [P, 2, ITEM * P], F32R)
        wl = sb("wl", [P, 2, ITEM * P], F32R)
        ident = sb("ident", [P, P])
        ones = sb("ones", [P, P])
        b64 = sb("b64", [P, P])
        perm_g = sb("perm_g", [P, P])
        perm_m = sb("perm_m", [MD, MD])
        rope = sb("rope", [P, 4, T])
        rbc = sb("rbc", [P, T])
        std = sb("std", [P, T])
        rr = sb("rr", [P, T])
        sq = sb("sq", [P, 2, T])
        acc = sb("acc", [P, T])
        yt = sb("yt", [P, 2, T])
        pad = sb("pad", [P, 2, T + 2])
        cv = sb("cv", [P, 2, T])
        pm = sb("pm", [P, DEPTH * PML])
        zT = sb("zT", [HEMB, T])
        h2 = sb("h2", [P, T + 4])
        w3 = sb("w3", [P, 4 * HD])
        fw1 = sb("fw1", [HEMB, DEPTH, HHID])
        fw2 = sb("fw2", [HHID, DEPTH, HHID])
        fbf = sb("fbf", [HHID, 4, DEPTH])
        fwl = sb("fwl", [HHID, 2, P])
        eps = sb("eps", [P, 1])
        nm = sb("nm", [P, 2, TC])
        ns = sb("ns", [P, 2, TC])

        with ExitStack() as s:
            gh = sb("gh", [P, DC, T], F32R, s)
            gl = sb("gl", [P, DC, T], F32R, s)
        prob = sb("prob", [P, 2, TC, T])
        probT = sb("probT", [P, TC, T])
        mqf = sb("mqf", [P, MH, T])

        with ExitStack() as s:
            fh = sb("fh", [P, FC, T], F32R, s)
            fl = sb("fl", [P, FC, T], F32R, s)
            gact = sb("gact", [P, T], F32, s)
            fprod = sb("fprod", [P, T], F32, s)
        with ExitStack() as s:
            xio = sb("xio", [P, TC, DM], F32, s)
            pstage = sb("pstage", [P, 3 * DEPTH, P], F32, s)
        uc = sb("uc", [P, 6, T])
        qf = sb("qf", [P, GH // 2, T])
        ka = sb("ka", [P, GKV, T], F32R)
        kb = sb("kb", [P, GKV, T], F32R)
        vg = sb("vg", [P, TC, 3 * GD])
        cq = sb("cq", [P, 2, T])
        ckv = sb("ckv", [P, T])
        kr = sb("kr", [P, T])
        with ExitStack() as s:
            TF = sb("TF", [P, 2, 2, T], F32, s)
            TI = sb("TI", [P, 2, 4, NF], F32, s)
            KP = sb("KP", [P, 2, 2, T], F32, s)
            KM = sb("KM", [P, 2, 2, T], F32, s)
            with ExitStack() as s2:
                h1 = sb("h1", [HHID, T], F32, s2)
                arg = sb("arg", [HHID, 2, T], F32, s2)
                win = sb("win", [P, 2, 4, HD], F32, s2)
                hsum = sb("hsum", [P, 4, T], F32, s2)
                hdif = sb("hdif", [P, 4, T], F32, s2)
            with ExitStack() as s2:
                ut = sb("ut", [P, 4, HD], F32, s2)
                ebuf = sb("ebuf", [P, 2, T], F32, s2)
                fa = sb("fa", [P, 2, T], F32, s2)
                fb = sb("fb", [P, 2, T], F32, s2)
                p1 = sb("p1", [P, 2, T], F32, s2)
                p2 = sb("p2", [P, 2, T], F32, s2)
                ya = sb("ya", [P, 2, T], F32, s2)
                yb = sb("yb", [P, 2, T], F32, s2)
        with ExitStack() as s:
            q2 = sb("q2", [P, 2, T], F32R, s)
            mkf = sb("mkf", [P, MH, T], F32, s)
            mv = sb("mv", [P, TC, 2, 3 * MV], F32, s)
            uqr = sb("uqr", [P, 2, MH * MD], F32, s)
            uqh = sb("uqh", [P, 2, MH * MD], F32R, s)
            uql = sb("uql", [P, 2, MH * MD], F32R, s)
            ukr = sb("ukr", [P, T], F32, s)
            ukh = sb("ukh", [P, T], F32R, s)
            ukl = sb("ukl", [P, T], F32R, s)
            cqh = sb("cqh", [P, 2, T], F32R, s)
            cql = sb("cql", [P, 2, T], F32R, s)
            ckh = sb("ckh", [P, T], F32R, s)
            ckl = sb("ckl", [P, T], F32R, s)

        ps = ctx.enter_context(nc.psum_tensor("ps", [P, 8, T], F32))

        S = {}
        for name in ("const_in", "x_in", "par_in", "filt_in", "tab_in", "mla_in", "raw0", "raw1", "out_sem",
                     "hi_ready", "lo_ready", "pe_item", "x_tr", "x_first", "par_tr", "par_ok", "const_ok",
                     "gh_ready", "gl_ready", "xsq", "xsq_used", "stat_pre", "std_pre", "rbc_ready",
                     "ysq", "ysq_used", "ycopy", "stat_post", "std_post", "x_new",
                     "evac", "conv1", "conv_done", "nsq", "nstat", "nstd", "nrm", "nperm", "roped", "vtr", "vcopy",
                     "khi", "klo",
                     "fw_ok", "f_mm", "f_arg", "f_sin", "fc_mm", "fc_done", "fd_mm", "fd_copy", "fd_done",
                     "ha_mm", "hu_copy", "he_mm", "ho_mm", "he_copy", "h_prod", "hc_mm", "h_done",
                     "q2hi", "q2lo", "s_tile", "nmax", "p_ready", "pt_tile", "pt_act", "pt_dve", "pv", "y_head",
                     "mhi", "mlo", "kr_copy", "b7_full", "b7_free",
                     "gsq", "gsq_used", "gstat", "gstd", "y_norm", "ygh", "ygl",
                     "f_evac", "f_conv1", "f_conv", "f_gelu", "f_prod", "f_hi", "f_lo",
                     "o_tr", "o_copy", "dve_self", "pe_marks", "dve_marks"):
            S[name] = sem(name)
        dve_self = S["dve_self"]

        def mark(eng, name):
            eng.sem_inc(S[name], 1)

        block = ctx.enter_context(nc.Block())

        def one(w, lay):
            return w[bass.ds(lay, 1)]

        GROUPS = [(uc, 0, 2, 0), (qf, 0, 4, 2), (cq, 0, 2, 6)]
        B7 = []
        for hh in range(MH):
            B7 += [("q", hh), ("perm", hh), ("k", hh)]
        B7 += [("v", s) for s in range(TC)]
        B7_AT = {h: B7[1 + 3 * (h - 1):1 + 3 * h] if h else B7[:1] for h in range(6)}
        assert sum(len(v) for v in B7_AT.values()) == len(B7)
        HEADS = GH + MH

        @block.sync
        def _(sp):
            tok = a["x"].rearrange("b (c p) d -> p (b c) d", p=P)
            sp.dma_start(xio[:], tok).then_inc(S["x_in"], 16)
            for dst, src in ((ident, "c_ident"), (b64, "c_b64"), (perm_g, "c_perm_g"), (perm_m, "c_perm_m"),
                             (rope, "c_rope"), (zT, "c_z")):
                sp.dma_start(dst[:], a[src]).then_inc(S["const_in"], 16)
            for l in range(DEPTH):
                for i, n in enumerate(("hy_filt_b1", "hy_filt_freq1", "hy_filt_b2", "hy_filt_freq2")):
                    sp.dma_start(fbf[:, i, l:l + 1], a[n][l].rearrange("(n o) -> n o", o=1)).then_inc(S["const_in"], 16)
            sp.dma_start(fw1[:], a["hy_filt_w1"].rearrange("l k n -> k l n")).then_inc(S["const_in"], 16)
            sp.dma_start(fw2[:], a["hy_filt_w2"].rearrange("l k n -> k l n")).then_inc(S["const_in"], 16)
            for l in range(DEPTH):
                nxt = (l + 1) % DEPTH
                rows = [("mix_pre", a["mix_pre_norm"][nxt]), ("hy_w", a["hy_conv_w"][l].rearrange("k n -> (k n)")),
                        ("hy_b", a["hy_conv_b"][l]), ("skip", a["hy_skip"][l].rearrange("k n -> (k n)")),
                        ("mqa", a["mla_q_a_norm"][l]), ("mkva", a["mla_kv_a_norm"][l]),
                        ("mix_post", a["mix_post_norm"][l]), ("ffn_pre", a["ffn_pre_norm"][l]),
                        ("ffn_post", a["ffn_post_norm"][l])]
                for n, v in rows:
                    k = v.shape[0] // P
                    sp.dma_start(pstage[PM[n]:PM[n] + k, 3 * l, :], v.rearrange("(k p) -> k p", p=P)).then_inc(S["par_in"], 16)
                g0 = PM["g_out"]
                for n, o, k in (("hy_out_norm", 0, 2), ("gqa_out_norm", 2, 4), ("mla_out_norm", 6, 2)):
                    sp.dma_start(pstage[g0 + o:g0 + o + k, 3 * l, :],
                                 a[n][l].rearrange("(k p) -> k p", p=P)).then_inc(S["par_in"], 16)
                for n, m in (("gqa_q_norm", "gq"), ("gqa_k_norm", "gk")):
                    for half in range(2):
                        sp.dma_start(pstage[PM[m]:PM[m] + 1, 3 * l, half * GD:(half + 1) * GD],
                                     a[n][l:l + 1, :]).then_inc(S["par_in"], 16)
                fw = a["ffn_conv_w"][l].rearrange("k (c p) -> k c p", p=P)
                for k, (tile, row) in enumerate(((1, 0), (1, 2 * FC), (2, 0))):
                    sp.dma_start(pstage[row:row + 2 * FC, 3 * l + tile, :], fw[k]).then_inc(S["par_in"], 16)
                sp.dma_start(pstage[2 * FC:4 * FC, 3 * l + 2, :],
                             a["ffn_conv_b"][l].rearrange("(c p) -> c p", p=P)).then_inc(S["par_in"], 16)

            w_in = a["w_in"].rearrange("l (c p) n -> l p c n", p=P)
            w_out = a["w_out"].rearrange("l (c p) n -> l p c n", p=P)
            w_up = a["w_up"].rearrange("l (c p) n -> l p c n", p=P)
            w_down = a["w_down"].rearrange("l (c p) n -> l p c n", p=P)

            def item(lay, n, src, tiles=ITEM, cols=P):
                slot = item.slot
                item.slot = 1 - slot
                sp.wait_ge(S["lo_ready"], lay * ITEMS + n + 1)
                dst = raw[:, slot, :].rearrange("p (c n) -> p c n", n=P)[:, 0:tiles, 0:cols]
                sp.dma_start(dst, src.rearrange("o p c n -> (o p) c n")).then_inc(S[f"raw{slot}"], 16)

            item.slot = 0
            with sp.Fori(0, DEPTH) as lay:
                for i in range(2):
                    item(lay, i, w_in[bass.ds(lay, 1), :, :, i * P:(i + 1) * P])
                sp.wait_ge(S["rbc_ready"], lay * 2 + 1)
                sp.wait_ge(S["gl_ready"], lay * 2 * DC + DC)
                for lo in range(0, 4 * HD, T):
                    sp.dma_start(w3[0:HHID, lo:lo + T], one(a["hy_filt_w3"], lay).rearrange("o k n -> (o k) n")[:, lo:lo + T]
                                 ).then_inc(S["filt_in"], 16)
                sp.dma_start(win[:], a["c_win"]).then_inc(S["filt_in"], 16)
                for i in range(2, 4):
                    item(lay, i, w_in[bass.ds(lay, 1), :, :, i * P:(i + 1) * P])
                sp.dma_start(TF[:], a["c_tf"]).then_inc(S["tab_in"], 16)
                sp.dma_start(TI[:], a["c_ti"]).then_inc(S["tab_in"], 16)
                with sp.Fori(4, WIN - 3, 2) as i:
                    for j in range(2):
                        item(lay, i + j, w_in[bass.ds(lay, 1), :, :, bass.ds((i + j) * P, P)])
                for i in range(WIN - 2, WIN):
                    w = min(P, D_IN - i * P)
                    item(lay, i, w_in[bass.ds(lay, 1), :, :, i * P:i * P + w], cols=w)
                for i in range(2):
                    item(lay, I_OUT + i, w_out[bass.ds(lay, 1), :, :, i * P:(i + 1) * P])
                sp.wait_ge(S["h_done"], lay * 2 + 2)
                sp.dma_start(uqr[:], one(a["mla_w_uq"], lay).rearrange("o (c p) n -> (o p) c n", p=P)).then_inc(S["mla_in"], 16)
                sp.dma_start(ukr[:], one(a["mla_w_ukv"], lay).rearrange("o p n -> (o p) n")).then_inc(S["mla_in"], 16)
                with sp.Fori(2, DC - 1, 2) as i:
                    for j in range(2):
                        item(lay, I_OUT + i + j, w_out[bass.ds(lay, 1), :, :, bass.ds((i + j) * P, P)])
                with sp.Fori(0, FC) as j:
                    item(lay, I_UP + 2 * j, w_up[bass.ds(lay, 1), :, :, bass.ds(j * P, P)])
                    item(lay, I_UP + 2 * j + 1, w_up[bass.ds(lay, 1), :, :, bass.ds(DFF + j * P, P)])
                with sp.Fori(0, DC - 1, 2) as m:
                    for j in range(2):
                        for i, (k, n) in enumerate(DOWN_PARTS):
                            item(lay, I_DOWN + (m + j) * 3 + i,
                                 w_down[bass.ds(lay, 1), :, k:k + n, bass.ds((m + j) * P, P)], tiles=n)
            res = out.rearrange("b (c p) d -> p (b c) d", p=P)
            for c in range(TC):
                sp.wait_ge(S["o_copy"], 2 * c + 2)
                sp.dma_start(res[:, c, :], xio[:, c, :]).then_inc(S["out_sem"], 16)
            sp.wait_ge(S["out_sem"], 16 * TC)

        @block.gpsimd
        def _(pool):
            nc.gpsimd.memset(ones[:], 1.0)
            nc.gpsimd.memset(eps[:], EPS)
            nc.gpsimd.memset(h2[:], 0.0)
            nc.gpsimd.memset(w3[:], 0.0)
            nc.gpsimd.memset(pad[:], 0.0)
            nc.gpsimd.memset(fwl[:], 0.0)
            nc.gpsimd.memset(raw[:], 0.0).then_inc(S["const_ok"], 1)
            pool.wait_ge(S["const_ok"], 1)
            pool.sem_inc(S["lo_ready"], 2)
            with pool.Fori(0, DEPTH * ITEMS, 2) as n:
                for slot in range(2):
                    pool.wait_ge(S["hi_ready"], n + slot + 1)
                    nc.gpsimd.tensor_tensor(wl[:, slot, :], raw[:, slot, :], wh[:, slot, :].bitcast(F32),
                                            ALU.subtract).then_inc(S["lo_ready"], 1)

        @block.scalar
        def _(act):
            A = nc.scalar.activation

            def hi(lay, n, slot):
                g = lay * ITEMS + n
                act.wait_ge(S[f"raw{slot}"], lay * (8 * ITEMS) + n * 8 + (16 - 8 * slot))
                act.wait_ge(S["pe_item"], g + 1)
                A(wh[:, slot, :], raw[:, slot, :], ACT.Copy).then_inc(S["hi_ready"], 1)

            def prep(q, off, first=False):
                for c in range(DC):
                    if not first:
                        act.wait_ge(S["x_new"], (q - 1) * DC + c + 1)
                    A(gh[:, c, :], xT[:, c, :], ACT.Copy, scale=pm[:, bass.ds(off + c, 1)] if not isinstance(off, int)
                      else pm[:, off + c:off + c + 1]).then_inc(S["gh_ready"], 1)
                    if not (first and c < 2):
                        act.wait_ge(S["xsq_used"], q * DC + c - 1)
                    A(sq[:, c % 2, :], xT[:, c, :], ACT.Square).then_inc(S["xsq"], 1)
                act.wait_ge(S["stat_pre"], q + 1)
                A(std[:], ps[:, 1, :], ACT.Sqrt, bias=eps[:, 0:1], scale=1.0 / DM).then_inc(S["std_pre"], 1)

            def ysquare(lay, b, m):
                k = (lay * 2 + b) * DC + m
                if m >= 2:
                    act.wait_ge(S["ysq_used"], k - 1)
                A(sq[:, m % 2, :], ps[:, m, :], ACT.Square).then_inc(S["ysq"], 1)
                if m < 2:
                    A(yt[:, m, :], ps[:, m, :], ACT.Copy).then_inc(S["ycopy"], 1)

            def post(lay, b):
                act.wait_ge(S["stat_post"], lay * 2 + b + 1)
                A(std[:], ps[:, 0, :], ACT.Sqrt, bias=eps[:, 0:1], scale=1.0 / DM).then_inc(S["std_post"], 1)

            for c in range(DC):
                act.wait_ge(S["x_tr"], c + 1)
                A(xT[:, c, :], ps[:, c % 4, :], ACT.Copy).then_inc(S["x_first"], 1)
            for i in range(3 * DEPTH):
                act.wait_ge(S["par_tr"], i + 1)
                n = PM_ROWS[i % 3]
                A(pm[:, i * P:i * P + n], ps[:, 4 + i % 3, 0:n], ACT.Copy).then_inc(S["par_ok"], 1)
            act.wait_ge(S["x_first"], DC)
            act.wait_ge(S["par_ok"], 3 * DEPTH)
            act.wait_ge(S["const_ok"], 1)
            prep(0, (DEPTH - 1) * PML + PM["mix_pre"], first=True)

            with act.Fori(0, DEPTH) as lay:
                col = lay * PML

                def par(name, i=0):
                    return pm[:, bass.ds(col + (PM[name] + i), 1)]

                def sines(k):
                    dst = h1[:] if k == 0 else h2[0:HHID, 1:T + 1]
                    act.wait_ge(S["f_arg"], lay * 2 + k + 1)
                    A(dst, arg[:, 0, :], ACT.Sin).then_inc(S["f_sin"], 1)

                def conv1(i):
                    act.wait_ge(S["evac"], lay * WIN + i + 1)
                    A(uc[:, i, :], pad[:, i % 2, 1:T + 1], ACT.Identity, scale=par("hy_w", 6 + i),
                      bias=par("hy_b", i)).then_inc(S["conv1"], 1)

                nsq_n = [0]

                def squares(i, src):
                    act.wait_ge(S["evac"], lay * WIN + i + 1)
                    k = nsq_n[0]
                    nsq_n[0] += 1
                    if k >= 2:
                        act.wait_ge(S["nstat"], lay * 7 + {2: 1, 3: 2, 4: 3, 5: 4, 6: 5, 7: 6}[k])
                    A(sq[:, k % 2, :], src, ACT.Square).then_inc(S["nsq"], 1)

                def root(k, width):
                    if k:
                        act.wait_ge(S["nrm"], lay * 7 + k)
                    act.wait_ge(S["nstat"], lay * 7 + k + 1)
                    A(std[:], ps[:, 2, :], ACT.Sqrt, bias=eps[:, 0:1], scale=1.0 / width).then_inc(S["nstd"], 1)

                def filt_copy(k):
                    act.wait_ge(S["fd_mm"], lay * 8 + 2 * k + 1)
                    if k:
                        act.wait_ge(S["fd_done"], lay * 4 + k)
                    A(yt[:, 0, :], ps[:, 4 + 2 * (k % 2), :], ACT.Copy).then_inc(S["fd_copy"], 1)

                def u_copy(o):
                    act.wait_ge(S["ha_mm"], lay * 2 + o + 1)
                    A(ut[:].rearrange("p (b c) d -> p b (c d)", b=2), ps[:, 4:6, :], ACT.Copy).then_inc(S["hu_copy"], 1)

                def e_copy(o):
                    act.wait_ge(S["he_mm"], lay * 2 + o + 1)
                    A(ebuf[:], ps[:, 6:8, :], ACT.Copy).then_inc(S["he_copy"], 1)

                hi(lay, 0, 0)
                sines(0)
                for t in range(WIN + 2):
                    if t + 1 < I_OUT + 2:
                        hi(lay, t + 1, (t + 1) % 2)
                    if t == 0:
                        sines(1)
                    i = t - 1
                    if 0 <= i < C_Q:
                        conv1(i)
                    if C_Q <= i < C_K:
                        squares(i, qf[:, i - C_Q, :])
                    if i == C_K:
                        squares(i, cv[:, 0, :])
                    if i in (C_MQ, C_MQ + 1):
                        squares(i, cq[:, i - C_MQ, :])
                    if i == C_MKV:
                        squares(i, ckv[:])
                    if C_Q <= t - 2 <= C_K:
                        root(t - 2 - C_Q, GD)
                    if t == C_MQ + 3:
                        root(5, MQR)
                    if t == C_MKV + 2:
                        root(6, MKVR)
                    if t in (6, 7):
                        filt_copy(2 * (t - 6))
                        filt_copy(2 * (t - 6) + 1)
                    if t == 8:
                        u_copy(0)
                    if t == 9:
                        e_copy(0)
                    if t == 12:
                        u_copy(1)
                    if t == 13:
                        e_copy(1)
                act.wait_ge(S["roped"], lay * 6 + 5)
                for kv in range(GKV):
                    rows = slice(kv * GD, (kv + 1) * GD)
                    for half in range(2):
                        A(ka[half * GD:(half + 1) * GD, kv, :], cv[rows, 0, :], ACT.Copy).then_inc(S["khi"], 1)

                gsq_n = [0]

                def group(g):
                    src, c0, n, _ = GROUPS[g]
                    for c in range(n):
                        k = gsq_n[0]
                        gsq_n[0] += 1
                        if k >= 2:
                            act.wait_ge(S["gsq_used"], lay * DC + k - 1)
                        A(sq[:, k % 2, :], src[:, c, :], ACT.Square).then_inc(S["gsq"], 1)
                    act.wait_ge(S["gstat"], lay * 3 + g + 1)
                    if g:
                        act.wait_ge(S["y_norm"], lay * DC + GROUPS[g][3])
                    A(std[:], ps[:, 7, :], ACT.Sqrt, bias=eps[:, 0:1], scale=1.0 / (n * P)).then_inc(S["gstd"], 1)

                act.wait_ge(S["h_done"], lay * 2 + 2)
                group(0)

                act.wait_ge(S["mla_in"], lay * 32 + 32)
                for dst, src in ((cqh, cq), (ckh, ckv), (uqh, uqr), (ukh, ukr)):
                    A(dst[:], src[:], ACT.Copy).then_inc(S["mhi"], 1)
                act.wait_ge(S["roped"], lay * 6 + 6)
                for hh in range(MH):
                    A(mkf[MN:MD, hh, :], kr[MN:MD, :], ACT.Copy).then_inc(S["kr_copy"], 1)

                def q_hi(h):
                    rows = slice((h % 2) * GD, (h % 2 + 1) * GD)
                    if h >= 2:
                        act.wait_ge(S["s_tile"], lay * 4 * HEADS + 4 * (h - 1))
                    A(q2[rows, h % 2, :], qf[rows, h // 2, :], ACT.Copy).then_inc(S["q2hi"], 1)

                def exps(h):
                    scale = GD ** -0.5 if h < GH else MD ** -0.5
                    act.wait_ge(S["nmax"], lay * HEADS + h + 1)
                    if h >= 2:
                        act.wait_ge(S["pt_tile"], lay * 4 * HEADS + 4 * (h - 1))
                    for qc in range(TC):
                        A(prob[:, h % 2, qc, :], ps[:, qc, :], ACT.Exp, bias=ns[:, h % 2, qc:qc + 1],
                          scale=scale).then_inc(S["p_ready"], 1)

                def pt_copies(h):
                    for sc in (0, 2):
                        act.wait_ge(S["pt_tile"], lay * 4 * HEADS + 4 * h + sc + 1)
                        if h and sc == 0:
                            act.wait_ge(S["pv"], lay * HEADS + h)
                        A(probT[:, sc, :], ps[:, 4 + sc % 2, :], ACT.Copy).then_inc(S["pt_act"], 1)

                q_hi(0)
                exps_done = 0
                for h in range(HEADS):
                    if h + 1 < GH:
                        q_hi(h + 1)
                    if h == 0:
                        exps(0)
                    if h + 1 < HEADS:
                        exps(h + 1)
                    pt_copies(h)
                for g, heads in ((1, GH), (2, HEADS)):
                    act.wait_ge(S["y_head"], lay * HEADS + heads)
                    group(g)
                for g, (src, _, n, c0) in enumerate(GROUPS):
                    for c in range(n):
                        act.wait_ge(S["y_norm"], lay * DC + c0 + c + 1)
                        A(gh[:, c0 + c, :], src[:, c, :], ACT.Copy).then_inc(S["ygh"], 1)

                for m in range(DC):
                    act.wait_ge(S["pe_item"], lay * ITEMS + I_OUT + m + 3)
                    ysquare(lay, 0, m)
                    hi(lay, I_OUT + m + 2, m % 2)
                post(lay, 0)
                prep(lay * 2 + 1, col + PM["ffn_pre"])

                with act.Fori(0, FC) as j:
                    r = lay * FC + j

                    def tap(k, b):
                        act.wait_ge(S["f_evac"], r * 2 + k + 3)
                        A(cv[:, k, :], pad[:, k, 1:T + 1], ACT.Identity,
                          scale=pm[:, bass.ds(col + j + (PM["ffn_w1"] + k * FC), 1)],
                          bias=pm[:, bass.ds(col + j + (PM["ffn_b"] + k * FC), 1)]).then_inc(S["f_conv1"], 1)

                    tap(0, 0)
                    hi(lay, j * 2 + (I_UP + 2), 0)
                    act.wait_ge(S["f_conv"], r * 2 + 1)
                    A(gact[:], cv[:, 0, :], ACT.Gelu_apprx_tanh).then_inc(S["f_gelu"], 1)
                    tap(1, 1)
                    hi(lay, j * 2 + (I_UP + 3), 1)
                    act.wait_ge(S["f_prod"], r + 1)
                    A(fh[:, bass.ds(j, 1), :], fprod[:].rearrange("p (o t) -> p o t", o=1), ACT.Copy).then_inc(S["f_hi"], 1)

                for m in range(DC):
                    for i in range(len(DOWN_PARTS)):
                        n = I_DOWN + 3 * m + i
                        if n + 2 < ITEMS:
                            hi(lay, n + 2, n % 2)
                    act.wait_ge(S["pe_item"], lay * ITEMS + I_DOWN + 3 * m + 2 + 3)
                    ysquare(lay, 1, m)
                post(lay, 1)
                prep(lay * 2 + 2, col + PM["mix_pre"])

            for c in range(TC):
                for b in range(2):
                    k = 2 * c + b
                    act.wait_ge(S["o_tr"], k + 1)
                    A(xio[:, c, b * T:(b + 1) * T], ps[:, 4 + k % 4, :], ACT.Copy).then_inc(S["o_copy"], 1)

        @block.tensor
        def _(pe):
            mm = nc.tensor.matmul

            pe.wait_ge(S["const_in"], 16 * (6 + 4 * DEPTH + 2))
            pe.wait_ge(S["x_in"], 16)
            for c in range(DC):
                if c >= 4:
                    pe.wait_ge(S["x_first"], c - 3)
                for t in range(TC):
                    ins = nc.tensor.transpose(ps[:, c % 4, t * P:(t + 1) * P], xio[:, t, c * P:(c + 1) * P], ident[:])
                ins.then_inc(S["x_tr"], 1)
            pe.wait_ge(S["par_in"], 16 * DEPTH * 20)
            for i in range(3 * DEPTH):
                n = PM_ROWS[i % 3]
                if i >= 3:
                    pe.wait_ge(S["par_ok"], i - 2)
                nc.tensor.transpose(ps[:, 4 + i % 3, 0:n], pstage[0:n, i, :], ident[0:n, 0:n]).then_inc(S["par_tr"], 1)
            pe.wait_ge(S["const_ok"], 1)
            pe.sem_inc(S["pe_item"], 2)

            def stat_pre(q):
                pe.wait_ge(S["xsq_used"], q * DC + DC)
                mm(ps[:, 1, :], ones[:], acc[:], start=True, stop=True).then_inc(S["stat_pre"], 1)

            def stat_post(lay, b):
                pe.wait_ge(S["ysq_used"], (lay * 2 + b) * DC + DC)
                pe.wait_ge(S["ycopy"], (lay * 2 + b) * 2 + 2)
                mm(ps[:, 0, :], ones[:], acc[:], start=True, stop=True).then_inc(S["stat_post"], 1)

            def tiles(lay, n, slot, bank, tile_n, rh, rl, k0, start, stop, cols=P, gate=None):
                g = lay * ITEMS + n
                pe.wait_ge(S["hi_ready"], g + 1)
                pe.wait_ge(S["lo_ready"], g + 3)
                for k in range(tile_n):
                    if gate:
                        gate(k)
                    w_hi = wh[:, slot, k * P:k * P + cols]
                    w_lo = wl[:, slot, k * P:k * P + cols]
                    x_hi, x_lo = rh[:, k0 + k, :], rl[:, k0 + k, :]
                    mm(ps[0:cols, bank, :], w_hi, x_hi, start=start and k == 0, stop=False)
                    mm(ps[0:cols, bank, :], w_hi, x_lo, start=False, stop=False)
                    ins = mm(ps[0:cols, bank, :], w_lo, x_hi, start=False, stop=stop and k == tile_n - 1)
                ins.then_inc(S["pe_item"], 1)

            stat_pre(0)

            with pe.Fori(0, DEPTH) as lay:
                def item(t):
                    if t >= 2:
                        pe.wait_ge(S["evac"], lay * WIN + t - 1)
                    cols = min(P, D_IN - t * P)

                    def gate(k):
                        if t == 0:
                            pe.wait_ge(S["gh_ready"], lay * 2 * DC + k + 1)
                            pe.wait_ge(S["gl_ready"], lay * 2 * DC + k + 1)
                    if t == 1:
                        pe.wait_ge(S["std_pre"], lay * 2 + 1)
                    tiles(lay, t, t % 2, t % 2, DC, gh, gl, 0, True, True, cols, gate)

                def filt_taps(j):
                    par_, c = divmod(j, 2)
                    if j == 0:
                        pe.wait_ge(S["f_sin"], lay * 2 + 2)
                        pe.wait_ge(S["filt_in"], lay * 48 + 48)
                    if j >= 2:
                        pe.wait_ge(S["fc_done"], lay * 4 + j - 1)
                    b = 4 + 2 * (j % 2)
                    w = w3[:].rearrange("k (o d n) -> k d o n", o=2, d=2)
                    t0 = 2 * P * c + par_
                    for d in range(2):
                        lo = t0 + 1 - d
                        ins = mm(ps[:, b + d, :].rearrange("p (o n) -> p o n", o=2), h2[:, lo:lo + 2 * P - 1:2], w[:, d, :, :],
                                 start=True, stop=True)
                    ins.then_inc(S["fc_mm"], 1)

                def filt_spec(k):
                    b = 4 + 2 * (k % 2)
                    if k == 0:
                        pe.wait_ge(S["tab_in"], lay * 32 + 32)
                        pe.wait_ge(S["fc_done"], lay * 4 + 4)
                    if k >= 2:
                        pe.wait_ge(S["fd_done"], lay * 4 + k - 1)
                    src = hsum if k < 2 else hdif
                    for par_ in range(2):
                        for c in range(2):
                            ins = mm(ps[:, b + par_, :], TF[:, par_, c, k * P:(k + 1) * P], src[:, 2 * par_ + c, :],
                                     start=(c == 0), stop=(c == 1))
                        ins.then_inc(S["fd_mm"], 1)

                def h_turn(o):
                    if o == 0:
                        pe.wait_ge(S["fd_done"], lay * 4 + 4)
                        pe.wait_ge(S["conv_done"], lay * 6 + 6)
                    else:
                        pe.wait_ge(S["h_done"], lay * 2 + 1)
                    for j in range(4):
                        par_, c = divmod(j, 2)
                        for cc in range(2):
                            t0 = 2 * P * c + par_
                            at = (j % 2) * HD + cc * P
                            ins = nc.tensor.transpose(ps[:, 4 + j // 2, at:at + P], uc[:, cc, t0:t0 + 2 * P - 1:2], ident[:])
                    ins.then_inc(S["ha_mm"], 1)

                def h_forward(o):
                    pe.wait_ge(S["hu_copy"], lay * 2 + o + 1)
                    for par_ in range(2):
                        for k in range(4):
                            b = (6 if par_ == 0 else 4) + k // 2
                            for c in range(2):
                                ins = mm(ps[:, b, (k % 2) * HD:(k % 2 + 1) * HD], TF[:, par_, c, k * P:(k + 1) * P],
                                         ut[:, 2 * par_ + c, :], start=(c == 0), stop=(c == 1))
                        ins.then_inc(S["he_mm" if par_ == 0 else "ho_mm"], 1)

                def h_inverse(o):
                    pe.wait_ge(S["h_prod"], lay * 2 + o + 1)
                    for cc in range(2):
                        for par_ in range(2):
                            spec = fa if par_ == 0 else fb
                            for k in range(4):
                                ri, fc = divmod(k, 2)
                                lo = fc * HD + cc * P
                                ins = mm(ps[:, 6 + cc, par_ * NF:(par_ + 1) * NF], spec[:, ri, lo:lo + P],
                                         TI[:, par_, k, :], start=(k == 0), stop=(k == 3))
                    ins.then_inc(S["hc_mm"], 1)

                def stat(k, chunks, weights, first_sq):
                    pe.wait_ge(S["nsq"], lay * 8 + first_sq + len(chunks))
                    if k:
                        pe.wait_ge(S["nstd"], lay * 7 + k)
                    for n, s_ in enumerate(chunks):
                        ins = mm(ps[:, 2, :], weights[:], sq[:, s_, :], start=(n == 0), stop=(n == len(chunks) - 1))
                    ins.then_inc(S["nstat"], 1)

                def permute(k, src):
                    pe.wait_ge(S["nrm"], lay * 7 + k + 1)
                    if k:
                        pe.wait_ge(S["roped"], lay * 6 + k)
                    mm(ps[:, 3, :], perm_g[:], src, start=True, stop=True).then_inc(S["nperm"], 1)

                pe.wait_ge(S["fw_ok"], lay + 1)
                mm(ps[:, 4, :], fwl[0:HEMB, 0, :], zT[:], start=True, stop=True).then_inc(S["f_mm"], 1)
                item(0)
                pe.wait_ge(S["f_sin"], lay * 2 + 1)
                mm(ps[:, 4, :], fwl[:, 1, :], h1[:], start=True, stop=True).then_inc(S["f_mm"], 1)
                for t in range(1, WIN + 2):
                    if 2 <= t < 6:
                        filt_taps(t - 2)
                    if t in (6, 7):
                        filt_spec(2 * (t - 6))
                        filt_spec(2 * (t - 6) + 1)
                    if t == 8:
                        h_turn(0)
                    if t == 9:
                        h_forward(0)
                    if t == 12:
                        h_turn(1)
                    if t == 13:
                        h_forward(1)
                    if t < WIN:
                        item(t)
                    if C_Q <= t - 1 <= C_K:
                        stat(t - 1 - C_Q, [(t - 1 - C_Q) % 2], b64, t - 1 - C_Q)
                    if C_Q <= t - 2 < C_K:
                        permute(t - 2 - C_Q, qf[:, t - 2 - C_Q, :])
                    if t - 2 == C_K:
                        permute(4, cv[:, 0, :])
                    if t == C_V + 2:
                        pe.wait_ge(S["evac"], lay * WIN + C_V + 1)
                        pe.wait_ge(S["roped"], lay * 6 + 5)
                        for s_ in range(TC):
                            ins = nc.tensor.transpose(ps[:, 3, s_ * P:(s_ + 1) * P], cv[:, 1, s_ * P:(s_ + 1) * P], ident[:])
                        ins.then_inc(S["vtr"], 1)
                    if t == 11:
                        h_inverse(0)
                    if t == C_MQ + 2:
                        stat(5, [1, 0], ones, 5)
                    if t == C_MKV + 1:
                        stat(6, [1], ones, 7)
                        h_inverse(1)
                    if t == WIN:
                        pe.wait_ge(S["evac"], lay * WIN + WIN)
                        pe.wait_ge(S["vcopy"], lay + 1)
                        mm(ps[0:MD, 3, :], perm_m[:], kr[0:MD, :], start=True, stop=True).then_inc(S["nperm"], 1)

                def group(g):
                    n = GROUPS[g][2]
                    if g:
                        pe.wait_ge(S["gstd"], lay * 3 + g)
                    pe.wait_ge(S["gsq_used"], lay * DC + GROUPS[g][3] + n)
                    mm(ps[:, 7, :], ones[:], acc[:], start=True, stop=True).then_inc(S["gstat"], 1)

                pe.wait_ge(S["h_done"], lay * 2 + 2)
                group(0)

                def scores(h):
                    for qc in range(TC):
                        cols = slice(qc * P, (qc + 1) * P)
                        if h == 0:
                            if qc == 0:
                                pe.wait_ge(S["evac"], lay * WIN + WIN)
                            if qc == 2:
                                pe.wait_ge(S["nstd"], lay * 7 + 7)
                            if qc == 3:
                                pe.wait_ge(S["roped"], lay * 6 + 6)
                        else:
                            pe.wait_ge(S["p_ready"], (lay * HEADS + h - 1) * 4 + qc + 1)
                        if h < GH:
                            if qc == 0:
                                pe.wait_ge(S["q2hi"], lay * GH + h + 1)
                                pe.wait_ge(S["q2lo"], lay * GH + h + 1)
                                if h == 0:
                                    pe.wait_ge(S["khi"], lay * 4 + 4)
                                    pe.wait_ge(S["klo"], lay * 4 + 4)
                            mm(ps[:, qc, :], q2[:, h % 2, cols], ka[:, h // 4, :], start=True, stop=False)
                            mm(ps[:, qc, :], q2[:, h % 2, cols], kb[:, h // 4, :], start=False, stop=True) \
                                .then_inc(S["s_tile"], 1)
                        else:
                            if h == GH and qc == 0:
                                pe.wait_ge(S["b7_free"], lay * len(B7) + len(B7))
                                pe.wait_ge(S["kr_copy"], lay * MH + MH)
                            mm(ps[:, qc, :], mqf[0:MD, h - GH, cols], mkf[0:MD, h - GH, :], start=True, stop=True) \
                                .then_inc(S["s_tile"], 1)

                def bank7(k):
                    kind, i = B7[k]
                    if k:
                        pe.wait_ge(S["b7_free"], lay * len(B7) + k)
                    else:
                        pe.wait_ge(S["gstd"], lay * 3 + 1)
                        pe.wait_ge(S["mhi"], lay * 4 + 4)
                        pe.wait_ge(S["mlo"], lay * 4 + 4)
                    if kind == "q":
                        n, last = 0, 5
                        for c in range(2):
                            for w, x in ((uqh, cqh), (uqh, cql), (uql, cqh)):
                                ins = mm(ps[0:MD, 7, :], w[:, c, i * MD:(i + 1) * MD], x[:, c, :], start=(n == 0), stop=(n == last))
                                n += 1
                    elif kind == "perm":
                        ins = mm(ps[0:MD, 7, :], perm_m[:], mqf[0:MD, i, :], start=True, stop=True)
                    elif kind == "k":
                        for n, (w, x) in enumerate(((ukh, ckh), (ukh, ckl), (ukl, ckh))):
                            ins = mm(ps[0:MN, 7, :], w[:, i * P:i * P + MN], x[:], start=(n == 0), stop=(n == 2))
                    else:
                        cols = slice(i * P, (i + 1) * P)
                        for n, (w, x) in enumerate(((ckh, ukh), (ckh, ukl), (ckl, ukh))):
                            ins = mm(ps[:, 7, :], w[:, cols], x[:], start=(n == 0), stop=(n == 2))
                    ins.then_inc(S["b7_full"], 1)

                def turn(h):
                    pe.wait_ge(S["p_ready"], (lay * HEADS + h) * 4 + 4)
                    for sc in range(TC):
                        if sc >= 2 or h:
                            k = (lay * HEADS + h) * 2 + sc // 2
                            pe.wait_ge(S["pt_act" if sc % 2 == 0 else "pt_dve"], k)
                        for qc in range(TC):
                            ins = nc.tensor.transpose(ps[:, 4 + sc % 2, qc * P:(qc + 1) * P],
                                                      prob[:, h % 2, qc, sc * P:(sc + 1) * P], ident[:])
                        ins.then_inc(S["pt_tile"], 1)

                def values(h):
                    if h:
                        pe.wait_ge(S["y_head"], lay * HEADS + h)
                    if h == 0:
                        pe.wait_ge(S["vcopy"], lay + 1)
                    pe.wait_ge(S["pt_act"], (lay * HEADS + h) * 2 + 2)
                    pe.wait_ge(S["pt_dve"], (lay * HEADS + h) * 2 + 2)
                    for sc in range(TC):
                        if h < GH:
                            v = vg[:, sc, (h // 4) * GD:(h // 4) * GD + P]
                        else:
                            i = h - GH
                            v = mv[:, sc, i // 2, (i % 2) * MV:(i % 2) * MV + P]
                        ins = mm(ps[:, 6, :], v, probT[:, sc, :], start=(sc == 0), stop=(sc == TC - 1))
                    ins.then_inc(S["pv"], 1)

                scores(0)
                k7 = 0
                for h in range(HEADS):
                    if h + 1 < HEADS:
                        scores(h + 1)
                    for _ in B7_AT.get(h, ()):
                        bank7(k7)
                        k7 += 1
                    turn(h)
                    values(h)
                group(1)
                group(2)

                def gate_out(k):
                    pe.wait_ge(S["ygh"], lay * DC + k + 1)
                    pe.wait_ge(S["ygl"], lay * DC + k + 1)

                pe.wait_ge(S["p_ready"], (lay * HEADS + HEADS) * 4)
                pe.wait_ge(S["y_head"], lay * HEADS + HEADS)
                for m in range(DC):
                    if m == DC - 1:
                        pe.wait_ge(S["gstd"], lay * 3 + 3)
                    tiles(lay, I_OUT + m, m % 2, m, DC, gh, gl, 0, True, True, gate=gate_out if m == 0 else None)
                stat_post(lay, 0)
                stat_pre(lay * 2 + 1)

                pe.wait_ge(S["gl_ready"], (lay * 2 + 2) * DC)
                mark(pe, "pe_marks")
                with pe.Fori(0, FC) as j:
                    r = lay * FC + j
                    for k in range(2):
                        pe.wait_ge(S["f_evac"], r * 2 + k + 1)
                        tiles(lay, j * 2 + (I_UP + k), k, 2 + k, DC, gh, gl, 0, True, True)

                pe.wait_ge(S["f_evac"], lay * 2 * FC + 2 * FC + 2)
                pe.wait_ge(S["rbc_ready"], lay * 2 + 2)
                for m in range(DC):
                    for i, (k0, n) in enumerate(DOWN_PARTS):
                        last = i == len(DOWN_PARTS) - 1

                        def gate_down(k, k0=k0):
                            if m == 0:
                                pe.wait_ge(S["f_hi"], lay * FC + k0 + k + 1)
                                pe.wait_ge(S["f_lo"], lay * FC + k0 + k + 1)

                        tiles(lay, I_DOWN + 3 * m + i, (3 * m + i) % 2, m, n, fh, fl, k0, i == 0, last, gate=gate_down)
                stat_post(lay, 1)
                stat_pre(lay * 2 + 2)

            pe.wait_ge(S["x_new"], 2 * DEPTH * DC)
            for c in range(TC):
                for b in range(2):
                    k = 2 * c + b
                    if k >= 4:
                        pe.wait_ge(S["o_copy"], k - 3)
                    for i in range(4):
                        ins = nc.tensor.transpose(ps[:, 4 + k % 4, i * P:(i + 1) * P],
                                                  xT[:, 4 * b + i, c * P:(c + 1) * P], ident[:])
                    ins.then_inc(S["o_tr"], 1)

        @block.vector
        def _(dve):
            V = Chain(dve, dve_self)
            tt, ts, stt = nc.vector.tensor_tensor, nc.vector.tensor_scalar, nc.vector.scalar_tensor_tensor
            copy, recip = nc.vector.tensor_copy, nc.vector.reciprocal

            def prep(q, off, update=None):
                def chunk(c):
                    dve.wait_ge(S["gh_ready"], q * DC + c + 1)
                    stt(out=gl[:, c, :], in0=xT[:, c, :], scalar=pm[:, bass.ds(off + c, 1)] if not isinstance(off, int)
                        else pm[:, off + c:off + c + 1], in1=gh[:, c, :].bitcast(F32), op0=ALU.mult,
                        op1=ALU.subtract).then_inc(S["gl_ready"], 1)
                    dve.wait_ge(S["xsq"], q * DC + c + 1)
                    if c == 0:
                        copy(acc[:], sq[:, 0, :]).then_inc(S["xsq_used"], 1)
                    else:
                        dve.wait_ge(S["xsq_used"], q * DC + c)
                        tt(acc[:], acc[:], sq[:, c % 2, :], ALU.add).then_inc(S["xsq_used"], 1)

                for c in range(DC + 1):
                    if update and c < DC:
                        update(c)
                    if c:
                        chunk(c - 1)
                dve.wait_ge(S["std_pre"], q + 1)
                recip(rbc[:], std[:]).then_inc(S["rbc_ready"], 1)
                dve.wait_ge(S["rbc_ready"], q + 1)

            def ysum(lay, b, m):
                k = (lay * 2 + b) * DC + m
                dve.wait_ge(S["ysq"], k + 1)
                if m == 0:
                    copy(acc[:], sq[:, 0, :]).then_inc(S["ysq_used"], 1)
                else:
                    dve.wait_ge(S["ysq_used"], k)
                    tt(acc[:], acc[:], sq[:, m % 2, :], ALU.add).then_inc(S["ysq_used"], 1)

            def residual(lay, b, gain, pre):
                dve.wait_ge(S["std_post"], lay * 2 + b + 1)
                V.do(recip(rr[:], std[:]))
                V.join()

                def update(c):
                    y = yt[:, c, :] if c < 2 else ps[:, c, :]
                    t = cv[:, c % 2, :]
                    V.do(stt(out=t, in0=y, scalar=pm[:, bass.ds(lay * PML + (gain + c), 1)], in1=rr[:],
                             op0=ALU.mult, op1=ALU.mult))
                    V.join()
                    tt(xT[:, c, :], xT[:, c, :], t, ALU.add).then_inc(S["x_new"], 1)
                    dve.wait_ge(S["x_new"], (lay * 2 + b) * DC + c + 1)

                prep(lay * 2 + b + 1, lay * PML + pre, update)

            dve.wait_ge(S["x_first"], DC)
            dve.wait_ge(S["par_ok"], 3 * DEPTH)
            dve.wait_ge(S["const_ok"], 1)
            dve.wait_ge(S["const_in"], 16 * (6 + 4 * DEPTH + 2))
            prep(0, (DEPTH - 1) * PML + PM["mix_pre"])
            dve.sem_inc(S["f_evac"], 2)

            with dve.Fori(0, DEPTH) as lay:
                V.restart()
                col = lay * PML

                def par(name, i=0, rows=slice(0, P)):
                    return pm[rows, bass.ds(col + (PM[name] + i), 1)]

                V.do(copy(fwl[0:HEMB, 0, 0:HHID], fw1[:, bass.ds(lay, 1), :].rearrange("k o n -> k (o n)")))
                V.join()
                copy(fwl[:, 1, 0:HHID], fw2[:, bass.ds(lay, 1), :].rearrange("k o n -> k (o n)")).then_inc(S["fw_ok"], 1)
                V.do(nc.vector.memset(kr[0:MN, :], 0.0))
                V.do(nc.vector.memset(vg[:, :, GD:2 * GD], 1.0))

                def sine_arg(k):
                    dve.wait_ge(S["f_mm"], lay * 2 + k + 1)
                    x, n = arg[:, 0, :], arg[:, 1, :]
                    V.do(ts(x, ps[0:HHID, 4, :], fbf[:, 2 * k, bass.ds(lay, 1)], fbf[:, 2 * k + 1, bass.ds(lay, 1)],
                            ALU.add, ALU.mult))
                    V.join()
                    V.do(ts(n, x, 1.0 / (2 * np.pi), MAGIC, ALU.mult, ALU.add))
                    V.join()
                    V.do(ts(n, n, -MAGIC, None, ALU.add))
                    V.join()
                    for part in PI2:
                        V.do(stt(out=x, in0=n, scalar=-part, in1=x, op0=ALU.mult, op1=ALU.add))
                        V.join()
                    ts(x, x, PI, -PI, ALU.min, ALU.max).then_inc(S["f_arg"], 1)

                def evac(t, dst, rows=P):
                    dve.wait_ge(S["pe_item"], lay * ITEMS + t + 3)
                    tt(dst, ps[0:rows, t % 2, :], rbc[0:rows, :], ALU.mult).then_inc(S["evac"], 1)

                def conv(i):
                    dve.wait_ge(S["conv1"], lay * 6 + i + 1)
                    u = uc[:, i, :]
                    V.do(stt(out=u, in0=pad[:, i % 2, 0:T], scalar=par("hy_w", i), in1=u, op0=ALU.mult, op1=ALU.add))
                    V.join()
                    stt(out=u, in0=pad[:, i % 2, 2:T + 2], scalar=par("hy_w", 12 + i), in1=u, op0=ALU.mult,
                        op1=ALU.add).then_inc(S["conv_done"], 1)

                def taps(j):
                    dve.wait_ge(S["fc_mm"], lay * 4 + j + 1)
                    b = 4 + 2 * (j % 2)
                    for d in range(2):
                        w = win[:, d, j, :].unsqueeze(1).to_broadcast([P, 2, HD])
                        V.do(tt(yt[:, d, :].rearrange("p (o n) -> p o n", o=2),
                                ps[:, b + d, :].rearrange("p (o n) -> p o n", o=2), w, ALU.mult))
                    V.join()
                    V.do(tt(hsum[:, j, :], yt[:, 0, :], yt[:, 1, :], ALU.add))
                    tt(hdif[:, j, :], yt[:, 0, :], yt[:, 1, :], ALU.subtract).then_inc(S["fc_done"], 1)
                    V.join()

                def spectrum(k):
                    dve.wait_ge(S["fd_copy"], lay * 4 + k + 1)
                    dve.wait_ge(S["fd_mm"], lay * 8 + 2 * k + 2)
                    ri, fc = divmod(k, 2)
                    o_ = ps[:, 5 + 2 * (k % 2), :].rearrange("p (o n) -> p o n", o=2)
                    e_ = yt[:, 0, :].rearrange("p (o n) -> p o n", o=2)
                    V.do(tt(KP[:, ri, :, fc * HD:(fc + 1) * HD], e_, o_, ALU.add))
                    tt(KM[:, ri, :, fc * HD:(fc + 1) * HD], e_, o_, ALU.subtract).then_inc(S["fd_done"], 1)

                def times(x, kk, o, dst):
                    kre = kk[:, 0:1, o, :].to_broadcast([P, 2, T])
                    kim = kk[:, 1:2, o, :].to_broadcast([P, 2, T])
                    V.do(tt(p1[:], x[:], kre, ALU.mult))
                    V.do(tt(p2[:], x[:], kim, ALU.mult))
                    V.join()
                    V.do(tt(dst[:, 0, :], p1[:, 0, :], p2[:, 1, :], ALU.subtract))
                    V.do(tt(dst[:, 1, :], p1[:, 1, :], p2[:, 0, :], ALU.add))
                    V.join()

                def h_first(o):
                    dve.wait_ge(S["he_copy"], lay * 2 + o + 1)
                    dve.wait_ge(S["ho_mm"], lay * 2 + o + 1)
                    V.do(tt(fa[:], ebuf[:], ps[:, 4:6, :], ALU.add))
                    V.do(tt(fb[:], ebuf[:], ps[:, 4:6, :], ALU.subtract))
                    V.join()
                    times(fa, KP, o, ya)

                def h_second(o):
                    times(fb, KM, o, yb)
                    V.do(tt(fa[:], ya[:], yb[:], ALU.add))
                    tt(fb[:], ya[:], yb[:], ALU.subtract).then_inc(S["h_prod"], 1)
                    V.join()

                def h_gate(o):
                    dve.wait_ge(S["hc_mm"], lay * 2 + o + 1)
                    for cc in range(2):
                        u = uc[:, cc, :].rearrange("p (n two) -> p two n", two=2)
                        y = ps[:, 6 + cc, :].rearrange("p (two n) -> p two n", two=2)
                        V.do(stt(out=u, in0=u, scalar=par("skip", 2 * o + cc), in1=y, op0=ALU.mult, op1=ALU.add))
                    V.join()
                    V.do(tt(uc[:, 0, :], uc[:, 0, :], uc[:, 2 + 2 * o, :], ALU.mult))
                    V.join()
                    tt(uc[:, 1, :], uc[:, 1, :], uc[:, 3 + 2 * o, :], ALU.mult).then_inc(S["h_done"], 1)
                    dve.wait_ge(S["h_done"], lay * 2 + o + 1)

                def norm(k, parts):
                    dve.wait_ge(S["nstd"], lay * 7 + k + 1)
                    V.do(recip(rr[:], std[:]))
                    V.join()
                    for n, (x, g) in enumerate(parts):
                        ins = stt(out=x, in0=x, scalar=g, in1=rr[:], op0=ALU.mult, op1=ALU.mult)
                        if n == len(parts) - 1:
                            ins.then_inc(S["nrm"], 1)
                        else:
                            V.do(ins)
                            V.join()
                    dve.wait_ge(S["nrm"], lay * 7 + k + 1)

                def rotate(k, x, rows, table, bank=3):
                    dve.wait_ge(S["nperm"], lay * 6 + k + 1)
                    V.do(tt(yt[rows, 0, :], x, rope[rows, table, :], ALU.mult))
                    V.do(tt(yt[rows, 1, :], ps[rows, bank, :], rope[rows, table + 1, :], ALU.mult))
                    V.join()
                    tt(x, yt[rows, 0, :], yt[rows, 1, :], ALU.add).then_inc(S["roped"], 1)

                everything = slice(0, P)
                sine_arg(0)
                for t in range(WIN + 2):
                    if t == 0:
                        evac(0, pad[:, 0, 1:T + 1])
                        sine_arg(1)
                    elif t < C_Q:
                        evac(t, pad[:, t % 2, 1:T + 1])
                    elif t < C_K:
                        evac(t, qf[:, t - C_Q, :])
                    elif t == C_K:
                        evac(t, cv[:, 0, :])
                    elif t == C_V:
                        evac(t, cv[:, 1, :])
                    elif t < C_MKV:
                        evac(t, cq[:, t - C_MQ, :])
                    elif t == C_MKV:
                        evac(t, ckv[:])
                    elif t == C_MKR:
                        V.join()
                        evac(t, kr[MN:MD, :], MR)
                    if 0 <= t - 1 < C_Q:
                        conv(t - 1)
                    if C_Q <= t - 1 < C_K:
                        norm(t - 1 - C_Q, [(qf[:, t - 1 - C_Q, :], par("gq"))])
                    if t - 1 == C_K:
                        norm(4, [(cv[:, 0, :], par("gk"))])
                    if C_Q <= t - 2 < C_K:
                        rotate(t - 2 - C_Q, qf[:, t - 2 - C_Q, :], everything, 0)
                    if t - 2 == C_K:
                        rotate(4, cv[:, 0, :], everything, 0)
                    if t == C_V + 2:
                        dve.wait_ge(S["vtr"], lay + 1)
                        v = ps[:, 3, :].rearrange("p (s n) -> p s n", s=TC)
                        V.do(copy(vg[:, :, 0:GD], v[:, :, 0:GD]))
                        copy(vg[:, :, 2 * GD:3 * GD], v[:, :, GD:2 * GD]).then_inc(S["vcopy"], 1)
                    if 1 <= t < 5:
                        taps(t - 1)
                    if t in (5, 6):
                        spectrum(2 * (t - 5))
                        spectrum(2 * (t - 5) + 1)
                    if t == 9:
                        h_first(0)
                    if t == 10:
                        h_second(0)
                    if t == 11:
                        h_gate(0)
                    if t == 13:
                        h_first(1)
                    if t == 14:
                        h_second(1)
                    if t == C_MQ + 2:
                        norm(5, [(cq[:, 0, :], par("mqa", 0)), (cq[:, 1, :], par("mqa", 1))])
                    if t == C_MKV + 1:
                        norm(6, [(ckv[:], par("mkva"))])
                        h_gate(1)
                    if t == WIN:
                        rotate(5, kr[MN:MD, :], slice(MN, MD), 2)
                for kv in range(GKV):
                    rows = slice(kv * GD, (kv + 1) * GD)
                    for half in range(2):
                        dve.wait_ge(S["khi"], lay * 4 + 2 * kv + 2)
                        tt(kb[half * GD:(half + 1) * GD, kv, :], cv[rows, 0, :], ka[rows, kv, :].bitcast(F32),
                           ALU.subtract).then_inc(S["klo"], 1)

                gsq_n = [0]

                def group(g):
                    src, _, n, c0 = GROUPS[g]
                    for c in range(n):
                        k = gsq_n[0]
                        gsq_n[0] += 1
                        dve.wait_ge(S["gsq"], lay * DC + k + 1)
                        if c == 0:
                            copy(acc[:], sq[:, k % 2, :]).then_inc(S["gsq_used"], 1)
                        else:
                            dve.wait_ge(S["gsq_used"], lay * DC + k)
                            tt(acc[:], acc[:], sq[:, k % 2, :], ALU.add).then_inc(S["gsq_used"], 1)
                    dve.wait_ge(S["gstd"], lay * 3 + g + 1)
                    V.do(recip(rr[:], std[:]))
                    V.join()
                    for c in range(n):
                        stt(out=src[:, c, :], in0=src[:, c, :], scalar=par("g_out", c0 + c), in1=rr[:], op0=ALU.mult,
                            op1=ALU.mult).then_inc(S["y_norm"], 1)

                group(0)

                for k, (dst, src, hi_) in enumerate(((cql, cq, cqh), (ckl, ckv, ckh), (uql, uqr, uqh), (ukl, ukr, ukh))):
                    dve.wait_ge(S["mhi"], lay * 4 + k + 1)
                    tt(dst[:], src[:], hi_[:].bitcast(F32), ALU.subtract).then_inc(S["mlo"], 1)
                V.do(nc.vector.memset(mv[:, :, :, MV:2 * MV], 1.0))

                def q_lo(h):
                    half = h % 2
                    rows, other = slice(half * GD, (half + 1) * GD), slice((1 - half) * GD, (2 - half) * GD)
                    dve.wait_ge(S["q2hi"], lay * GH + h + 1)
                    tt(q2[other, half, :], qf[rows, h // 2, :], q2[rows, half, :].bitcast(F32),
                       ALU.subtract).then_inc(S["q2lo"], 1)

                def maxima(h):
                    scale = GD ** -0.5 if h < GH else MD ** -0.5
                    for qc in range(TC):
                        dve.wait_ge(S["s_tile"], (lay * HEADS + h) * 4 + qc + 1)
                        V.do(nc.vector.reduce_max(nm[:, h % 2, qc:qc + 1], ps[:, qc, :], AX.X))
                    V.join()
                    ts(ns[:, h % 2, :], nm[:, h % 2, :], -scale, None, ALU.mult).then_inc(S["nmax"], 1)

                def pt_copies(h):
                    for sc in (1, 3):
                        dve.wait_ge(S["pt_tile"], (lay * HEADS + h) * 4 + sc + 1)
                        if h and sc == 1:
                            dve.wait_ge(S["pv"], lay * HEADS + h)
                        copy(probT[:, sc, :], ps[:, 5, :]).then_inc(S["pt_dve"], 1)

                def bank7(k):
                    kind, i = B7[k]
                    dve.wait_ge(S["b7_full"], lay * len(B7) + k + 1)
                    if kind == "q":
                        copy(mqf[0:MD, i, :], ps[0:MD, 7, :]).then_inc(S["b7_free"], 1)
                        dve.wait_ge(S["b7_free"], lay * len(B7) + k + 1)
                    elif kind == "perm":
                        V.do(tt(yt[0:MD, 0, :], mqf[0:MD, i, :], rope[0:MD, 2, :], ALU.mult))
                        V.do(tt(yt[0:MD, 1, :], ps[0:MD, 7, :], rope[0:MD, 3, :], ALU.mult))
                        V.join()
                        tt(mqf[0:MD, i, :], yt[0:MD, 0, :], yt[0:MD, 1, :], ALU.add).then_inc(S["b7_free"], 1)
                    elif kind == "k":
                        copy(mkf[0:MN, i, :], ps[0:MN, 7, :]).then_inc(S["b7_free"], 1)
                    else:
                        v = ps[:, 7, :].rearrange("p (a b n) -> p a b n", a=2, b=2)
                        V.do(copy(mv[:, i, :, 0:MV], v[:, :, 0, MN:MN + MV]))
                        copy(mv[:, i, :, 2 * MV:3 * MV], v[:, :, 1, MN:MN + MV]).then_inc(S["b7_free"], 1)

                def head_out(h):
                    dve.wait_ge(S["pv"], lay * HEADS + h + 1)
                    swapped = (h // 4) % 2 if h < GH else h % 2
                    o_rows = slice(GD, 2 * GD) if swapped else slice(0, GD)
                    d_rows = slice(0, GD) if swapped else slice(GD, 2 * GD)
                    rows = slice((h % 2) * GD, (h % 2 + 1) * GD)
                    V.do(recip(rr[o_rows, :], ps[d_rows, 6, :]))
                    V.join()
                    dst = qf[rows, h // 2, :] if h < GH else cq[rows, (h - GH) // 2, :]
                    tt(dst, ps[o_rows, 6, :], rr[o_rows, :], ALU.mult).then_inc(S["y_head"], 1)

                q_lo(0)
                maxima(0)
                k7 = 0
                for h in range(HEADS):
                    if h + 1 < GH:
                        q_lo(h + 1)
                    if h + 1 < HEADS:
                        maxima(h + 1)
                    for _ in B7_AT.get(h, ()):
                        bank7(k7)
                        k7 += 1
                    pt_copies(h)
                    head_out(h)
                dve.wait_ge(S["y_head"], lay * HEADS + HEADS)
                group(1)
                group(2)
                for g, (src, _, n, c0) in enumerate(GROUPS):
                    for c in range(n):
                        dve.wait_ge(S["ygh"], lay * DC + c0 + c + 1)
                        tt(gl[:, c0 + c, :], src[:, c, :], gh[:, c0 + c, :].bitcast(F32), ALU.subtract).then_inc(S["ygl"], 1)

                for m in range(DC):
                    ysum(lay, 0, m)
                residual(lay, 0, PM["mix_post"], PM["ffn_pre"])

                V.join()
                mark(dve, "dve_marks")
                with dve.Fori(0, FC) as j:
                    V.restart()
                    r = lay * FC + j

                    def f_evac(k):
                        dve.wait_ge(S["pe_item"], lay * ITEMS + j * 2 + (I_UP + k + 3))
                        tt(pad[:, k, 1:T + 1], ps[:, 2 + k, :], rbc[:], ALU.mult).then_inc(S["f_evac"], 1)

                    def f_conv(k):
                        dve.wait_ge(S["f_conv1"], r * 2 + k + 1)
                        c = cv[:, k, :]
                        V.do(stt(out=c, in0=pad[:, k, 0:T], scalar=pm[:, bass.ds(col + j + (PM["ffn_w0"] + k * FC), 1)],
                                 in1=c, op0=ALU.mult, op1=ALU.add))
                        V.join()
                        stt(out=c, in0=pad[:, k, 2:T + 2], scalar=pm[:, bass.ds(col + j + (PM["ffn_w2"] + k * FC), 1)],
                            in1=c, op0=ALU.mult, op1=ALU.add).then_inc(S["f_conv"], 1)

                    f_evac(0)
                    f_conv(0)
                    f_evac(1)
                    f_conv(1)
                    dve.wait_ge(S["f_gelu"], r + 1)
                    dve.wait_ge(S["f_conv"], r * 2 + 2)
                    tt(fprod[:], gact[:], cv[:, 1, :], ALU.mult).then_inc(S["f_prod"], 1)
                    dve.wait_ge(S["f_hi"], r + 1)
                    tt(fl[:, bass.ds(j, 1), :], fprod[:].rearrange("p (o t) -> p o t", o=1),
                       fh[:, bass.ds(j, 1), :].bitcast(F32), ALU.subtract).then_inc(S["f_lo"], 1)
                    V.join()
                    mark(dve, "dve_marks")

                V.restart()
                for m in range(DC):
                    ysum(lay, 1, m)
                residual(lay, 1, PM["ffn_post"], PM["mix_pre"])
                V.join()
                mark(dve, "dve_marks")


def constants():
    c = {}
    c["c_ident"] = np.eye(P, dtype=np.float32)
    c["c_b64"] = np.kron(np.eye(2), np.ones((GD, GD))).astype(np.float32)

    def swap(n, at, total):
        m = np.zeros((total, total), np.float32)
        for i in range(n):
            m[at + n + i, at + i] = -1.0
            m[at + i, at + n + i] = 1.0
        return m

    c["c_perm_g"] = swap(GD // 2, 0, P) + swap(GD // 2, GD, P)
    c["c_perm_m"] = swap(MR // 2, MN, MD)
    rows, cols = np.divmod(np.arange(T), GRID_W)

    def angles(rot):
        n = rot // 4
        inv = (np.float32(10000.0) ** (-np.arange(n, dtype=np.float32) / np.float32(n))).astype(np.float32)
        ang = np.concatenate([rows[:, None].astype(np.float32) * inv, cols[:, None].astype(np.float32) * inv], -1)
        return ang.astype(np.float64)

    rope = np.zeros((P, 4, T), np.float32)
    g, m = angles(GD), angles(MR)
    for i in range(4):
        rope[i * GD // 2:(i + 1) * GD // 2, 0] = np.cos(g).T
        rope[i * GD // 2:(i + 1) * GD // 2, 1] = np.sin(g).T
    rope[:MN, 2] = 1.0
    for i in range(2):
        at = MN + i * MR // 2
        rope[at:at + MR // 2, 2] = np.cos(m).T
        rope[at:at + MR // 2, 3] = np.sin(m).T
    c["c_rope"] = rope
    bands = (HEMB - 1) // 2
    t = np.linspace(0.0, 1.0, T, dtype=np.float32)[:, None]
    w = (np.float32(2.0 * np.pi) * np.arange(T, dtype=np.float32)[:, None] / np.float32(T)).astype(np.float32)
    f = np.linspace(1e-4, bands - 1, bands, dtype=np.float32)[None, :]
    fw = (f * w).astype(np.float32).astype(np.float64)
    c["c_z"] = np.ascontiguousarray(np.concatenate([t, np.cos(fw), -np.sin(fw)], -1).astype(np.float32).T)
    lo, hi = np.log(1e-2) / 1.5, np.log(1e-2) / 0.3
    deltas = np.linspace(lo, hi, HD, dtype=np.float32)
    window = np.exp((-t * np.abs(deltas)[None, :]).astype(np.float64)).astype(np.float32)
    late = np.concatenate([np.zeros((1, HD), np.float32), window[:-1]])
    tiles = lambda x: x.reshape(2, P, 2, HD).transpose(1, 2, 0, 3).reshape(P, 4, HD)
    c["c_win"] = np.ascontiguousarray(np.stack([tiles(window), tiles(late)], 1))
    theta = np.pi * (2 * np.arange(NF) + 1) / (2 * T)
    tf = np.zeros((P, 2, 2, T), np.float32)
    ti = np.zeros((P, 2, 4, NF), np.float32)
    for par in range(2):
        ang = np.outer(2 * np.arange(NF) + par, theta)
        fwd = np.concatenate([np.cos(ang), -np.sin(ang)], 1)
        for k in range(2):
            tf[:, par, k] = fwd[k * P:(k + 1) * P]
        inv = np.stack([np.cos(ang).T, -np.sin(ang).T]) / T
        ti[:, par] = inv.reshape(2, 2, P, NF).transpose(2, 0, 1, 3).reshape(P, 4, NF)
    c["c_tf"], c["c_ti"] = tf, ti
    return c


NAMES = ['x', 'mix_pre_norm', 'w_in', 'hy_conv_w', 'hy_conv_b', 'hy_filt_w1', 'hy_filt_b1', 'hy_filt_freq1',
         'hy_filt_w2', 'hy_filt_b2', 'hy_filt_freq2', 'hy_filt_w3', 'hy_skip', 'gqa_q_norm', 'gqa_k_norm',
         'mla_q_a_norm', 'mla_w_uq', 'mla_kv_a_norm', 'mla_w_ukv', 'hy_out_norm', 'gqa_out_norm', 'mla_out_norm',
         'w_out', 'mix_post_norm', 'ffn_pre_norm', 'w_up', 'ffn_conv_w', 'ffn_conv_b', 'w_down', 'ffn_post_norm']


def kernel(**inputs):
    import concourse.bacc as bacc
    from concourse.bass_utils import run_bass_kernel_spmd

    nc = bacc.Bacc("TRN2", target_bir_lowering=False, num_devices=1, dynamic_dma_scratch_size=1024)
    arrays = {n: np.ascontiguousarray(inputs[n]) for n in NAMES}
    arrays.update(constants())
    aps = {n: nc.dram_tensor(n, v.shape, F32, kind="ExternalInput").ap() for n, v in arrays.items()}
    out = nc.dram_tensor("out", (1, T, DM), F32, kind="ExternalOutput").ap()
    build(nc, aps, out)
    r = run_bass_kernel_spmd(nc, [arrays], core_ids=[0])
    return r.results[0]["out"]
```

```python
from contextlib import ExitStack

import concourse.bass as bass
import numpy as np
from concourse import mybir

F32 = mybir.dt.float32
F32R = mybir.dt.float32r
ACT = mybir.ActivationFunctionType
ALU = mybir.AluOpType
AX = mybir.AxisListType

P = 128
DM, T, DEPTH = 1024, 512, 2
DC = DM // P
TC = T // P
GRID_W = 64
EPS = 1e-6
HD, HEMB, HHID = 256, 33, 64
GH, GKV, GD = 8, 2, 64
MH, MQR, MKVR, MN, MR, MV = 4, 256, 128, 64, 32, 64
MD = MN + MR
DFF = 2816
FC = DFF // P
D_IN = 3 * HD + GH * GD + 2 * GKV * GD + MQR + MKVR + MR
NF = T // 2

WIN = -(-D_IN // P)
C_Q = 3 * HD // P
C_K = C_Q + GH * GD // P
C_V = C_K + 1
C_MQ = C_V + 1
C_MKV = C_MQ + MQR // P
C_MKR = C_MKV + 1
assert C_MKR == WIN - 1 and D_IN - C_MKR * P == MR

ITEM = 8
I_OUT = WIN
I_UP = I_OUT + DC
I_DOWN = I_UP + 2 * FC
DOWN_PARTS = [(k, min(ITEM, FC - k)) for k in range(0, FC, ITEM)]
ITEMS = I_DOWN + DC * len(DOWN_PARTS)
assert I_OUT % 2 == 0 and I_UP % 2 == 0 and I_DOWN % 2 == 0 and ITEMS % 2 == 0

PM = {}
_at = 0
for _name, _n in (("mix_pre", DC), ("hy_w", 18), ("hy_b", 6), ("skip", 4), ("mqa", 2), ("mkva", 1),
                  ("g_out", DC), ("mix_post", DC), ("ffn_pre", DC), ("ffn_post", DC), ("gq", 1), ("gk", 1)):
    PM[_name] = _at
    _at += _n
PM_A = _at
PM["ffn_w0"], PM["ffn_w1"], PM["ffn_w2"], PM["ffn_b"] = P, P + 2 * FC, 2 * P, 2 * P + 2 * FC
PM_ROWS = [PM_A, 4 * FC, 4 * FC]
PML = 3 * P

MAGIC = 1.5 * 2.0 ** 23
PI2 = (6.28125, 0.0019350051879882812, 3.019916e-07)
PI = 3.1415925


class Chain:

    def __init__(self, eng, sem):
        self.eng, self.sem, self.n = eng, sem, 0

    def do(self, ins):
        ins.then_inc(self.sem, 1)
        self.n += 1

    def join(self):
        self.eng.wait_ge(self.sem, self.n)

    def restart(self):
        self.eng.sem_clear(self.sem)
        self.n = 0


def build(nc, a, out):
    ctx = ExitStack()
    with ctx:
        def sb(name, shape, dt=F32, scope=ctx):
            return scope.enter_context(nc.sbuf_tensor(name, shape, dt))

        def sem(name):
            return ctx.enter_context(nc.semaphore(name))

        xT = sb("xT", [P, DC, T])
        raw = sb("raw", [P, 2, ITEM * P])
        wh = sb("wh", [P, 2, ITEM * P], F32R)
        wl = sb("wl", [P, 2, ITEM * P], F32R)
        ident = sb("ident", [P, P])
        ones = sb("ones", [P, P])
        b64 = sb("b64", [P, P])
        perm_g = sb("perm_g", [P, P])
        perm_m = sb("perm_m", [MD, MD])
        rope = sb("rope", [P, 4, T])
        rbc = sb("rbc", [P, T])
        std = sb("std", [P, T])
        rr = sb("rr", [P, 2, T])
        sq = sb("sq", [P, 2, T])
        acc = sb("acc", [P, T])
        yt = sb("yt", [P, 2, T])
        pad = sb("pad", [P, 2, T + 2])
        cv = sb("cv", [P, 2, T])
        pm = sb("pm", [P, DEPTH * PML])
        zT = sb("zT", [HEMB, T])
        h2 = sb("h2", [P, T + 4])
        w3 = sb("w3", [P, 4 * HD])
        fw1 = sb("fw1", [HEMB, DEPTH, HHID])
        fw2 = sb("fw2", [HHID, DEPTH, HHID])
        fbf = sb("fbf", [HHID, 4, DEPTH])
        fwl = sb("fwl", [HHID, 2, P])
        eps = sb("eps", [P, 1])
        nm = sb("nm", [P, 2, TC])
        ns = sb("ns", [P, 2, TC])

        with ExitStack() as s:
            gh = sb("gh", [P, DC, T], F32R, s)
            gl = sb("gl", [P, DC, T], F32R, s)
        prob = sb("prob", [P, 2, TC, T])
        probT0 = sb("probT0", [P, TC, T])
        mqf = sb("mqf", [P, MH, T])

        with ExitStack() as s:
            fh = sb("fh", [P, FC, T], F32R, s)
            fl = sb("fl", [P, FC, T], F32R, s)
            gact = sb("gact", [P, T], F32, s)
            fprod = sb("fprod", [P, T], F32, s)
        with ExitStack() as s:
            xio = sb("xio", [P, TC, DM], F32, s)
            pstage = sb("pstage", [P, 3 * DEPTH, P], F32, s)
        uc = sb("uc", [P, 6, T])
        qf = sb("qf", [P, GH // 2, T])
        ka = sb("ka", [P, GKV, T], F32R)
        kb = sb("kb", [P, GKV, T], F32R)
        vg = sb("vg", [P, TC, 3 * GD])
        cq = sb("cq", [P, 2, T])
        ckv = sb("ckv", [P, T])
        kr = sb("kr", [P, T])
        with ExitStack() as s:
            TF = sb("TF", [P, 2, 2, T], F32, s)
            TI = sb("TI", [P, 2, 4, NF], F32, s)
            KP = sb("KP", [P, 2, 2, T], F32, s)
            KM = sb("KM", [P, 2, 2, T], F32, s)
            with ExitStack() as s2:
                h1 = sb("h1", [HHID, T], F32, s2)
                arg = sb("arg", [HHID, 2, T], F32, s2)
                win = sb("win", [P, 2, 4, HD], F32, s2)
                hsum = sb("hsum", [P, 4, T], F32, s2)
                hdif = sb("hdif", [P, 4, T], F32, s2)
            with ExitStack() as s2:
                ut = sb("ut", [P, 4, HD], F32, s2)
                ebuf = sb("ebuf", [P, 2, T], F32, s2)
                fa = sb("fa", [P, 2, T], F32, s2)
                fb = sb("fb", [P, 2, T], F32, s2)
                p1 = sb("p1", [P, 2, T], F32, s2)
                p2 = sb("p2", [P, 2, T], F32, s2)
                ya = sb("ya", [P, 2, T], F32, s2)
        with ExitStack() as s:
            probT1 = sb("probT1", [P, TC, T], F32, s)
            q2 = sb("q2", [P, 2, T], F32R, s)
            mkf = sb("mkf", [P, MH, T], F32, s)
            mv = sb("mv", [P, TC, 2, 3 * MV], F32, s)
            uqr = sb("uqr", [P, 2, MH * MD], F32, s)
            uqh = sb("uqh", [P, 2, MH * MD], F32R, s)
            uql = sb("uql", [P, 2, MH * MD], F32R, s)
            ukr = sb("ukr", [P, T], F32, s)
            ukh = sb("ukh", [P, T], F32R, s)
            ukl = sb("ukl", [P, T], F32R, s)
            cqh = sb("cqh", [P, 2, T], F32R, s)
            cql = sb("cql", [P, 2, T], F32R, s)
            ckh = sb("ckh", [P, T], F32R, s)
            ckl = sb("ckl", [P, T], F32R, s)

        probT = [probT0, probT1]

        ps = ctx.enter_context(nc.psum_tensor("ps", [P, 8, T], F32))

        S = {}
        for name in ("const_in", "x_in", "par_in", "filt_in", "tab_in", "mla_in", "raw0", "raw1", "out_sem",
                     "hi_ready", "lo_ready", "pe_item", "x_tr", "x_first", "par_tr", "par_ok", "const_ok",
                     "gh_ready", "gl_ready", "xsq", "xsq_used", "rbc_ready", "t_ready", "act_self", "act_marks", "head_inv",
                     "ysq", "ysq_used", "ycopy", "stat_post", "rms_post", "x_new",
                     "evac", "conv1", "conv_done", "nsq", "nstat", "nstd", "nrm", "nperm", "roped", "vtr", "vcopy",
                     "khi", "klo",
                     "fw_ok", "f_mm", "f_arg", "f_sin", "fc_mm", "fc_done", "fd_mm", "fd_copy", "fd_done",
                     "ha_mm", "hu_copy", "he_mm", "ho_mm", "he_copy", "h_prod", "hc_mm", "h_done",
                     "q2hi", "q2lo", "s_tile", "nmax", "p_ready", "pt_tile", "pt_act", "pt_dve", "pv", "y_head",
                     "mhi", "mlo", "kr_copy", "b7_full", "b7_free",
                     "gsq", "gsq_used", "gstat", "gstd", "y_norm", "ygh", "ygl",
                     "f_evac", "f_conv1", "f_conv", "f_gelu", "f_prod", "f_hi", "f_lo",
                     "o_tr", "o_copy", "dve_self", "pe_marks", "dve_marks", "pool_marks"):
            S[name] = sem(name)
        dve_self = S["dve_self"]

        def mark(eng, name):
            eng.sem_inc(S[name], 1)

        block = ctx.enter_context(nc.Block())

        def one(w, lay):
            return w[bass.ds(lay, 1)]

        GROUPS = [(uc, 0, 2, 0), (qf, 0, 4, 2), (cq, 0, 2, 6)]
        B7 = []
        for hh in range(MH):
            B7 += [("q", hh), ("perm", hh), ("k", hh)]
        B7 += [("v", s) for s in range(TC)]
        assert len(B7) == 2 * GH
        HEADS = GH + MH

        @block.sync
        def _(sp):
            tok = a["x"].rearrange("b (c p) d -> p (b c) d", p=P)
            sp.dma_start(xio[:], tok).then_inc(S["x_in"], 16)
            for dst, src in ((ident, "c_ident"), (b64, "c_b64"), (perm_g, "c_perm_g"), (perm_m, "c_perm_m"),
                             (rope, "c_rope"), (zT, "c_z")):
                sp.dma_start(dst[:], a[src]).then_inc(S["const_in"], 16)
            for l in range(DEPTH):
                for i, n in enumerate(("hy_filt_b1", "hy_filt_freq1", "hy_filt_b2", "hy_filt_freq2")):
                    sp.dma_start(fbf[:, i, l:l + 1], a[n][l].rearrange("(n o) -> n o", o=1)).then_inc(S["const_in"], 16)
            sp.dma_start(fw1[:], a["hy_filt_w1"].rearrange("l k n -> k l n")).then_inc(S["const_in"], 16)
            sp.dma_start(fw2[:], a["hy_filt_w2"].rearrange("l k n -> k l n")).then_inc(S["const_in"], 16)
            for l in range(DEPTH):
                rows = [("mix_pre", a["mix_pre_norm"][l]), ("hy_w", a["hy_conv_w"][l].rearrange("k n -> (k n)")),
                        ("hy_b", a["hy_conv_b"][l]), ("skip", a["hy_skip"][l].rearrange("k n -> (k n)")),
                        ("mqa", a["mla_q_a_norm"][l]), ("mkva", a["mla_kv_a_norm"][l]),
                        ("mix_post", a["mix_post_norm"][l]), ("ffn_pre", a["ffn_pre_norm"][l]),
                        ("ffn_post", a["ffn_post_norm"][l])]
                for n, v in rows:
                    k = v.shape[0] // P
                    sp.dma_start(pstage[PM[n]:PM[n] + k, 3 * l, :], v.rearrange("(k p) -> k p", p=P)).then_inc(S["par_in"], 16)
                g0 = PM["g_out"]
                for n, o, k in (("hy_out_norm", 0, 2), ("gqa_out_norm", 2, 4), ("mla_out_norm", 6, 2)):
                    sp.dma_start(pstage[g0 + o:g0 + o + k, 3 * l, :],
                                 a[n][l].rearrange("(k p) -> k p", p=P)).then_inc(S["par_in"], 16)
                for n, m in (("gqa_q_norm", "gq"), ("gqa_k_norm", "gk")):
                    for half in range(2):
                        sp.dma_start(pstage[PM[m]:PM[m] + 1, 3 * l, half * GD:(half + 1) * GD],
                                     a[n][l:l + 1, :]).then_inc(S["par_in"], 16)
                fw = a["ffn_conv_w"][l].rearrange("k (c p) -> k c p", p=P)
                for k, (tile, row) in enumerate(((1, 0), (1, 2 * FC), (2, 0))):
                    sp.dma_start(pstage[row:row + 2 * FC, 3 * l + tile, :], fw[k]).then_inc(S["par_in"], 16)
                sp.dma_start(pstage[2 * FC:4 * FC, 3 * l + 2, :],
                             a["ffn_conv_b"][l].rearrange("(c p) -> c p", p=P)).then_inc(S["par_in"], 16)

            w_in = a["w_in"].rearrange("l (c p) n -> l p c n", p=P)
            w_out = a["w_out"].rearrange("l (c p) n -> l p c n", p=P)
            w_up = a["w_up"].rearrange("l (c p) n -> l p c n", p=P)
            w_down = a["w_down"].rearrange("l (c p) n -> l p c n", p=P)

            def item(lay, n, src, tiles=ITEM, cols=P):
                slot = item.slot
                item.slot = 1 - slot
                sp.wait_ge(S["lo_ready"], lay * ITEMS + n + 1)
                dst = raw[:, slot, :].rearrange("p (c n) -> p c n", n=P)[:, 0:tiles, 0:cols]
                sp.dma_start(dst, src.rearrange("o p c n -> (o p) c n")).then_inc(S[f"raw{slot}"], 16)

            item.slot = 0
            for i in range(2):
                item(0, i, w_in[0:1, :, :, i * P:(i + 1) * P])
            sp.wait_ge(S["par_ok"], 3 * DEPTH)
            with sp.Fori(0, DEPTH) as lay:
                sp.wait_ge(S["x_new"], lay * 2 * DC + DC)
                for lo in range(0, 4 * HD, T):
                    sp.dma_start(w3[0:HHID, lo:lo + T], one(a["hy_filt_w3"], lay).rearrange("o k n -> (o k) n")[:, lo:lo + T]
                                 ).then_inc(S["filt_in"], 16)
                sp.dma_start(win[:], a["c_win"]).then_inc(S["filt_in"], 16)
                for i in range(2, 4):
                    item(lay, i, w_in[bass.ds(lay, 1), :, :, i * P:(i + 1) * P])
                sp.dma_start(TF[:], a["c_tf"]).then_inc(S["tab_in"], 16)
                sp.dma_start(TI[:], a["c_ti"]).then_inc(S["tab_in"], 16)
                with sp.Fori(4, WIN - 3, 2) as i:
                    for j in range(2):
                        item(lay, i + j, w_in[bass.ds(lay, 1), :, :, bass.ds((i + j) * P, P)])
                for i in range(WIN - 2, WIN):
                    w = min(P, D_IN - i * P)
                    item(lay, i, w_in[bass.ds(lay, 1), :, :, i * P:i * P + w], cols=w)
                for i in range(2):
                    item(lay, I_OUT + i, w_out[bass.ds(lay, 1), :, :, i * P:(i + 1) * P])
                sp.wait_ge(S["h_done"], lay * 2 + 2)
                sp.dma_start(uqr[:], one(a["mla_w_uq"], lay).rearrange("o (c p) n -> (o p) c n", p=P)).then_inc(S["mla_in"], 16)
                sp.dma_start(ukr[:], one(a["mla_w_ukv"], lay).rearrange("o p n -> (o p) n")).then_inc(S["mla_in"], 16)
                with sp.Fori(2, DC - 1, 2) as i:
                    for j in range(2):
                        item(lay, I_OUT + i + j, w_out[bass.ds(lay, 1), :, :, bass.ds((i + j) * P, P)])
                with sp.Fori(0, FC) as j:
                    item(lay, I_UP + 2 * j, w_up[bass.ds(lay, 1), :, :, bass.ds(j * P, P)])
                    item(lay, I_UP + 2 * j + 1, w_up[bass.ds(lay, 1), :, :, bass.ds(DFF + j * P, P)])
                with sp.Fori(0, DC - 1, 2) as m:
                    for j in range(2):
                        for i, (k, n) in enumerate(DOWN_PARTS):
                            item(lay, I_DOWN + (m + j) * 3 + i,
                                 w_down[bass.ds(lay, 1), :, k:k + n, bass.ds((m + j) * P, P)], tiles=n)
                assert DEPTH == 2
                for i in range(2):
                    item(lay, ITEMS + i, w_in[DEPTH - 1:DEPTH, :, :, i * P:(i + 1) * P])
            res = out.rearrange("b (c p) d -> p (b c) d", p=P)
            for c in range(TC):
                sp.wait_ge(S["o_copy"], 2 * c + 2)
                sp.dma_start(res[:, c, :], xio[:, c, :]).then_inc(S["out_sem"], 16)
            sp.wait_ge(S["out_sem"], 16 * TC)

        @block.gpsimd
        def _(pool):
            nc.gpsimd.memset(ones[:], 1.0)
            nc.gpsimd.memset(eps[:], EPS)
            nc.gpsimd.memset(h2[:], 0.0)
            nc.gpsimd.memset(w3[:], 0.0)
            nc.gpsimd.memset(pad[:], 0.0)
            nc.gpsimd.memset(fwl[:], 0.0)
            nc.gpsimd.memset(raw[:], 0.0).then_inc(S["const_ok"], 1)
            pool.wait_ge(S["const_ok"], 1)
            pool.sem_inc(S["lo_ready"], 2)

            def lo(g, slot):
                pool.wait_ge(S["hi_ready"], g + 1)
                nc.gpsimd.tensor_tensor(wl[:, slot, :], raw[:, slot, :], wh[:, slot, :].bitcast(F32),
                                        ALU.subtract).then_inc(S["lo_ready"], 1)

            def add(lay, b):
                for c in range(DC):
                    pool.wait_ge(S["t_ready"], (lay * 2 + b) * DC + c + 1)
                    nc.gpsimd.tensor_tensor(xT[:, c, :], xT[:, c, :], cv[:, c % 2, :], ALU.add).then_inc(S["x_new"], 1)

            lo(0, 0)
            lo(1, 1)
            pool.wait_ge(S["x_first"], DC)
            pool.sem_inc(S["x_new"], DC)
            with pool.Fori(0, DEPTH) as lay:
                with pool.Fori(2, I_OUT + 1, 2) as n:
                    for slot in range(2):
                        lo(lay * ITEMS + n + slot, slot)
                for h in range(GH):
                    half = h % 2
                    rows, other = slice(half * GD, (half + 1) * GD), slice((1 - half) * GD, (2 - half) * GD)
                    if h == 0:
                        pool.wait_ge(S["lo_ready"], lay * ITEMS + I_OUT + 4)
                    else:
                        pool.wait_ge(S["q2lo"], lay * GH + h)
                    pool.wait_ge(S["q2hi"], lay * GH + h + 1)
                    nc.gpsimd.tensor_tensor(q2[other, half, :], qf[rows, h // 2, :], q2[rows, half, :].bitcast(F32),
                                            ALU.subtract).then_inc(S["q2lo"], 1)
                pool.wait_ge(S["q2lo"], lay * GH + GH)
                mark(pool, "pool_marks")
                with pool.Fori(I_OUT + 2, I_UP + 1, 2) as n:
                    for slot in range(2):
                        lo(lay * ITEMS + n + slot, slot)
                add(lay, 0)
                with pool.Fori(I_UP + 2, ITEMS + 1, 2) as n:
                    for slot in range(2):
                        lo(lay * ITEMS + n + slot, slot)
                add(lay, 1)

        @block.scalar
        def _(act):
            A = nc.scalar.activation

            def hi(lay, n, slot):
                g = lay * ITEMS + n
                act.wait_ge(S[f"raw{slot}"], lay * (8 * ITEMS) + n * 8 + (16 - 8 * slot))
                act.wait_ge(S["pe_item"], g + 1)
                A(wh[:, slot, :], raw[:, slot, :], ACT.Copy).then_inc(S["hi_ready"], 1)

            C = Chain(act, S["act_self"])

            def inverse_root(dst, tmp, src, width, bias=True):
                if bias:
                    C.do(A(tmp, src, ACT.Ln, bias=eps[:, 0:1], scale=1.0 / width))
                else:
                    C.do(A(tmp, src, ACT.Ln))
                C.join()
                return A(dst, tmp, ACT.Exp, scale=-0.5 if bias else -1.0)

            def tables(name):
                nc.scalar.preload_act_table_set(name)

            def prep(q, off):
                for c in range(DC):
                    act.wait_ge(S["x_new"], q * DC + c + 1)
                    A(gh[:, c, :], xT[:, c, :], ACT.Copy, scale=pm[:, bass.ds(off + c, 1)]).then_inc(S["gh_ready"], 1)
                    if c >= 2:
                        act.wait_ge(S["xsq_used"], q * DC + c - 1)
                    A(sq[:, c % 2, :], xT[:, c, :], ACT.Square).then_inc(S["xsq"], 1)
                act.wait_ge(S["xsq_used"], q * DC + DC)
                inverse_root(rbc[:], std[:], ps[:, 1, :], DM).then_inc(S["rbc_ready"], 1)

            def ysquare(lay, b, m):
                k = (lay * 2 + b) * DC + m
                if m >= 2:
                    act.wait_ge(S["ysq_used"], k - 1)
                A(sq[:, m % 2, :], ps[:, m, :], ACT.Square).then_inc(S["ysq"], 1)
                if m < 2:
                    A(yt[:, m, :], ps[:, m, :], ACT.Copy).then_inc(S["ycopy"], 1)

            def post(lay, b):
                act.wait_ge(S["stat_post"], lay * 2 + b + 1)
                inverse_root(rr[:, 0, :], std[:], ps[:, 0, :], DM).then_inc(S["rms_post"], 1)

            for c in range(DC):
                act.wait_ge(S["x_tr"], c + 1)
                A(xT[:, c, :], ps[:, c % 4, :], ACT.Copy).then_inc(S["x_first"], 1)
            for i in range(3 * DEPTH):
                act.wait_ge(S["par_tr"], i + 1)
                n = PM_ROWS[i % 3]
                A(pm[:, i * P:i * P + n], ps[:, 4 + i % 3, 0:n], ACT.Copy).then_inc(S["par_ok"], 1)
            act.wait_ge(S["x_first"], DC)
            act.wait_ge(S["par_ok"], 3 * DEPTH)
            act.wait_ge(S["const_ok"], 1)
            tables("natural_log_exp_and_others")
            hi(0, 0, 0)
            hi(0, 1, 1)

            with act.Fori(0, DEPTH) as lay:
                C.restart()
                col = lay * PML

                def par(name, i=0):
                    return pm[:, bass.ds(col + (PM[name] + i), 1)]

                def sines(k):
                    dst = h1[:] if k == 0 else h2[0:HHID, 1:T + 1]
                    act.wait_ge(S["f_arg"], lay * 2 + k + 1)
                    A(dst, arg[:, 0, :], ACT.Sin).then_inc(S["f_sin"], 1)

                def conv1(i):
                    act.wait_ge(S["evac"], lay * WIN + i + 1)
                    A(uc[:, i, :], pad[:, i % 2, 1:T + 1], ACT.Identity, scale=par("hy_w", 6 + i),
                      bias=par("hy_b", i)).then_inc(S["conv1"], 1)

                nsq_n = [0]

                def squares(i, src):
                    act.wait_ge(S["evac"], lay * WIN + i + 1)
                    k = nsq_n[0]
                    nsq_n[0] += 1
                    if k >= 2:
                        act.wait_ge(S["nstat"], lay * 7 + {2: 1, 3: 2, 4: 3, 5: 4, 6: 5, 7: 6}[k])
                    A(sq[:, k % 2, :], src, ACT.Square).then_inc(S["nsq"], 1)

                def root(k, width):
                    if k:
                        act.wait_ge(S["nrm"], lay * 7 + k)
                    act.wait_ge(S["nstat"], lay * 7 + k + 1)
                    inverse_root(rr[:, 0, :], std[:], ps[:, 2, :], width).then_inc(S["nstd"], 1)

                def filt_copy(k):
                    act.wait_ge(S["fd_mm"], lay * 8 + 2 * k + 1)
                    if k:
                        act.wait_ge(S["fd_done"], lay * 4 + k)
                    A(yt[:, 0, :], ps[:, 4 + 2 * (k % 2), :], ACT.Copy).then_inc(S["fd_copy"], 1)

                def u_copy(o):
                    act.wait_ge(S["ha_mm"], lay * 2 + o + 1)
                    A(ut[:].rearrange("p (b c) d -> p b (c d)", b=2), ps[:, 4:6, :], ACT.Copy).then_inc(S["hu_copy"], 1)

                def e_copy(o):
                    act.wait_ge(S["he_mm"], lay * 2 + o + 1)
                    A(ebuf[:], ps[:, 6:8, :], ACT.Copy).then_inc(S["he_copy"], 1)

                prep(lay * 2, col + PM["mix_pre"])
                sines(0)
                for t in range(WIN + 2):
                    if 2 <= t + 1 < I_OUT + 2:
                        hi(lay, t + 1, (t + 1) % 2)
                    if t == 0:
                        sines(1)
                        tables("natural_log_exp_and_others")
                    i = t - 1
                    if 0 <= i < C_Q:
                        conv1(i)
                    if C_Q <= i < C_K:
                        squares(i, qf[:, i - C_Q, :])
                    if i == C_K:
                        squares(i, cv[:, 0, :])
                    if i in (C_MQ, C_MQ + 1):
                        squares(i, cq[:, i - C_MQ, :])
                    if i == C_MKV:
                        squares(i, ckv[:])
                    if C_Q <= t - 2 <= C_K:
                        root(t - 2 - C_Q, GD)
                    if t == C_MQ + 3:
                        root(5, MQR)
                    if t == C_MKV + 2:
                        root(6, MKVR)
                    if t in (6, 7):
                        filt_copy(2 * (t - 6))
                        filt_copy(2 * (t - 6) + 1)
                    if t == 8:
                        u_copy(0)
                    if t == 9:
                        e_copy(0)
                    if t == 12:
                        u_copy(1)
                    if t == 13:
                        e_copy(1)
                act.wait_ge(S["roped"], lay * 6 + 5)
                for kv in range(GKV):
                    rows = slice(kv * GD, (kv + 1) * GD)
                    for half in range(2):
                        A(ka[half * GD:(half + 1) * GD, kv, :], cv[rows, 0, :], ACT.Copy).then_inc(S["khi"], 1)

                gsq_n = [0]

                def group(g):
                    src, c0, n, _ = GROUPS[g]
                    for c in range(n):
                        k = gsq_n[0]
                        gsq_n[0] += 1
                        if k >= 2:
                            act.wait_ge(S["gsq_used"], lay * DC + k - 1)
                        A(sq[:, k % 2, :], src[:, c, :], ACT.Square).then_inc(S["gsq"], 1)
                    act.wait_ge(S["gstat"], lay * 3 + g + 1)
                    if g:
                        act.wait_ge(S["y_norm"], lay * DC + GROUPS[g][3])
                    inverse_root(rr[:, 0, :], std[:], ps[:, 7, :], n * P).then_inc(S["gstd"], 1)

                act.wait_ge(S["h_done"], lay * 2 + 2)
                group(0)

                act.wait_ge(S["mla_in"], lay * 32 + 32)
                for dst, src in ((cqh, cq), (ckh, ckv), (uqh, uqr), (ukh, ukr)):
                    A(dst[:], src[:], ACT.Copy).then_inc(S["mhi"], 1)
                act.wait_ge(S["roped"], lay * 6 + 6)
                for hh in range(MH):
                    A(mkf[MN:MD, hh, :], kr[MN:MD, :], ACT.Copy).then_inc(S["kr_copy"], 1)

                def q_hi(h):
                    rows = slice((h % 2) * GD, (h % 2 + 1) * GD)
                    if h >= 2:
                        act.wait_ge(S["s_tile"], lay * 4 * HEADS + 4 * (h - 1))
                    A(q2[rows, h % 2, :], qf[rows, h // 2, :], ACT.Copy).then_inc(S["q2hi"], 1)

                def exps(h):
                    scale = GD ** -0.5 if h < GH else MD ** -0.5
                    act.wait_ge(S["nmax"], lay * HEADS + h + 1)
                    if h >= 2:
                        act.wait_ge(S["pt_tile"], lay * 4 * HEADS + 4 * (h - 1))
                    for qc in range(TC):
                        A(prob[:, h % 2, qc, :], ps[:, qc, :], ACT.Exp, bias=ns[:, h % 2, qc:qc + 1],
                          scale=scale).then_inc(S["p_ready"], 1)

                def pt_copy(h, sc):
                    act.wait_ge(S["pt_tile"], lay * 4 * HEADS + 4 * h + sc + 1)
                    if h >= 2 and sc == 0:
                        act.wait_ge(S["pv"], lay * HEADS + h - 1)
                    A(probT[h % 2][:, sc, :], ps[:, 4, :], ACT.Copy).then_inc(S["pt_act"], 1)

                def denominators(h):
                    act.wait_ge(S["pv"], lay * HEADS + h + 1)
                    swapped = (h // 4) % 2 if h < GH else h % 2
                    o_rows = slice(GD, 2 * GD) if swapped else slice(0, GD)
                    d_rows = slice(0, GD) if swapped else slice(GD, 2 * GD)
                    if h >= 2:
                        act.wait_ge(S["y_head"], lay * HEADS + h - 1)
                    inverse_root(rr[o_rows, h % 2, :], std[o_rows, :], ps[d_rows, 6, :], 1,
                                 bias=False).then_inc(S["head_inv"], 1)

                act.wait_ge(S["y_norm"], lay * DC + 2)
                q_hi(0)
                q_hi(1)
                exps(0)
                for h in range(HEADS):
                    pt_copy(h, 0)
                    if h + 1 < HEADS:
                        exps(h + 1)
                    if h + 2 < GH:
                        q_hi(h + 2)
                    if h:
                        denominators(h - 1)
                    pt_copy(h, 2)
                denominators(HEADS - 1)
                for g, heads in ((1, GH), (2, HEADS)):
                    act.wait_ge(S["y_head"], lay * HEADS + heads)
                    group(g)
                for g, (src, _, n, c0) in enumerate(GROUPS):
                    for c in range(n):
                        act.wait_ge(S["y_norm"], lay * DC + c0 + c + 1)
                        A(gh[:, c0 + c, :], src[:, c, :], ACT.Copy).then_inc(S["ygh"], 1)

                for m in range(DC):
                    act.wait_ge(S["pe_item"], lay * ITEMS + I_OUT + m + 3)
                    ysquare(lay, 0, m)
                    hi(lay, I_OUT + m + 2, m % 2)
                post(lay, 0)
                prep(lay * 2 + 1, col + PM["ffn_pre"])

                tables("gelu_apprx_tanh_and_others")
                mark(act, "act_marks")
                with act.Fori(0, FC) as j:
                    r = lay * FC + j

                    def tap(k, b):
                        act.wait_ge(S["f_evac"], r * 2 + k + 3)
                        A(cv[:, k, :], pad[:, k, 1:T + 1], ACT.Identity,
                          scale=pm[:, bass.ds(col + j + (PM["ffn_w1"] + k * FC), 1)],
                          bias=pm[:, bass.ds(col + j + (PM["ffn_b"] + k * FC), 1)]).then_inc(S["f_conv1"], 1)

                    tap(0, 0)
                    hi(lay, j * 2 + (I_UP + 2), 0)
                    act.wait_ge(S["f_conv"], r * 2 + 1)
                    A(gact[:], cv[:, 0, :], ACT.Gelu_apprx_tanh).then_inc(S["f_gelu"], 1)
                    tap(1, 1)
                    hi(lay, j * 2 + (I_UP + 3), 1)
                    act.wait_ge(S["f_prod"], r + 1)
                    A(fh[:, bass.ds(j, 1), :], fprod[:].rearrange("p (o t) -> p o t", o=1), ACT.Copy).then_inc(S["f_hi"], 1)

                tables("natural_log_exp_and_others")
                for m in range(DC):
                    for i in range(len(DOWN_PARTS)):
                        n = I_DOWN + 3 * m + i
                        hi(lay, n + 2, n % 2)
                    act.wait_ge(S["pe_item"], lay * ITEMS + I_DOWN + 3 * m + 2 + 3)
                    ysquare(lay, 1, m)
                post(lay, 1)
                C.join()
                mark(act, "act_marks")

            for c in range(TC):
                for b in range(2):
                    k = 2 * c + b
                    act.wait_ge(S["o_tr"], k + 1)
                    A(xio[:, c, b * T:(b + 1) * T], ps[:, 4 + k % 4, :], ACT.Copy).then_inc(S["o_copy"], 1)

        @block.tensor
        def _(pe):
            mm = nc.tensor.matmul

            pe.wait_ge(S["const_in"], 16 * (6 + 4 * DEPTH + 2))
            pe.wait_ge(S["x_in"], 16)
            for c in range(DC):
                if c >= 4:
                    pe.wait_ge(S["x_first"], c - 3)
                for t in range(TC):
                    ins = nc.tensor.transpose(ps[:, c % 4, t * P:(t + 1) * P], xio[:, t, c * P:(c + 1) * P], ident[:])
                ins.then_inc(S["x_tr"], 1)
            pe.wait_ge(S["par_in"], 16 * DEPTH * 20)
            for i in range(3 * DEPTH):
                n = PM_ROWS[i % 3]
                if i >= 3:
                    pe.wait_ge(S["par_ok"], i - 2)
                nc.tensor.transpose(ps[:, 4 + i % 3, 0:n], pstage[0:n, i, :], ident[0:n, 0:n]).then_inc(S["par_tr"], 1)
            pe.wait_ge(S["const_ok"], 1)
            pe.sem_inc(S["pe_item"], 2)

            def square_sum(q, k):
                pe.wait_ge(S["xsq"], q * DC + k + 1)
                mm(ps[:, 1, :], ones[:], sq[:, k % 2, :], start=(k == 0), stop=(k == DC - 1)).then_inc(S["xsq_used"], 1)

            def stat_post(lay, b):
                pe.wait_ge(S["ysq_used"], (lay * 2 + b) * DC + DC)
                pe.wait_ge(S["ycopy"], (lay * 2 + b) * 2 + 2)
                mm(ps[:, 0, :], ones[:], acc[:], start=True, stop=True).then_inc(S["stat_post"], 1)

            def tiles(lay, n, slot, bank, tile_n, rh, rl, k0, start, stop, cols=P, gate=None):
                g = lay * ITEMS + n
                pe.wait_ge(S["hi_ready"], g + 1)
                pe.wait_ge(S["lo_ready"], g + 3)
                for k in range(tile_n):
                    if gate:
                        gate(k)
                    w_hi = wh[:, slot, k * P:k * P + cols]
                    w_lo = wl[:, slot, k * P:k * P + cols]
                    x_hi, x_lo = rh[:, k0 + k, :], rl[:, k0 + k, :]
                    mm(ps[0:cols, bank, :], w_hi, x_hi, start=start and k == 0, stop=False)
                    mm(ps[0:cols, bank, :], w_hi, x_lo, start=False, stop=False)
                    ins = mm(ps[0:cols, bank, :], w_lo, x_hi, start=False, stop=stop and k == tile_n - 1)
                ins.then_inc(S["pe_item"], 1)

            with pe.Fori(0, DEPTH) as lay:
                def item(t):
                    if t >= 2:
                        pe.wait_ge(S["evac"], lay * WIN + t - 1)
                    cols = min(P, D_IN - t * P)

                    def gate(k):
                        if t == 0:
                            square_sum(lay * 2, k)
                            pe.wait_ge(S["gh_ready"], lay * 2 * DC + k + 1)
                            pe.wait_ge(S["gl_ready"], lay * 2 * DC + k + 1)
                    if t == 1:
                        pe.wait_ge(S["rbc_ready"], lay * 2 + 1)
                    tiles(lay, t, t % 2, t % 2, DC, gh, gl, 0, True, True, cols, gate)

                def filt_taps(j):
                    par_, c = divmod(j, 2)
                    if j == 0:
                        pe.wait_ge(S["f_sin"], lay * 2 + 2)
                        pe.wait_ge(S["filt_in"], lay * 48 + 48)
                    if j >= 2:
                        pe.wait_ge(S["fc_done"], lay * 4 + j - 1)
                    b = 4 + 2 * (j % 2)
                    w = w3[:].rearrange("k (o d n) -> k d o n", o=2, d=2)
                    t0 = 2 * P * c + par_
                    for d in range(2):
                        lo = t0 + 1 - d
                        ins = mm(ps[:, b + d, :].rearrange("p (o n) -> p o n", o=2), h2[:, lo:lo + 2 * P - 1:2], w[:, d, :, :],
                                 start=True, stop=True)
                    ins.then_inc(S["fc_mm"], 1)

                def filt_spec(k):
                    b = 4 + 2 * (k % 2)
                    if k == 0:
                        pe.wait_ge(S["tab_in"], lay * 32 + 32)
                        pe.wait_ge(S["fc_done"], lay * 4 + 4)
                    if k >= 2:
                        pe.wait_ge(S["fd_done"], lay * 4 + k - 1)
                    src = hsum if k < 2 else hdif
                    for par_ in range(2):
                        for c in range(2):
                            ins = mm(ps[:, b + par_, :], TF[:, par_, c, k * P:(k + 1) * P], src[:, 2 * par_ + c, :],
                                     start=(c == 0), stop=(c == 1))
                        ins.then_inc(S["fd_mm"], 1)

                def h_turn(o):
                    if o == 0:
                        pe.wait_ge(S["fd_done"], lay * 4 + 4)
                        pe.wait_ge(S["conv_done"], lay * 6 + 6)
                    else:
                        pe.wait_ge(S["h_done"], lay * 2 + 1)
                    for j in range(4):
                        par_, c = divmod(j, 2)
                        for cc in range(2):
                            t0 = 2 * P * c + par_
                            at = (j % 2) * HD + cc * P
                            ins = nc.tensor.transpose(ps[:, 4 + j // 2, at:at + P], uc[:, cc, t0:t0 + 2 * P - 1:2], ident[:])
                    ins.then_inc(S["ha_mm"], 1)

                def h_forward(o):
                    pe.wait_ge(S["hu_copy"], lay * 2 + o + 1)
                    for par_ in range(2):
                        for k in range(4):
                            b = (6 if par_ == 0 else 4) + k // 2
                            for c in range(2):
                                ins = mm(ps[:, b, (k % 2) * HD:(k % 2 + 1) * HD], TF[:, par_, c, k * P:(k + 1) * P],
                                         ut[:, 2 * par_ + c, :], start=(c == 0), stop=(c == 1))
                        ins.then_inc(S["he_mm" if par_ == 0 else "ho_mm"], 1)

                def h_inverse(o):
                    pe.wait_ge(S["h_prod"], lay * 2 + o + 1)
                    for cc in range(2):
                        for par_ in range(2):
                            spec = fa if par_ == 0 else fb
                            for k in range(4):
                                ri, fc = divmod(k, 2)
                                lo = fc * HD + cc * P
                                ins = mm(ps[:, 6 + cc, par_ * NF:(par_ + 1) * NF], spec[:, ri, lo:lo + P],
                                         TI[:, par_, k, :], start=(k == 0), stop=(k == 3))
                    ins.then_inc(S["hc_mm"], 1)

                def stat(k, chunks, weights, first_sq):
                    pe.wait_ge(S["nsq"], lay * 8 + first_sq + len(chunks))
                    if k:
                        pe.wait_ge(S["nstd"], lay * 7 + k)
                    for n, s_ in enumerate(chunks):
                        ins = mm(ps[:, 2, :], weights[:], sq[:, s_, :], start=(n == 0), stop=(n == len(chunks) - 1))
                    ins.then_inc(S["nstat"], 1)

                def permute(k, src):
                    pe.wait_ge(S["nrm"], lay * 7 + k + 1)
                    if k:
                        pe.wait_ge(S["roped"], lay * 6 + k)
                    mm(ps[:, 3, :], perm_g[:], src, start=True, stop=True).then_inc(S["nperm"], 1)

                pe.wait_ge(S["fw_ok"], lay + 1)
                mm(ps[:, 4, :], fwl[0:HEMB, 0, :], zT[:], start=True, stop=True).then_inc(S["f_mm"], 1)
                item(0)
                pe.wait_ge(S["f_sin"], lay * 2 + 1)
                mm(ps[:, 4, :], fwl[:, 1, :], h1[:], start=True, stop=True).then_inc(S["f_mm"], 1)
                for t in range(1, WIN + 2):
                    if 2 <= t < 6:
                        filt_taps(t - 2)
                    if t in (6, 7):
                        filt_spec(2 * (t - 6))
                        filt_spec(2 * (t - 6) + 1)
                    if t == 8:
                        h_turn(0)
                    if t == 9:
                        h_forward(0)
                    if t == 12:
                        h_turn(1)
                    if t == 13:
                        h_forward(1)
                    if t < WIN:
                        item(t)
                    if C_Q <= t - 1 <= C_K:
                        stat(t - 1 - C_Q, [(t - 1 - C_Q) % 2], b64, t - 1 - C_Q)
                    if C_Q <= t - 2 < C_K:
                        permute(t - 2 - C_Q, qf[:, t - 2 - C_Q, :])
                    if t - 2 == C_K:
                        permute(4, cv[:, 0, :])
                    if t == C_V + 2:
                        pe.wait_ge(S["evac"], lay * WIN + C_V + 1)
                        pe.wait_ge(S["roped"], lay * 6 + 5)
                        for s_ in range(TC):
                            ins = nc.tensor.transpose(ps[:, 3, s_ * P:(s_ + 1) * P], cv[:, 1, s_ * P:(s_ + 1) * P], ident[:])
                        ins.then_inc(S["vtr"], 1)
                    if t == 11:
                        h_inverse(0)
                    if t == C_MQ + 2:
                        stat(5, [1, 0], ones, 5)
                    if t == C_MKV + 1:
                        stat(6, [1], ones, 7)
                        h_inverse(1)
                    if t == WIN:
                        pe.wait_ge(S["evac"], lay * WIN + WIN)
                        pe.wait_ge(S["vcopy"], lay + 1)
                        mm(ps[0:MD, 3, :], perm_m[:], kr[0:MD, :], start=True, stop=True).then_inc(S["nperm"], 1)

                def group(g):
                    n = GROUPS[g][2]
                    if g:
                        pe.wait_ge(S["gstd"], lay * 3 + g)
                    pe.wait_ge(S["gsq_used"], lay * DC + GROUPS[g][3] + n)
                    mm(ps[:, 7, :], ones[:], acc[:], start=True, stop=True).then_inc(S["gstat"], 1)

                pe.wait_ge(S["h_done"], lay * 2 + 2)
                group(0)

                def scores(h):
                    for qc in range(TC):
                        cols = slice(qc * P, (qc + 1) * P)
                        if h == 0:
                            if qc == 0:
                                pe.wait_ge(S["evac"], lay * WIN + WIN)
                            if qc == 2:
                                pe.wait_ge(S["nstd"], lay * 7 + 7)
                            if qc == 3:
                                pe.wait_ge(S["roped"], lay * 6 + 6)
                        else:
                            pe.wait_ge(S["p_ready"], (lay * HEADS + h - 1) * 4 + qc + 1)
                        if h < GH:
                            if qc == 0:
                                pe.wait_ge(S["q2hi"], lay * GH + h + 1)
                                pe.wait_ge(S["q2lo"], lay * GH + h + 1)
                                if h == 0:
                                    pe.wait_ge(S["khi"], lay * 4 + 4)
                                    pe.wait_ge(S["klo"], lay * 4 + 4)
                            mm(ps[:, qc, :], q2[:, h % 2, cols], ka[:, h // 4, :], start=True, stop=False)
                            mm(ps[:, qc, :], q2[:, h % 2, cols], kb[:, h // 4, :], start=False, stop=True) \
                                .then_inc(S["s_tile"], 1)
                        else:
                            if h == GH and qc == 0:
                                pe.wait_ge(S["b7_free"], lay * len(B7) + 3 * MH)
                                pe.wait_ge(S["kr_copy"], lay * MH + MH)
                            mm(ps[:, qc, :], mqf[0:MD, h - GH, cols], mkf[0:MD, h - GH, :], start=True, stop=True) \
                                .then_inc(S["s_tile"], 1)

                def bank7(k):
                    kind, i = B7[k]
                    if k:
                        pe.wait_ge(S["b7_free"], lay * len(B7) + k)
                    else:
                        pe.wait_ge(S["gstd"], lay * 3 + 1)
                        pe.wait_ge(S["mhi"], lay * 4 + 4)
                        pe.wait_ge(S["mlo"], lay * 4 + 4)
                    if kind == "q":
                        n, last = 0, 5
                        for c in range(2):
                            for w, x in ((uqh, cqh), (uqh, cql), (uql, cqh)):
                                ins = mm(ps[0:MD, 7, :], w[:, c, i * MD:(i + 1) * MD], x[:, c, :], start=(n == 0), stop=(n == last))
                                n += 1
                    elif kind == "perm":
                        ins = mm(ps[0:MD, 7, :], perm_m[:], mqf[0:MD, i, :], start=True, stop=True)
                    elif kind == "k":
                        for n, (w, x) in enumerate(((ukh, ckh), (ukh, ckl), (ukl, ckh))):
                            ins = mm(ps[0:MN, 7, :], w[:, i * P:i * P + MN], x[:], start=(n == 0), stop=(n == 2))
                    else:
                        cols = slice(i * P, (i + 1) * P)
                        for n, (w, x) in enumerate(((ckh, ukh), (ckh, ukl), (ckl, ukh))):
                            ins = mm(ps[:, 7, :], w[:, cols], x[:], start=(n == 0), stop=(n == 2))
                    ins.then_inc(S["b7_full"], 1)

                def turn(h, tiles_):
                    pe.wait_ge(S["p_ready"], (lay * HEADS + h) * 4 + 4)
                    for sc in tiles_:
                        if sc >= 2 or h:
                            k = (lay * HEADS + h) * 2 + sc // 2
                            pe.wait_ge(S["pt_act" if sc % 2 == 0 else "pt_dve"], k)
                        for qc in range(TC):
                            ins = nc.tensor.transpose(ps[:, 4 + sc % 2, qc * P:(qc + 1) * P],
                                                      prob[:, h % 2, qc, sc * P:(sc + 1) * P], ident[:])
                        ins.then_inc(S["pt_tile"], 1)

                def values(h):
                    if h:
                        pe.wait_ge(S["y_head"], lay * HEADS + h)
                    if h == 0:
                        pe.wait_ge(S["vcopy"], lay + 1)
                    if h == GH:
                        pe.wait_ge(S["b7_free"], lay * len(B7) + len(B7))
                    pe.wait_ge(S["pt_act"], (lay * HEADS + h) * 2 + 2)
                    pe.wait_ge(S["pt_dve"], (lay * HEADS + h) * 2 + 2)
                    for sc in range(TC):
                        if h < GH:
                            v = vg[:, sc, (h // 4) * GD:(h // 4) * GD + P]
                        else:
                            i = h - GH
                            v = mv[:, sc, i // 2, (i % 2) * MV:(i % 2) * MV + P]
                        ins = mm(ps[:, 6, :], v, probT[h % 2][:, sc, :], start=(sc == 0), stop=(sc == TC - 1))
                    ins.then_inc(S["pv"], 1)

                scores(0)
                for h in range(HEADS):
                    if h + 1 < HEADS:
                        scores(h + 1)
                    if h < GH:
                        bank7(2 * h)
                    turn(h, (0, 1))
                    if h:
                        values(h - 1)
                    turn(h, (2, 3))
                    if h < GH:
                        bank7(2 * h + 1)
                values(HEADS - 1)
                group(1)
                group(2)

                def gate_out(k):
                    pe.wait_ge(S["ygh"], lay * DC + k + 1)
                    pe.wait_ge(S["ygl"], lay * DC + k + 1)

                pe.wait_ge(S["p_ready"], (lay * HEADS + HEADS) * 4)
                pe.wait_ge(S["y_head"], lay * HEADS + HEADS)
                for m in range(DC):
                    if m == DC - 1:
                        pe.wait_ge(S["gstd"], lay * 3 + 3)
                    tiles(lay, I_OUT + m, m % 2, m, DC, gh, gl, 0, True, True, gate=gate_out if m == 0 else None)
                stat_post(lay, 0)

                def gate_up(k):
                    if k == 0:
                        pe.wait_ge(S["t_ready"], lay * 2 * DC + 3)
                    square_sum(lay * 2 + 1, k)
                    pe.wait_ge(S["gh_ready"], (lay * 2 + 1) * DC + k + 1)
                    pe.wait_ge(S["gl_ready"], (lay * 2 + 1) * DC + k + 1)

                def up(j, gate=None):
                    for k in range(2):
                        pe.wait_ge(S["f_evac"], (lay * FC + j) * 2 + k + 1)
                        tiles(lay, j * 2 + (I_UP + k), k, 2 + k, DC, gh, gl, 0, True, True,
                              gate=gate if k == 0 else None)

                up(0, gate_up)
                mark(pe, "pe_marks")
                with pe.Fori(1, FC) as j:
                    up(j)

                pe.wait_ge(S["f_evac"], lay * 2 * FC + 2 * FC + 2)
                pe.wait_ge(S["rbc_ready"], lay * 2 + 2)
                for m in range(DC):
                    for i, (k0, n) in enumerate(DOWN_PARTS):
                        last = i == len(DOWN_PARTS) - 1

                        def gate_down(k, k0=k0):
                            if m == 0:
                                pe.wait_ge(S["f_hi"], lay * FC + k0 + k + 1)
                                pe.wait_ge(S["f_lo"], lay * FC + k0 + k + 1)

                        tiles(lay, I_DOWN + 3 * m + i, (3 * m + i) % 2, m, n, fh, fl, k0, i == 0, last, gate=gate_down)
                stat_post(lay, 1)

            pe.wait_ge(S["x_new"], (2 * DEPTH + 1) * DC)
            for c in range(TC):
                for b in range(2):
                    k = 2 * c + b
                    if k >= 4:
                        pe.wait_ge(S["o_copy"], k - 3)
                    for i in range(4):
                        ins = nc.tensor.transpose(ps[:, 4 + k % 4, i * P:(i + 1) * P],
                                                  xT[:, 4 * b + i, c * P:(c + 1) * P], ident[:])
                    ins.then_inc(S["o_tr"], 1)

        @block.vector
        def _(dve):
            V = Chain(dve, dve_self)
            tt, ts, stt = nc.vector.tensor_tensor, nc.vector.tensor_scalar, nc.vector.scalar_tensor_tensor
            copy = nc.vector.tensor_copy

            def operand_lo(q, off, c):
                dve.wait_ge(S["gh_ready"], q * DC + c + 1)
                stt(out=gl[:, c, :], in0=xT[:, c, :], scalar=pm[:, bass.ds(off + c, 1)], in1=gh[:, c, :].bitcast(F32),
                    op0=ALU.mult, op1=ALU.subtract).then_inc(S["gl_ready"], 1)

            def ysum(lay, b, m):
                k = (lay * 2 + b) * DC + m
                dve.wait_ge(S["ysq"], k + 1)
                if m == 0:
                    copy(acc[:], sq[:, 0, :]).then_inc(S["ysq_used"], 1)
                else:
                    dve.wait_ge(S["ysq_used"], k)
                    tt(acc[:], acc[:], sq[:, m % 2, :], ALU.add).then_inc(S["ysq_used"], 1)

            def step(lay, b, gain, c):
                y = yt[:, c, :] if c < 2 else ps[:, c, :]
                if c >= 2:
                    dve.wait_ge(S["x_new"], (lay * 2 + b + 1) * DC + c - 1)
                stt(out=cv[:, c % 2, :], in0=y, scalar=pm[:, bass.ds(lay * PML + (gain + c), 1)], in1=rr[:, 0, :],
                    op0=ALU.mult, op1=ALU.mult).then_inc(S["t_ready"], 1)

            dve.wait_ge(S["x_first"], DC)
            dve.wait_ge(S["par_ok"], 3 * DEPTH)
            dve.wait_ge(S["const_ok"], 1)
            dve.wait_ge(S["const_in"], 16 * (6 + 4 * DEPTH + 2))
            dve.sem_inc(S["f_evac"], 2)

            with dve.Fori(0, DEPTH) as lay:
                V.restart()
                col = lay * PML

                def par(name, i=0, rows=slice(0, P)):
                    return pm[rows, bass.ds(col + (PM[name] + i), 1)]

                V.do(copy(fwl[0:HEMB, 0, 0:HHID], fw1[:, bass.ds(lay, 1), :].rearrange("k o n -> k (o n)")))
                V.join()
                copy(fwl[:, 1, 0:HHID], fw2[:, bass.ds(lay, 1), :].rearrange("k o n -> k (o n)")).then_inc(S["fw_ok"], 1)
                V.do(nc.vector.memset(kr[0:MN, :], 0.0))
                V.do(nc.vector.memset(vg[:, :, GD:2 * GD], 1.0))

                def sine_arg(k):
                    dve.wait_ge(S["f_mm"], lay * 2 + k + 1)
                    x, n = arg[:, 0, :], arg[:, 1, :]
                    V.do(ts(x, ps[0:HHID, 4, :], fbf[:, 2 * k, bass.ds(lay, 1)], fbf[:, 2 * k + 1, bass.ds(lay, 1)],
                            ALU.add, ALU.mult))
                    V.join()
                    V.do(ts(n, x, 1.0 / (2 * np.pi), MAGIC, ALU.mult, ALU.add))
                    V.join()
                    V.do(ts(n, n, -MAGIC, None, ALU.add))
                    V.join()
                    for part in PI2:
                        V.do(stt(out=x, in0=n, scalar=-part, in1=x, op0=ALU.mult, op1=ALU.add))
                        V.join()
                    ts(x, x, PI, -PI, ALU.min, ALU.max).then_inc(S["f_arg"], 1)

                def evac(t, dst, rows=P):
                    dve.wait_ge(S["pe_item"], lay * ITEMS + t + 3)
                    tt(dst, ps[0:rows, t % 2, :], rbc[0:rows, :], ALU.mult).then_inc(S["evac"], 1)

                def conv(i):
                    dve.wait_ge(S["conv1"], lay * 6 + i + 1)
                    u = uc[:, i, :]
                    V.do(stt(out=u, in0=pad[:, i % 2, 0:T], scalar=par("hy_w", i), in1=u, op0=ALU.mult, op1=ALU.add))
                    V.join()
                    stt(out=u, in0=pad[:, i % 2, 2:T + 2], scalar=par("hy_w", 12 + i), in1=u, op0=ALU.mult,
                        op1=ALU.add).then_inc(S["conv_done"], 1)

                def taps(j):
                    dve.wait_ge(S["fc_mm"], lay * 4 + j + 1)
                    b = 4 + 2 * (j % 2)
                    for d in range(2):
                        w = win[:, d, j, :].unsqueeze(1).to_broadcast([P, 2, HD])
                        V.do(tt(yt[:, d, :].rearrange("p (o n) -> p o n", o=2),
                                ps[:, b + d, :].rearrange("p (o n) -> p o n", o=2), w, ALU.mult))
                    V.join()
                    V.do(tt(hsum[:, j, :], yt[:, 0, :], yt[:, 1, :], ALU.add))
                    tt(hdif[:, j, :], yt[:, 0, :], yt[:, 1, :], ALU.subtract).then_inc(S["fc_done"], 1)
                    V.join()

                def spectrum(k):
                    dve.wait_ge(S["fd_copy"], lay * 4 + k + 1)
                    dve.wait_ge(S["fd_mm"], lay * 8 + 2 * k + 2)
                    ri, fc = divmod(k, 2)
                    o_ = ps[:, 5 + 2 * (k % 2), :].rearrange("p (o n) -> p o n", o=2)
                    e_ = yt[:, 0, :].rearrange("p (o n) -> p o n", o=2)
                    V.do(tt(KP[:, ri, :, fc * HD:(fc + 1) * HD], e_, o_, ALU.add))
                    tt(KM[:, ri, :, fc * HD:(fc + 1) * HD], e_, o_, ALU.subtract).then_inc(S["fd_done"], 1)

                def times(x, kk, o, dst):
                    kre = kk[:, 0:1, o, :].to_broadcast([P, 2, T])
                    kim = kk[:, 1:2, o, :].to_broadcast([P, 2, T])
                    V.do(tt(p1[:], x[:], kre, ALU.mult))
                    V.do(tt(p2[:], x[:], kim, ALU.mult))
                    V.join()
                    V.do(tt(dst[:, 0, :], p1[:, 0, :], p2[:, 1, :], ALU.subtract))
                    V.do(tt(dst[:, 1, :], p1[:, 1, :], p2[:, 0, :], ALU.add))
                    V.join()

                def h_first(o):
                    dve.wait_ge(S["he_copy"], lay * 2 + o + 1)
                    dve.wait_ge(S["ho_mm"], lay * 2 + o + 1)
                    V.do(tt(fa[:], ebuf[:], ps[:, 4:6, :], ALU.add))
                    V.do(tt(fb[:], ebuf[:], ps[:, 4:6, :], ALU.subtract))
                    V.join()
                    times(fa, KP, o, ya)

                def h_second(o):
                    times(fb, KM, o, ebuf)
                    V.do(tt(fa[:], ya[:], ebuf[:], ALU.add))
                    tt(fb[:], ya[:], ebuf[:], ALU.subtract).then_inc(S["h_prod"], 1)
                    V.join()

                def h_gate(o):
                    dve.wait_ge(S["hc_mm"], lay * 2 + o + 1)
                    for cc in range(2):
                        u = uc[:, cc, :].rearrange("p (n two) -> p two n", two=2)
                        y = ps[:, 6 + cc, :].rearrange("p (two n) -> p two n", two=2)
                        V.do(stt(out=u, in0=u, scalar=par("skip", 2 * o + cc), in1=y, op0=ALU.mult, op1=ALU.add))
                    V.join()
                    V.do(tt(uc[:, 0, :], uc[:, 0, :], uc[:, 2 + 2 * o, :], ALU.mult))
                    V.join()
                    tt(uc[:, 1, :], uc[:, 1, :], uc[:, 3 + 2 * o, :], ALU.mult).then_inc(S["h_done"], 1)
                    dve.wait_ge(S["h_done"], lay * 2 + o + 1)

                def norm(k, parts):
                    dve.wait_ge(S["nstd"], lay * 7 + k + 1)
                    for n, (x, g) in enumerate(parts):
                        ins = stt(out=x, in0=x, scalar=g, in1=rr[:, 0, :], op0=ALU.mult, op1=ALU.mult)
                        if n == len(parts) - 1:
                            ins.then_inc(S["nrm"], 1)
                        else:
                            V.do(ins)
                            V.join()
                    dve.wait_ge(S["nrm"], lay * 7 + k + 1)

                def rotate(k, x, rows, table, bank=3):
                    dve.wait_ge(S["nperm"], lay * 6 + k + 1)
                    V.do(tt(yt[rows, 0, :], x, rope[rows, table, :], ALU.mult))
                    V.do(tt(yt[rows, 1, :], ps[rows, bank, :], rope[rows, table + 1, :], ALU.mult))
                    V.join()
                    tt(x, yt[rows, 0, :], yt[rows, 1, :], ALU.add).then_inc(S["roped"], 1)

                everything = slice(0, P)
                for c in range(DC):
                    operand_lo(lay * 2, col + PM["mix_pre"], c)
                sine_arg(0)
                dve.wait_ge(S["rbc_ready"], lay * 2 + 1)
                for t in range(WIN + 2):
                    if t == 0:
                        evac(0, pad[:, 0, 1:T + 1])
                        sine_arg(1)
                    elif t < C_Q:
                        evac(t, pad[:, t % 2, 1:T + 1])
                    elif t < C_K:
                        evac(t, qf[:, t - C_Q, :])
                    elif t == C_K:
                        evac(t, cv[:, 0, :])
                    elif t == C_V:
                        evac(t, cv[:, 1, :])
                    elif t < C_MKV:
                        evac(t, cq[:, t - C_MQ, :])
                    elif t == C_MKV:
                        evac(t, ckv[:])
                    elif t == C_MKR:
                        V.join()
                        evac(t, kr[MN:MD, :], MR)
                    if 0 <= t - 1 < C_Q:
                        conv(t - 1)
                    if C_Q <= t - 1 < C_K:
                        norm(t - 1 - C_Q, [(qf[:, t - 1 - C_Q, :], par("gq"))])
                    if t - 1 == C_K:
                        norm(4, [(cv[:, 0, :], par("gk"))])
                    if C_Q <= t - 2 < C_K:
                        rotate(t - 2 - C_Q, qf[:, t - 2 - C_Q, :], everything, 0)
                    if t - 2 == C_K:
                        rotate(4, cv[:, 0, :], everything, 0)
                    if t == C_V + 2:
                        dve.wait_ge(S["vtr"], lay + 1)
                        v = ps[:, 3, :].rearrange("p (s n) -> p s n", s=TC)
                        V.do(copy(vg[:, :, 0:GD], v[:, :, 0:GD]))
                        copy(vg[:, :, 2 * GD:3 * GD], v[:, :, GD:2 * GD]).then_inc(S["vcopy"], 1)
                    if 1 <= t < 5:
                        taps(t - 1)
                    if t in (5, 6):
                        spectrum(2 * (t - 5))
                        spectrum(2 * (t - 5) + 1)
                    if t == 9:
                        h_first(0)
                    if t == 10:
                        h_second(0)
                    if t == 11:
                        h_gate(0)
                    if t == 13:
                        h_first(1)
                    if t == 14:
                        h_second(1)
                    if t == C_MQ + 2:
                        norm(5, [(cq[:, 0, :], par("mqa", 0)), (cq[:, 1, :], par("mqa", 1))])
                    if t == C_MKV + 1:
                        norm(6, [(ckv[:], par("mkva"))])
                        h_gate(1)
                    if t == WIN:
                        rotate(5, kr[MN:MD, :], slice(MN, MD), 2)
                for kv in range(GKV):
                    rows = slice(kv * GD, (kv + 1) * GD)
                    for half in range(2):
                        dve.wait_ge(S["khi"], lay * 4 + 2 * kv + 2)
                        tt(kb[half * GD:(half + 1) * GD, kv, :], cv[rows, 0, :], ka[rows, kv, :].bitcast(F32),
                           ALU.subtract).then_inc(S["klo"], 1)

                gsq_n = [0]

                def group(g):
                    src, _, n, c0 = GROUPS[g]
                    for c in range(n):
                        k = gsq_n[0]
                        gsq_n[0] += 1
                        dve.wait_ge(S["gsq"], lay * DC + k + 1)
                        if c == 0:
                            copy(acc[:], sq[:, k % 2, :]).then_inc(S["gsq_used"], 1)
                        else:
                            dve.wait_ge(S["gsq_used"], lay * DC + k)
                            tt(acc[:], acc[:], sq[:, k % 2, :], ALU.add).then_inc(S["gsq_used"], 1)
                    dve.wait_ge(S["gstd"], lay * 3 + g + 1)
                    for c in range(n):
                        stt(out=src[:, c, :], in0=src[:, c, :], scalar=par("g_out", c0 + c), in1=rr[:, 0, :], op0=ALU.mult,
                            op1=ALU.mult).then_inc(S["y_norm"], 1)

                group(0)

                for k, (dst, src, hi_) in enumerate(((cql, cq, cqh), (ckl, ckv, ckh), (uql, uqr, uqh), (ukl, ukr, ukh))):
                    dve.wait_ge(S["mhi"], lay * 4 + k + 1)
                    tt(dst[:], src[:], hi_[:].bitcast(F32), ALU.subtract).then_inc(S["mlo"], 1)
                V.do(nc.vector.memset(mv[:, :, :, MV:2 * MV], 1.0))

                def maxima(h):
                    scale = GD ** -0.5 if h < GH else MD ** -0.5
                    for qc in range(TC):
                        dve.wait_ge(S["s_tile"], (lay * HEADS + h) * 4 + qc + 1)
                        V.do(nc.vector.reduce_max(nm[:, h % 2, qc:qc + 1], ps[:, qc, :], AX.X))
                    V.join()
                    ts(ns[:, h % 2, :], nm[:, h % 2, :], -scale, None, ALU.mult).then_inc(S["nmax"], 1)

                def pt_copy(h, sc):
                    dve.wait_ge(S["pt_tile"], (lay * HEADS + h) * 4 + sc + 1)
                    if h >= 2 and sc == 1:
                        dve.wait_ge(S["pv"], lay * HEADS + h - 1)
                    copy(probT[h % 2][:, sc, :], ps[:, 5, :]).then_inc(S["pt_dve"], 1)

                def bank7(k):
                    kind, i = B7[k]
                    dve.wait_ge(S["b7_full"], lay * len(B7) + k + 1)
                    if kind == "q":
                        copy(mqf[0:MD, i, :], ps[0:MD, 7, :]).then_inc(S["b7_free"], 1)
                        dve.wait_ge(S["b7_free"], lay * len(B7) + k + 1)
                    elif kind == "perm":
                        V.do(tt(yt[0:MD, 0, :], mqf[0:MD, i, :], rope[0:MD, 2, :], ALU.mult))
                        V.do(tt(yt[0:MD, 1, :], ps[0:MD, 7, :], rope[0:MD, 3, :], ALU.mult))
                        V.join()
                        tt(mqf[0:MD, i, :], yt[0:MD, 0, :], yt[0:MD, 1, :], ALU.add).then_inc(S["b7_free"], 1)
                    elif kind == "k":
                        copy(mkf[0:MN, i, :], ps[0:MN, 7, :]).then_inc(S["b7_free"], 1)
                    else:
                        v = ps[:, 7, :].rearrange("p (a b n) -> p a b n", a=2, b=2)
                        V.do(copy(mv[:, i, :, 0:MV], v[:, :, 0, MN:MN + MV]))
                        copy(mv[:, i, :, 2 * MV:3 * MV], v[:, :, 1, MN:MN + MV]).then_inc(S["b7_free"], 1)

                def head_out(h):
                    swapped = (h // 4) % 2 if h < GH else h % 2
                    o_rows = slice(GD, 2 * GD) if swapped else slice(0, GD)
                    rows = slice((h % 2) * GD, (h % 2 + 1) * GD)
                    dst = qf[rows, h // 2, :] if h < GH else cq[rows, (h - GH) // 2, :]
                    if h < GH:
                        dve.wait_ge(S["q2lo"], lay * GH + h + 1)
                    dve.wait_ge(S["head_inv"], lay * HEADS + h + 1)
                    tt(dst, ps[o_rows, 6, :], rr[o_rows, h % 2, :], ALU.mult).then_inc(S["y_head"], 1)

                maxima(0)
                for h in range(HEADS):
                    if h + 1 < HEADS:
                        maxima(h + 1)
                    pt_copy(h, 1)
                    if h < GH:
                        bank7(2 * h)
                    if h:
                        head_out(h - 1)
                    pt_copy(h, 3)
                    if h < GH:
                        bank7(2 * h + 1)
                head_out(HEADS - 1)
                dve.wait_ge(S["y_head"], lay * HEADS + HEADS)
                group(1)
                group(2)
                for g, (src, _, n, c0) in enumerate(GROUPS):
                    for c in range(n):
                        dve.wait_ge(S["ygh"], lay * DC + c0 + c + 1)
                        tt(gl[:, c0 + c, :], src[:, c, :], gh[:, c0 + c, :].bitcast(F32), ALU.subtract).then_inc(S["ygl"], 1)

                for m in range(DC):
                    ysum(lay, 0, m)
                dve.wait_ge(S["rms_post"], lay * 2 + 1)
                for c in range(DC + 2):
                    if c < DC:
                        step(lay, 0, PM["mix_post"], c)
                    if c >= 2:
                        operand_lo(lay * 2 + 1, col + PM["ffn_pre"], c - 2)
                dve.wait_ge(S["rbc_ready"], lay * 2 + 2)

                V.join()
                mark(dve, "dve_marks")
                with dve.Fori(0, FC) as j:
                    V.restart()
                    r = lay * FC + j

                    def f_evac(k):
                        dve.wait_ge(S["pe_item"], lay * ITEMS + j * 2 + (I_UP + k + 3))
                        tt(pad[:, k, 1:T + 1], ps[:, 2 + k, :], rbc[:], ALU.mult).then_inc(S["f_evac"], 1)

                    def f_conv(k):
                        dve.wait_ge(S["f_conv1"], r * 2 + k + 1)
                        c = cv[:, k, :]
                        V.do(stt(out=c, in0=pad[:, k, 0:T], scalar=pm[:, bass.ds(col + j + (PM["ffn_w0"] + k * FC), 1)],
                                 in1=c, op0=ALU.mult, op1=ALU.add))
                        V.join()
                        stt(out=c, in0=pad[:, k, 2:T + 2], scalar=pm[:, bass.ds(col + j + (PM["ffn_w2"] + k * FC), 1)],
                            in1=c, op0=ALU.mult, op1=ALU.add).then_inc(S["f_conv"], 1)

                    f_evac(0)
                    f_conv(0)
                    f_evac(1)
                    f_conv(1)
                    dve.wait_ge(S["f_gelu"], r + 1)
                    dve.wait_ge(S["f_conv"], r * 2 + 2)
                    tt(fprod[:], gact[:], cv[:, 1, :], ALU.mult).then_inc(S["f_prod"], 1)
                    dve.wait_ge(S["f_hi"], r + 1)
                    tt(fl[:, bass.ds(j, 1), :], fprod[:].rearrange("p (o t) -> p o t", o=1),
                       fh[:, bass.ds(j, 1), :].bitcast(F32), ALU.subtract).then_inc(S["f_lo"], 1)
                    V.join()
                    mark(dve, "dve_marks")

                V.restart()
                for m in range(DC):
                    ysum(lay, 1, m)
                dve.wait_ge(S["rms_post"], lay * 2 + 2)
                for c in range(DC):
                    step(lay, 1, PM["ffn_post"], c)
                V.join()
                mark(dve, "dve_marks")


def constants():
    c = {}
    c["c_ident"] = np.eye(P, dtype=np.float32)
    c["c_b64"] = np.kron(np.eye(2), np.ones((GD, GD))).astype(np.float32)

    def swap(n, at, total):
        m = np.zeros((total, total), np.float32)
        for i in range(n):
            m[at + n + i, at + i] = -1.0
            m[at + i, at + n + i] = 1.0
        return m

    c["c_perm_g"] = swap(GD // 2, 0, P) + swap(GD // 2, GD, P)
    c["c_perm_m"] = swap(MR // 2, MN, MD)
    rows, cols = np.divmod(np.arange(T), GRID_W)

    def angles(rot):
        n = rot // 4
        inv = (np.float32(10000.0) ** (-np.arange(n, dtype=np.float32) / np.float32(n))).astype(np.float32)
        ang = np.concatenate([rows[:, None].astype(np.float32) * inv, cols[:, None].astype(np.float32) * inv], -1)
        return ang.astype(np.float64)

    rope = np.zeros((P, 4, T), np.float32)
    g, m = angles(GD), angles(MR)
    for i in range(4):
        rope[i * GD // 2:(i + 1) * GD // 2, 0] = np.cos(g).T
        rope[i * GD // 2:(i + 1) * GD // 2, 1] = np.sin(g).T
    rope[:MN, 2] = 1.0
    for i in range(2):
        at = MN + i * MR // 2
        rope[at:at + MR // 2, 2] = np.cos(m).T
        rope[at:at + MR // 2, 3] = np.sin(m).T
    c["c_rope"] = rope
    bands = (HEMB - 1) // 2
    t = np.linspace(0.0, 1.0, T, dtype=np.float32)[:, None]
    w = (np.float32(2.0 * np.pi) * np.arange(T, dtype=np.float32)[:, None] / np.float32(T)).astype(np.float32)
    f = np.linspace(1e-4, bands - 1, bands, dtype=np.float32)[None, :]
    fw = (f * w).astype(np.float32).astype(np.float64)
    c["c_z"] = np.ascontiguousarray(np.concatenate([t, np.cos(fw), -np.sin(fw)], -1).astype(np.float32).T)
    lo, hi = np.log(1e-2) / 1.5, np.log(1e-2) / 0.3
    deltas = np.linspace(lo, hi, HD, dtype=np.float32)
    window = np.exp((-t * np.abs(deltas)[None, :]).astype(np.float64)).astype(np.float32)
    late = np.concatenate([np.zeros((1, HD), np.float32), window[:-1]])
    tiles = lambda x: x.reshape(2, P, 2, HD).transpose(1, 2, 0, 3).reshape(P, 4, HD)
    c["c_win"] = np.ascontiguousarray(np.stack([tiles(window), tiles(late)], 1))
    theta = np.pi * (2 * np.arange(NF) + 1) / (2 * T)
    tf = np.zeros((P, 2, 2, T), np.float32)
    ti = np.zeros((P, 2, 4, NF), np.float32)
    for par in range(2):
        ang = np.outer(2 * np.arange(NF) + par, theta)
        fwd = np.concatenate([np.cos(ang), -np.sin(ang)], 1)
        for k in range(2):
            tf[:, par, k] = fwd[k * P:(k + 1) * P]
        inv = np.stack([np.cos(ang).T, -np.sin(ang).T]) / T
        ti[:, par] = inv.reshape(2, 2, P, NF).transpose(2, 0, 1, 3).reshape(P, 4, NF)
    c["c_tf"], c["c_ti"] = tf, ti
    return c


NAMES = ['x', 'mix_pre_norm', 'w_in', 'hy_conv_w', 'hy_conv_b', 'hy_filt_w1', 'hy_filt_b1', 'hy_filt_freq1',
         'hy_filt_w2', 'hy_filt_b2', 'hy_filt_freq2', 'hy_filt_w3', 'hy_skip', 'gqa_q_norm', 'gqa_k_norm',
         'mla_q_a_norm', 'mla_w_uq', 'mla_kv_a_norm', 'mla_w_ukv', 'hy_out_norm', 'gqa_out_norm', 'mla_out_norm',
         'w_out', 'mix_post_norm', 'ffn_pre_norm', 'w_up', 'ffn_conv_w', 'ffn_conv_b', 'w_down', 'ffn_post_norm']


def kernel(**inputs):
    import concourse.bacc as bacc
    from concourse.bass_utils import run_bass_kernel_spmd

    nc = bacc.Bacc("TRN2", target_bir_lowering=False, num_devices=1, dynamic_dma_scratch_size=1024)
    arrays = {n: np.ascontiguousarray(inputs[n]) for n in NAMES}
    arrays.update(constants())
    aps = {n: nc.dram_tensor(n, v.shape, F32, kind="ExternalInput").ap() for n, v in arrays.items()}
    out = nc.dram_tensor("out", (1, T, DM), F32, kind="ExternalOutput").ap()
    build(nc, aps, out)
    r = run_bass_kernel_spmd(nc, [arrays], core_ids=[0])
    return r.results[0]["out"]
```

```python
from contextlib import ExitStack

import concourse.bass as bass
import numpy as np
from concourse import mybir

F32 = mybir.dt.float32
F32R = mybir.dt.float32r
ACT = mybir.ActivationFunctionType
ALU = mybir.AluOpType
AX = mybir.AxisListType

P = 128
DM, T, DEPTH = 1024, 512, 2
DC = DM // P
TC = T // P
GRID_W = 64
EPS = 1e-6
HD, HEMB, HHID = 256, 33, 64
GH, GKV, GD = 8, 2, 64
MH, MQR, MKVR, MN, MR, MV = 4, 256, 128, 64, 32, 64
MD = MN + MR
DFF = 2816
FC = DFF // P
D_IN = 3 * HD + GH * GD + 2 * GKV * GD + MQR + MKVR + MR
NF = T // 2

WIN = -(-D_IN // P)
C_Q = 3 * HD // P
C_K = C_Q + GH * GD // P
C_V = C_K + 1
C_MQ = C_V + 1
C_MKV = C_MQ + MQR // P
C_MKR = C_MKV + 1
assert C_MKR == WIN - 1 and D_IN - C_MKR * P == MR

ITEM = 8
I_OUT = WIN
I_UP = I_OUT + DC
I_DOWN = I_UP + 2 * FC
DOWN_PARTS = [(k, min(ITEM, FC - k)) for k in range(0, FC, ITEM)]
ITEMS = I_DOWN + DC * len(DOWN_PARTS)
assert DEPTH == 2 and DEPTH * HHID == P
assert I_OUT % 2 == 0 and I_UP % 2 == 0 and I_DOWN % 2 == 0 and ITEMS % 2 == 0

PM = {}
_at = 0
for _name, _n in (("mix_pre", DC), ("hy_w", 18), ("hy_b", 6), ("skip", 4), ("mqa", 2), ("mkva", 1),
                  ("g_out", DC), ("mix_post", DC), ("ffn_pre", DC), ("ffn_post", DC), ("gq", 1), ("gk", 1)):
    PM[_name] = _at
    _at += _n
PM_A = _at
PM["ffn_w0"], PM["ffn_w1"], PM["ffn_w2"], PM["ffn_b"] = P, P + 2 * FC, 2 * P, 2 * P + 2 * FC
PM_ROWS = [PM_A, 4 * FC, 4 * FC]
PML = 3 * P

MAGIC = 1.5 * 2.0 ** 23
PI2 = (6.28125, 0.0019350051879882812, 3.019916e-07)
PI = 3.1415925


class Chain:

    def __init__(self, eng, sem):
        self.eng, self.sem, self.n = eng, sem, 0

    def do(self, ins):
        ins.then_inc(self.sem, 1)
        self.n += 1

    def join(self):
        self.eng.wait_ge(self.sem, self.n)

    def restart(self):
        self.eng.sem_clear(self.sem)
        self.n = 0


def build(nc, a, out):
    ctx = ExitStack()
    with ctx:
        def sb(name, shape, dt=F32, scope=ctx):
            return scope.enter_context(nc.sbuf_tensor(name, shape, dt))

        def sem(name):
            return ctx.enter_context(nc.semaphore(name))

        xT = sb("xT", [P, DC, T])
        raw = sb("raw", [P, 2, ITEM * P])
        wh = sb("wh", [P, 2, ITEM * P], F32R)
        wl = sb("wl", [P, 2, ITEM * P], F32R)
        ident = sb("ident", [P, P])
        ones = sb("ones", [P, P])
        b64 = sb("b64", [P, P])
        perm_g = sb("perm_g", [P, P])
        perm_m = sb("perm_m", [MD, MD])
        rope = sb("rope", [P, 4, T])
        rbc = sb("rbc", [P, T])
        std = sb("std", [P, T])
        rr = sb("rr", [P, 2, T])
        sq = sb("sq", [P, 2, T])
        acc = sb("acc", [P, T])
        yt = sb("yt", [P, 2, T])
        pad = sb("pad", [P, 2, T + 2])
        cv = sb("cv", [P, 2, T])
        pm = sb("pm", [P, DEPTH * PML])
        h2 = sb("h2", [P, T + 4])
        w3 = sb("w3", [P, DEPTH, 4 * HD])
        eps = sb("eps", [P, 1])
        nm = sb("nm", [P, 2, TC])
        ns = sb("ns", [P, 2, TC])

        with ExitStack() as s:
            gh = sb("gh", [P, DC, T], F32R, s)
            gl = sb("gl", [P, DC, T], F32R, s)
        prob = sb("prob", [P, 2, TC, T])
        probT0 = sb("probT0", [P, TC, T])
        mqf = sb("mqf", [P, MH, T])

        with ExitStack() as s:
            tb = sb("tb", [P, DC, T], F32, s)
            xout = sb("xout", [P, TC, DM], F32, s)
        with ExitStack() as s:
            fh = sb("fh", [P, FC, T], F32R, s)
            fl = sb("fl", [P, FC, T], F32R, s)
            gact = sb("gact", [P, T], F32, s)
            fprod = sb("fprod", [P, T], F32, s)
        with ExitStack() as s:
            xio = sb("xio", [P, TC, DM], F32, s)
            pstage = sb("pstage", [P, 3 * DEPTH, P], F32, s)
            zT = sb("zT", [HEMB, T], F32, s)
            fw1 = sb("fw1", [HEMB, DEPTH, HHID], F32, s)
            fw2 = sb("fw2", [P, P], F32, s)
            fst = sb("fst", [4, P], F32, s)
            fbf = sb("fbf", [P, 4], F32, s)
            h1 = sb("h1", [P, T], F32, s)
            arg = sb("arg", [P, 2, T], F32, s)
        uc = sb("uc", [P, 6, T])
        qf = sb("qf", [P, GH // 2, T])
        ka = sb("ka", [P, GKV, T], F32R)
        kb = sb("kb", [P, GKV, T], F32R)
        vg = sb("vg", [P, TC, 3 * GD])
        cq = sb("cq", [P, 2, T])
        ckv = sb("ckv", [P, T])
        kr = sb("kr", [P, T])
        with ExitStack() as s:
            TF = sb("TF", [P, 2, 2, T], F32, s)
            TI = sb("TI", [P, 2, 4, NF], F32, s)
            KP = sb("KP", [P, 2, 2, T], F32, s)
            KM = sb("KM", [P, 2, 2, T], F32, s)
            with ExitStack() as s2:
                win = sb("win", [P, 2, 4, HD], F32, s2)
                hsum = sb("hsum", [P, 4, T], F32, s2)
                hdif = sb("hdif", [P, 4, T], F32, s2)
            with ExitStack() as s2:
                ut = sb("ut", [P, 4, HD], F32, s2)
                ebuf = sb("ebuf", [P, 2, T], F32, s2)
                fa = sb("fa", [P, 2, T], F32, s2)
                fb = sb("fb", [P, 2, T], F32, s2)
                p1 = sb("p1", [P, 2, T], F32, s2)
                p2 = sb("p2", [P, 2, T], F32, s2)
                ya = sb("ya", [P, 2, T], F32, s2)
        with ExitStack() as s:
            with ExitStack() as s2:
                q2 = sb("q2", [P, 2, T], F32R, s2)
                ckh = sb("ckh", [P, T], F32R, s2)
                ckl = sb("ckl", [P, T], F32R, s2)
                cqh = sb("cqh", [P, 2, T], F32R, s2)
                cql = sb("cql", [P, 2, T], F32R, s2)
                uqr = sb("uqr", [P, 2, MH * MD], F32, s2)
                uqh = sb("uqh", [P, 2, MH * MD], F32R, s2)
                uql = sb("uql", [P, 2, MH * MD], F32R, s2)
                ukr = sb("ukr", [P, T], F32, s2)
                ukh = sb("ukh", [P, T], F32R, s2)
                ukl = sb("ukl", [P, T], F32R, s2)
            yh = sb("yh", [P, DC, T], F32R, s)
            yl = sb("yl", [P, DC, T], F32R, s)
            mkf = sb("mkf", [P, MH, T], F32, s)
            mv = sb("mv", [P, TC, 2, 3 * MV], F32, s)
            probT1 = sb("probT1", [P, TC, T], F32, s)
        probT = [probT0, probT1]
        groot = [rbc[:], cv[:, 1, :], rbc[:]]

        ps = ctx.enter_context(nc.psum_tensor("ps", [P, 8, T], F32))

        S = {}
        for name in (
                "ident_in", "fconst_in", "fw2_in", "const_in", "x_in0", "x_in1", "x_in2", "x_in3", "par_in", "w3_in",
                "filt_in", "tab_in", "mla_in", "raw0", "raw1", "out_sem",
                "raw_ok", "const_ok", "x_tr", "x_first", "fst_tr", "par_tr", "par_ok", "f_mm", "f_arg", "f_sin",
                "hi_ready", "lo_ready", "pe_item",
                "x_new", "gh_ready", "gl_ready", "xsq", "xsq_used", "rbc_ready",
                "ysq", "ysq_used", "ycopy", "stat_post", "rms_post", "t_ready",
                "evac", "conv1", "conv_done", "nsq", "nstat", "nstd", "nrm", "nperm", "roped", "vtr", "vcopy", "khi", "klo",
                "fc_mm", "fc_done", "fd_mm", "fd_copy", "fd_done",
                "ha_mm", "hu_copy", "he_mm", "ho_mm", "he_copy", "h_prod", "hc_mm", "h_done",
                "q2hi", "q2lo", "s_tile", "nmax", "p_ready", "pt_tile", "pt_act", "pt_dve", "pv", "head_inv", "y_head",
                "mhi", "mlo", "kr_copy", "b7_full", "b7_free",
                "gsq", "gsq_used", "gstat", "gstd", "y_norm", "ygh", "ygl",
                "f_evac", "f_conv1", "f_conv", "f_gelu", "f_prod", "f_hi", "f_lo",
                "o_tr", "o_copy", "dve_self", "act_self", "pe_marks", "dve_marks", "act_marks", "pool_marks"):
            S[name] = sem(name)
        dve_self = S["dve_self"]

        def mark(eng, name):
            eng.sem_inc(S[name], 1)

        block = ctx.enter_context(nc.Block())

        def one(w, lay):
            return w[bass.ds(lay, 1)]

        GROUPS = [(uc, 0, 2, 0), (qf, 0, 4, 2), (cq, 0, 2, 6)]
        B7 = []
        for hh in range(MH):
            B7 += [("q", hh), ("perm", hh), ("k", hh)]
        B7 += [("v", s) for s in range(TC)]
        assert len(B7) == 2 * GH
        HEADS = GH + MH

        @block.sync
        def _(sp):
            tok = a["x"].rearrange("b (c p) d -> p (b c) d", p=P)
            sp.dma_start(ident[:], a["c_ident"]).then_inc(S["ident_in"], 16)

            w_in = a["w_in"].rearrange("l (c p) n -> l p c n", p=P)
            w_out = a["w_out"].rearrange("l (c p) n -> l p c n", p=P)
            w_up = a["w_up"].rearrange("l (c p) n -> l p c n", p=P)
            w_down = a["w_down"].rearrange("l (c p) n -> l p c n", p=P)

            def item(lay, n, src, tiles=ITEM, cols=P):
                slot = item.slot
                item.slot = 1 - slot
                sp.wait_ge(S["lo_ready"], lay * ITEMS + n + 1)
                dst = raw[:, slot, :].rearrange("p (c n) -> p c n", n=P)[:, 0:tiles, 0:cols]
                sp.dma_start(dst, src.rearrange("o p c n -> (o p) c n")).then_inc(S[f"raw{slot}"], 16)

            item.slot = 0

            def x_quarter(i):
                cols = slice(i * DM // 4, (i + 1) * DM // 4)
                sp.dma_start(xio[:, :, cols], tok[:, :, cols]).then_inc(S[f"x_in{i}"], 16)

            x_quarter(0)
            sp.dma_start(zT[:], a["c_z"]).then_inc(S["fconst_in"], 16)
            sp.dma_start(fw1[:], a["hy_filt_w1"].rearrange("l k n -> k l n")).then_inc(S["fconst_in"], 16)
            for i, n in enumerate(("hy_filt_b1", "hy_filt_freq1", "hy_filt_b2", "hy_filt_freq2")):
                sp.dma_start(fst[i:i + 1, :], a[n].rearrange("(o l) n -> o (l n)", o=1)).then_inc(S["fconst_in"], 16)
            x_quarter(1)
            x_quarter(2)
            item(0, 0, w_in[0:1, :, :, 0:P])
            x_quarter(3)
            sp.wait_ge(S["const_ok"], 1)
            for l in range(DEPTH):
                at = slice(l * HHID, (l + 1) * HHID)
                sp.dma_start(fw2[at, at], a["hy_filt_w2"][l]).then_inc(S["fw2_in"], 16)
            stage = pstage[:].rearrange("p (l t) n -> p t l n", t=3)
            g0 = PM["g_out"]
            rows = [(PM["mix_pre"], 0, a["mix_pre_norm"]), (PM["hy_w"], 0, a["hy_conv_w"].rearrange("l k n -> l (k n)")),
                    (PM["hy_b"], 0, a["hy_conv_b"]), (PM["skip"], 0, a["hy_skip"].rearrange("l k n -> l (k n)")),
                    (PM["mqa"], 0, a["mla_q_a_norm"]), (PM["mkva"], 0, a["mla_kv_a_norm"]),
                    (g0, 0, a["hy_out_norm"]), (g0 + 2, 0, a["gqa_out_norm"]), (g0 + 6, 0, a["mla_out_norm"]),
                    (PM["mix_post"], 0, a["mix_post_norm"]), (PM["ffn_pre"], 0, a["ffn_pre_norm"]),
                    (PM["ffn_post"], 0, a["ffn_post_norm"]),
                    (0, 1, a["ffn_conv_w"][:, 0, :]), (2 * FC, 1, a["ffn_conv_w"][:, 1, :]),
                    (0, 2, a["ffn_conv_w"][:, 2, :]), (2 * FC, 2, a["ffn_conv_b"])]
            for row, tile, v in rows:
                sp.dma_start(stage[row:row + v.shape[1] // P, tile, :, :],
                             v.rearrange("l (k p) -> k l p", p=P)).then_inc(S["par_in"], 16)
            for n, m in (("gqa_q_norm", "gq"), ("gqa_k_norm", "gk")):
                for half in range(2):
                    sp.dma_start(stage[PM[m]:PM[m] + 1, 0, :, half * GD:(half + 1) * GD],
                                 a[n].rearrange("(o l) n -> o l n", o=1)).then_inc(S["par_in"], 16)

            item(0, 1, w_in[0:1, :, :, P:2 * P])
            for l in range(DEPTH):
                for lo in range(0, 4 * HD, T):
                    sp.dma_start(w3[l * HHID:(l + 1) * HHID, l, lo:lo + T], a["hy_filt_w3"][l][:, lo:lo + T]
                                 ).then_inc(S["w3_in"], 16)
            for dst, src in ((b64, "c_b64"), (perm_g, "c_perm_g"), (perm_m, "c_perm_m"), (rope, "c_rope")):
                sp.dma_start(dst[:], a[src]).then_inc(S["const_in"], 16)
            sp.wait_ge(S["par_ok"], 3 * DEPTH)
            sp.wait_ge(S["f_sin"], 2)
            with sp.Fori(0, DEPTH) as lay:
                sp.wait_ge(S["x_new"], lay * 2 * DC + DC)
                sp.dma_start(win[:], a["c_win"]).then_inc(S["filt_in"], 16)
                for i in range(2, 4):
                    item(lay, i, w_in[bass.ds(lay, 1), :, :, i * P:(i + 1) * P])
                sp.dma_start(TF[:], a["c_tf"]).then_inc(S["tab_in"], 16)
                sp.dma_start(TI[:], a["c_ti"]).then_inc(S["tab_in"], 16)
                with sp.Fori(4, WIN - 3, 2) as i:
                    for j in range(2):
                        item(lay, i + j, w_in[bass.ds(lay, 1), :, :, bass.ds((i + j) * P, P)])
                for i in range(WIN - 2, WIN):
                    w = min(P, D_IN - i * P)
                    item(lay, i, w_in[bass.ds(lay, 1), :, :, i * P:i * P + w], cols=w)
                sp.wait_ge(S["h_prod"], lay * 2 + 2)
                sp.dma_start(uqr[:], one(a["mla_w_uq"], lay).rearrange("o (c p) n -> (o p) c n", p=P)).then_inc(S["mla_in"], 16)
                sp.dma_start(ukr[:], one(a["mla_w_ukv"], lay).rearrange("o p n -> (o p) n")).then_inc(S["mla_in"], 16)
                for i in range(2):
                    item(lay, I_OUT + i, w_out[bass.ds(lay, 1), :, :, i * P:(i + 1) * P])
                with sp.Fori(2, DC - 1, 2) as i:
                    for j in range(2):
                        item(lay, I_OUT + i + j, w_out[bass.ds(lay, 1), :, :, bass.ds((i + j) * P, P)])
                with sp.Fori(0, FC) as j:
                    item(lay, I_UP + 2 * j, w_up[bass.ds(lay, 1), :, :, bass.ds(j * P, P)])
                    item(lay, I_UP + 2 * j + 1, w_up[bass.ds(lay, 1), :, :, bass.ds(DFF + j * P, P)])
                with sp.Fori(0, DC - 1, 2) as m:
                    for j in range(2):
                        for i, (k, n) in enumerate(DOWN_PARTS):
                            item(lay, I_DOWN + (m + j) * 3 + i,
                                 w_down[bass.ds(lay, 1), :, k:k + n, bass.ds((m + j) * P, P)], tiles=n)
                assert DEPTH == 2
                for i in range(2):
                    item(lay, ITEMS + i, w_in[DEPTH - 1:DEPTH, :, :, i * P:(i + 1) * P])
            res = out.rearrange("b (c p) d -> p (b c) d", p=P)
            for c in range(0, DC, 2):
                cols = slice(c * P, (c + 2) * P)
                sp.wait_ge(S["o_copy"], c + 2)
                sp.dma_start(res[:, :, cols], xout[:, :, cols]).then_inc(S["out_sem"], 16)
            sp.wait_ge(S["out_sem"], 16 * (DC // 2))

        @block.gpsimd
        def _(pool):
            nc.gpsimd.memset(raw[:], 0.0).then_inc(S["raw_ok"], 1)
            pool.wait_ge(S["raw_ok"], 1)
            pool.sem_inc(S["lo_ready"], 2)
            nc.gpsimd.memset(ones[:], 1.0)
            nc.gpsimd.memset(eps[:], EPS)
            nc.gpsimd.memset(h2[:], 0.0)
            nc.gpsimd.memset(fw2[:], 0.0)
            nc.gpsimd.memset(w3[:], 0.0)
            nc.gpsimd.memset(pad[:], 0.0).then_inc(S["const_ok"], 1)

            def lo(g, slot):
                pool.wait_ge(S["hi_ready"], g + 1)
                nc.gpsimd.tensor_tensor(wl[:, slot, :], raw[:, slot, :], wh[:, slot, :].bitcast(F32),
                                        ALU.subtract).then_inc(S["lo_ready"], 1)

            def add(lay, b):
                for c in range(DC):
                    pool.wait_ge(S["t_ready"], (lay * 2 + b) * DC + c + 1)
                    nc.gpsimd.tensor_tensor(xT[:, c, :], xT[:, c, :], tb[:, c, :], ALU.add).then_inc(S["x_new"], 1)

            lo(0, 0)
            lo(1, 1)
            pool.wait_ge(S["x_first"], DC)
            pool.sem_inc(S["x_new"], DC)
            with pool.Fori(0, DEPTH) as lay:
                with pool.Fori(2, I_OUT - 1, 2) as n:
                    for slot in range(2):
                        lo(lay * ITEMS + n + slot, slot)

                def q_lo(h):
                    half = h % 2
                    rows, other = slice(half * GD, (half + 1) * GD), slice((1 - half) * GD, (2 - half) * GD)
                    pool.wait_ge(S["q2hi"], lay * GH + h + 1)
                    nc.gpsimd.tensor_tensor(q2[other, half, :], qf[rows, h // 2, :], q2[rows, half, :].bitcast(F32),
                                            ALU.subtract).then_inc(S["q2lo"], 1)

                pool.wait_ge(S["lo_ready"], lay * ITEMS + I_OUT + 2)
                q_lo(0)
                pool.wait_ge(S["q2lo"], lay * GH + 1)
                q_lo(1)
                pool.wait_ge(S["q2lo"], lay * GH + 2)
                for slot in range(2):
                    lo(lay * ITEMS + (I_OUT + slot), slot)
                pool.wait_ge(S["lo_ready"], lay * ITEMS + I_OUT + 4)
                for h in range(2, GH):
                    q_lo(h)
                    pool.wait_ge(S["q2lo"], lay * GH + h + 1)
                mark(pool, "pool_marks")
                with pool.Fori(I_OUT + 2, I_UP + 1, 2) as n:
                    for slot in range(2):
                        lo(lay * ITEMS + n + slot, slot)
                add(lay, 0)
                with pool.Fori(I_UP + 2, ITEMS + 1, 2) as n:
                    for slot in range(2):
                        lo(lay * ITEMS + n + slot, slot)
                add(lay, 1)

        @block.scalar
        def _(act):
            A = nc.scalar.activation

            def hi(lay, n, slot):
                g = lay * ITEMS + n
                act.wait_ge(S[f"raw{slot}"], lay * (8 * ITEMS) + n * 8 + (16 - 8 * slot))
                act.wait_ge(S["pe_item"], g + 1)
                A(wh[:, slot, :], raw[:, slot, :], ACT.Copy).then_inc(S["hi_ready"], 1)

            C = Chain(act, S["act_self"])

            def inverse_root(dst, tmp, src, width, bias=True):
                if bias:
                    C.do(A(tmp, src, ACT.Ln, bias=eps[:, 0:1], scale=1.0 / width))
                else:
                    C.do(A(tmp, src, ACT.Ln))
                C.join()
                return A(dst, tmp, ACT.Exp, scale=-0.5 if bias else -1.0)

            def tables(name):
                nc.scalar.preload_act_table_set(name)

            def prep(q, off):
                for c in range(DC):
                    act.wait_ge(S["x_new"], q * DC + c + 1)
                    A(gh[:, c, :], xT[:, c, :], ACT.Copy, scale=pm[:, bass.ds(off + c, 1)]).then_inc(S["gh_ready"], 1)
                    if c >= 2:
                        act.wait_ge(S["xsq_used"], q * DC + c - 1)
                    A(sq[:, c % 2, :], xT[:, c, :], ACT.Square).then_inc(S["xsq"], 1)
                act.wait_ge(S["xsq_used"], q * DC + DC)
                inverse_root(rbc[:], std[:], ps[:, 1, :], DM).then_inc(S["rbc_ready"], 1)

            def ysquare(lay, b, m):
                if m >= 2:
                    act.wait_ge(S["ysq_used"], (lay * 2 + b) * (DC - 1) + m - 1)
                A(sq[:, m % 2, :], ps[:, m, :], ACT.Square).then_inc(S["ysq"], 1)
                if m < 2:
                    A(yt[:, m, :], ps[:, m, :], ACT.Copy).then_inc(S["ycopy"], 1)

            def post(lay, b):
                act.wait_ge(S["stat_post"], lay * 2 + b + 1)
                inverse_root(rr[:, 0, :], std[:], ps[:, 0, :], DM).then_inc(S["rms_post"], 1)

            def sines(k):
                act.wait_ge(S["f_arg"], k + 1)
                A(h1[:] if k == 0 else h2[:, 1:T + 1], arg[:, 0, :], ACT.Sin).then_inc(S["f_sin"], 1)

            for c in range(DC):
                act.wait_ge(S["x_tr"], c + 1)
                A(xT[:, c, :], ps[:, c % 4, :], ACT.Copy).then_inc(S["x_first"], 1)
                if c == 5:
                    sines(0)
            act.wait_ge(S["pe_item"], 2)
            hi(0, 0, 0)
            for i in range(3 * DEPTH):
                act.wait_ge(S["par_tr"], i + 1)
                n = PM_ROWS[i % 3]
                A(pm[:, i * P:i * P + n], ps[:, 4 + i % 2, 0:n], ACT.Copy).then_inc(S["par_ok"], 1)
            act.wait_ge(S["const_ok"], 1)
            sines(1)
            tables("natural_log_exp_and_others")
            act.wait_ge(S["x_first"], DC)
            act.wait_ge(S["par_ok"], 3 * DEPTH)
            act.wait_ge(S["const_ok"], 1)
            hi(0, 1, 1)

            with act.Fori(0, DEPTH) as lay:
                C.restart()
                col = lay * PML

                def par(name, i=0):
                    return pm[:, bass.ds(col + (PM[name] + i), 1)]

                def conv1(i):
                    act.wait_ge(S["evac"], lay * WIN + i + 1)
                    A(uc[:, i, :], pad[:, i % 2, 1:T + 1], ACT.Identity, scale=par("hy_w", 6 + i),
                      bias=par("hy_b", i)).then_inc(S["conv1"], 1)

                nsq_n = [0]

                def squares(i, src):
                    act.wait_ge(S["evac"], lay * WIN + i + 1)
                    k = nsq_n[0]
                    nsq_n[0] += 1
                    if k >= 2:
                        act.wait_ge(S["nstat"], lay * 7 + {2: 1, 3: 2, 4: 3, 5: 4, 6: 5, 7: 6}[k])
                    A(sq[:, k % 2, :], src, ACT.Square).then_inc(S["nsq"], 1)

                def root(k, width):
                    if k:
                        act.wait_ge(S["nrm"], lay * 7 + k)
                    act.wait_ge(S["nstat"], lay * 7 + k + 1)
                    inverse_root(rr[:, 0, :], std[:], ps[:, 2, :], width).then_inc(S["nstd"], 1)

                def khi():
                    act.wait_ge(S["roped"], lay * 6 + 5)
                    for kv in range(GKV):
                        rows = slice(kv * GD, (kv + 1) * GD)
                        for half in range(2):
                            A(ka[half * GD:(half + 1) * GD, kv, :], cv[rows, 0, :], ACT.Copy).then_inc(S["khi"], 1)

                def q_hi(h):
                    rows = slice((h % 2) * GD, (h % 2 + 1) * GD)
                    if h >= 2:
                        act.wait_ge(S["s_tile"], lay * 4 * HEADS + 4 * (h - 1))
                    A(q2[rows, h % 2, :], qf[rows, h // 2, :], ACT.Copy).then_inc(S["q2hi"], 1)

                def filt_copy(k):
                    act.wait_ge(S["fd_mm"], lay * 8 + 2 * k + 1)
                    if k:
                        act.wait_ge(S["fd_done"], lay * 4 + k)
                    A(yt[:, 0, :], ps[:, 4 + 2 * (k % 2), :], ACT.Copy).then_inc(S["fd_copy"], 1)

                def u_copy(o):
                    act.wait_ge(S["ha_mm"], lay * 2 + o + 1)
                    A(ut[:].rearrange("p (b c) d -> p b (c d)", b=2), ps[:, 4:6, :], ACT.Copy).then_inc(S["hu_copy"], 1)

                def e_copy(o):
                    act.wait_ge(S["he_mm"], lay * 2 + o + 1)
                    A(ebuf[:], ps[:, 6:8, :], ACT.Copy).then_inc(S["he_copy"], 1)

                prep(lay * 2, col + PM["mix_pre"])
                for t in range(WIN + 2):
                    if 2 <= t + 1 < I_OUT + 2:
                        hi(lay, t + 1, (t + 1) % 2)
                    i = t - 1
                    if 0 <= i < C_Q:
                        conv1(i)
                    if C_Q <= i < C_K:
                        squares(i, qf[:, i - C_Q, :])
                    if i == C_K:
                        squares(i, cv[:, 0, :])
                    if i in (C_MQ, C_MQ + 1):
                        squares(i, cq[:, i - C_MQ, :])
                    if i == C_MKV:
                        squares(i, ckv[:])
                    if C_Q <= t - 2 <= C_K:
                        root(t - 2 - C_Q, GD)
                    if t == C_MQ + 3:
                        root(5, MQR)
                    if t == C_MKV + 2:
                        root(6, MKVR)
                    if t in (3, 4):
                        filt_copy(2 * (t - 3))
                        filt_copy(2 * (t - 3) + 1)
                    if t == 5:
                        u_copy(0)
                    if t == 6:
                        e_copy(0)
                    if t == 9:
                        u_copy(1)
                    if t == 10:
                        e_copy(1)
                    if t == C_K + 3:
                        khi()
                    if t == C_K + 4:
                        act.wait_ge(S["h_prod"], lay * 2 + 2)
                        q_hi(0)
                        q_hi(1)
                        act.wait_ge(S["mla_in"], lay * 32 + 32)
                        for dst, src in ((uqh, uqr), (ukh, ukr)):
                            A(dst[:], src[:], ACT.Copy).then_inc(S["mhi"], 1)
                    if t == WIN:
                        act.wait_ge(S["h_done"], lay * 2 + 2)
                        act.wait_ge(S["nrm"], lay * 7 + 6)
                        A(cqh[:], cq[:], ACT.Copy).then_inc(S["mhi"], 1)
                    if t == WIN + 1:
                        act.wait_ge(S["nrm"], lay * 7 + 7)
                        A(ckh[:], ckv[:], ACT.Copy).then_inc(S["mhi"], 1)

                gsq_n = [0]

                def group_squares(g):
                    src, c0, n, _ = GROUPS[g]
                    for c in range(n):
                        k = gsq_n[0]
                        gsq_n[0] += 1
                        if k >= 2:
                            act.wait_ge(S["gsq_used"], lay * DC + k - 1)
                        A(sq[:, k % 2, :], src[:, c, :], ACT.Square).then_inc(S["gsq"], 1)

                def group_root(g):
                    act.wait_ge(S["gstat"], lay * 3 + g + 1)
                    act.wait_ge(S["head_inv"], lay * HEADS + (GH, GH + 1, HEADS)[g])
                    if g == 2:
                        act.wait_ge(S["y_norm"], lay * DC + GROUPS[1][3])
                    inverse_root(groot[g], std[:], ps[:, 7, :], GROUPS[g][2] * P).then_inc(S["gstd"], 1)
                    act.wait_ge(S["gstd"], lay * 3 + g + 1)

                def group_hi(g):
                    src, _, n, c0 = GROUPS[g]
                    for c in range(n):
                        act.wait_ge(S["y_norm"], lay * DC + c0 + c + 1)
                        A(yh[:, c0 + c, :], src[:, c, :], ACT.Copy).then_inc(S["ygh"], 1)

                def kr_copies():
                    act.wait_ge(S["roped"], lay * 6 + 6)
                    for hh in range(MH):
                        A(mkf[MN:MD, hh, :], kr[MN:MD, :], ACT.Copy).then_inc(S["kr_copy"], 1)

                def exps(h):
                    scale = GD ** -0.5 if h < GH else MD ** -0.5
                    act.wait_ge(S["nmax"], lay * HEADS + h + 1)
                    if h >= 2:
                        act.wait_ge(S["pt_tile"], lay * 4 * HEADS + 4 * (h - 1))
                    for qc in range(TC):
                        A(prob[:, h % 2, qc, :], ps[:, qc, :], ACT.Exp, bias=ns[:, h % 2, qc:qc + 1],
                          scale=scale).then_inc(S["p_ready"], 1)

                def pt_copy(h, sc):
                    act.wait_ge(S["pt_tile"], lay * 4 * HEADS + 4 * h + sc + 1)
                    if h >= 2 and sc == 0:
                        act.wait_ge(S["pv"], lay * HEADS + h - 1)
                    A(probT[h % 2][:, sc, :], ps[:, 4, :], ACT.Copy).then_inc(S["pt_act"], 1)

                def denominators(h):
                    act.wait_ge(S["pv"], lay * HEADS + h + 1)
                    swapped = (h // 4) % 2 if h < GH else h % 2
                    o_rows = slice(GD, 2 * GD) if swapped else slice(0, GD)
                    d_rows = slice(0, GD) if swapped else slice(GD, 2 * GD)
                    if h >= 2:
                        act.wait_ge(S["y_head"], lay * HEADS + h - 1)
                    inverse_root(rr[o_rows, h % 2, :], std[o_rows, :], ps[d_rows, 6, :], 1,
                                 bias=False).then_inc(S["head_inv"], 1)

                exps(0)
                for h in range(HEADS):
                    pt_copy(h, 0)
                    if h + 1 < HEADS:
                        exps(h + 1)
                    if h + 2 < GH:
                        q_hi(h + 2)
                    if h:
                        denominators(h - 1)
                    pt_copy(h, 2)
                    if h == 1:
                        kr_copies()
                    if h == GH - 1:
                        group_squares(0)
                    if h == GH:
                        group_root(0)
                        act.wait_ge(S["y_head"], lay * HEADS + GH)
                        group_squares(1)
                    if h == GH + 1:
                        group_root(1)
                    if h == GH + 2:
                        group_hi(0)
                    if h == GH + 3:
                        group_hi(1)
                denominators(HEADS - 1)
                act.wait_ge(S["y_head"], lay * HEADS + HEADS)
                group_squares(2)
                group_root(2)
                group_hi(2)

                for m in range(DC):
                    act.wait_ge(S["pe_item"], lay * ITEMS + I_OUT + m + 3)
                    hi(lay, I_OUT + m + 2, m % 2)
                    ysquare(lay, 0, m)
                post(lay, 0)
                prep(lay * 2 + 1, col + PM["ffn_pre"])

                tables("gelu_apprx_tanh_and_others")
                mark(act, "act_marks")
                with act.Fori(0, FC) as j:
                    r = lay * FC + j

                    def tap(k):
                        act.wait_ge(S["f_evac"], r * 2 + k + 3)
                        A(cv[:, k, :], pad[:, k, 1:T + 1], ACT.Identity,
                          scale=pm[:, bass.ds(col + j + (PM["ffn_w1"] + k * FC), 1)],
                          bias=pm[:, bass.ds(col + j + (PM["ffn_b"] + k * FC), 1)]).then_inc(S["f_conv1"], 1)

                    hi(lay, j * 2 + (I_UP + 2), 0)
                    tap(0)
                    act.wait_ge(S["f_conv"], r * 2 + 1)
                    A(gact[:], cv[:, 0, :], ACT.Gelu_apprx_tanh).then_inc(S["f_gelu"], 1)
                    hi(lay, j * 2 + (I_UP + 3), 1)
                    tap(1)
                    act.wait_ge(S["f_prod"], r + 1)
                    A(fh[:, bass.ds(j, 1), :], fprod[:].rearrange("p (o t) -> p o t", o=1), ACT.Copy).then_inc(S["f_hi"], 1)

                tables("natural_log_exp_and_others")
                for m in range(DC):
                    for i in range(len(DOWN_PARTS)):
                        n = I_DOWN + 3 * m + i
                        hi(lay, n + 2, n % 2)
                    act.wait_ge(S["pe_item"], lay * ITEMS + I_DOWN + 3 * m + 2 + 3)
                    ysquare(lay, 1, m)
                post(lay, 1)
                C.join()
                mark(act, "act_marks")

            for c in range(DC):
                act.wait_ge(S["o_tr"], c + 1)
                A(xout[:, :, c * P:(c + 1) * P], ps[:, 4 + c % 4, :].rearrange("p (t n) -> p t n", t=TC),
                  ACT.Copy).then_inc(S["o_copy"], 1)

        @block.tensor
        def _(pe):
            mm = nc.tensor.matmul

            def filt_layer(k):
                w, x = (fw1[:].rearrange("k l n -> k (l n)"), zT[:]) if k == 0 else (fw2[:], h1[:])
                mm(ps[:, 6, :], w, x, start=True, stop=True).then_inc(S["f_mm"], 1)

            pe.sem_inc(S["pe_item"], 2)
            pe.wait_ge(S["ident_in"], 16)
            for c in range(DC):
                if c % 2 == 0:
                    pe.wait_ge(S[f"x_in{c // 2}"], 16)
                if c >= 4:
                    pe.wait_ge(S["x_first"], c - 3)
                for t in range(TC):
                    ins = nc.tensor.transpose(ps[:, c % 4, t * P:(t + 1) * P], xio[:, t, c * P:(c + 1) * P], ident[:])
                ins.then_inc(S["x_tr"], 1)
                if c == 1:
                    pe.wait_ge(S["fconst_in"], 16 * 6)
                    nc.tensor.transpose(ps[:, 5, 0:4], fst[:], ident[0:4, 0:4]).then_inc(S["fst_tr"], 1)
                    filt_layer(0)
            pe.wait_ge(S["fw2_in"], 16 * DEPTH)
            pe.wait_ge(S["f_sin"], 1)
            filt_layer(1)
            pe.wait_ge(S["par_in"], 16 * 20)
            for i in range(3 * DEPTH):
                n = PM_ROWS[i % 3]
                if i >= 2:
                    pe.wait_ge(S["par_ok"], i - 1)
                nc.tensor.transpose(ps[:, 4 + i % 2, 0:n], pstage[0:n, i, :], ident[0:n, 0:n]).then_inc(S["par_tr"], 1)
            pe.wait_ge(S["f_sin"], 2)
            pe.wait_ge(S["const_ok"], 1)

            def square_sum(q, k):
                pe.wait_ge(S["xsq"], q * DC + k + 1)
                mm(ps[:, 1, :], ones[:], sq[:, k % 2, :], start=(k == 0), stop=(k == DC - 1)).then_inc(S["xsq_used"], 1)

            def stat_post(lay, b):
                pe.wait_ge(S["ysq_used"], (lay * 2 + b + 1) * (DC - 1))
                pe.wait_ge(S["ycopy"], (lay * 2 + b) * 2 + 2)
                mm(ps[:, 0, :], ones[:], acc[:], start=True, stop=False)
                pe.wait_ge(S["ysq"], (lay * 2 + b + 1) * DC)
                mm(ps[:, 0, :], ones[:], sq[:, (DC - 1) % 2, :], start=False, stop=True).then_inc(S["stat_post"], 1)

            def tiles(lay, n, slot, bank, tile_n, rh, rl, k0, start, stop, cols=P, gate=None, ks=None):
                g = lay * ITEMS + n
                pe.wait_ge(S["hi_ready"], g + 1)
                pe.wait_ge(S["lo_ready"], g + 3)
                for k in ks or range(tile_n):
                    if gate:
                        gate(k)
                    w_hi = wh[:, slot, k * P:k * P + cols]
                    w_lo = wl[:, slot, k * P:k * P + cols]
                    x_hi, x_lo = rh[:, k0 + k, :], rl[:, k0 + k, :]
                    mm(ps[0:cols, bank, :], w_hi, x_hi, start=start and k == 0, stop=False)
                    mm(ps[0:cols, bank, :], w_hi, x_lo, start=False, stop=False)
                    ins = mm(ps[0:cols, bank, :], w_lo, x_hi, start=False, stop=stop and k == tile_n - 1)
                if ks is None or ks[-1] == tile_n - 1:
                    ins.then_inc(S["pe_item"], 1)

            with pe.Fori(0, DEPTH) as lay:
                def item(t):
                    if t >= 2:
                        pe.wait_ge(S["evac"], lay * WIN + t - 1)
                    cols = min(P, D_IN - t * P)

                    def gate(k):
                        if t == 0:
                            square_sum(lay * 2, k)
                            pe.wait_ge(S["gh_ready"], lay * 2 * DC + k + 1)
                            pe.wait_ge(S["gl_ready"], lay * 2 * DC + k + 1)
                    if t == 1:
                        pe.wait_ge(S["rbc_ready"], lay * 2 + 1)
                    tiles(lay, t, t % 2, t % 2, DC, gh, gl, 0, True, True, cols, gate)

                def filt_taps(j):
                    par_, c = divmod(j, 2)
                    if j == 0:
                        pe.wait_ge(S["filt_in"], lay * 16 + 16)
                        pe.wait_ge(S["w3_in"], 16 * 2 * DEPTH)
                    if j >= 2:
                        pe.wait_ge(S["fc_done"], lay * 4 + j - 1)
                    b = 4 + 2 * (j % 2)
                    w = w3[:, bass.ds(lay, 1), :].rearrange("k l (o d n) -> k d (l o) n", o=2, d=2)
                    t0 = 2 * P * c + par_
                    for d in range(2):
                        lo = t0 + 1 - d
                        ins = mm(ps[:, b + d, :].rearrange("p (o n) -> p o n", o=2), h2[:, lo:lo + 2 * P - 1:2], w[:, d, :, :],
                                 start=True, stop=True)
                    ins.then_inc(S["fc_mm"], 1)

                def filt_spec(k):
                    b = 4 + 2 * (k % 2)
                    if k == 0:
                        pe.wait_ge(S["tab_in"], lay * 32 + 32)
                        pe.wait_ge(S["fc_done"], lay * 4 + 4)
                    if k >= 2:
                        pe.wait_ge(S["fd_done"], lay * 4 + k - 1)
                    src = hsum if k < 2 else hdif
                    for par_ in range(2):
                        for c in range(2):
                            ins = mm(ps[:, b + par_, :], TF[:, par_, c, k * P:(k + 1) * P], src[:, 2 * par_ + c, :],
                                     start=(c == 0), stop=(c == 1))
                        ins.then_inc(S["fd_mm"], 1)

                def h_turn(o):
                    if o == 0:
                        pe.wait_ge(S["fd_done"], lay * 4 + 4)
                        pe.wait_ge(S["conv_done"], lay * 6 + 2)
                    else:
                        pe.wait_ge(S["h_done"], lay * 2 + 1)
                    for j in range(4):
                        par_, c = divmod(j, 2)
                        for cc in range(2):
                            t0 = 2 * P * c + par_
                            at = (j % 2) * HD + cc * P
                            ins = nc.tensor.transpose(ps[:, 4 + j // 2, at:at + P], uc[:, cc, t0:t0 + 2 * P - 1:2], ident[:])
                    ins.then_inc(S["ha_mm"], 1)

                def h_forward(o):
                    pe.wait_ge(S["hu_copy"], lay * 2 + o + 1)
                    for par_ in range(2):
                        for k in range(4):
                            b = (6 if par_ == 0 else 4) + k // 2
                            for c in range(2):
                                ins = mm(ps[:, b, (k % 2) * HD:(k % 2 + 1) * HD], TF[:, par_, c, k * P:(k + 1) * P],
                                         ut[:, 2 * par_ + c, :], start=(c == 0), stop=(c == 1))
                        ins.then_inc(S["he_mm" if par_ == 0 else "ho_mm"], 1)

                def h_inverse(o):
                    pe.wait_ge(S["h_prod"], lay * 2 + o + 1)
                    for cc in range(2):
                        for par_ in range(2):
                            spec = fa if par_ == 0 else fb
                            for k in range(4):
                                ri, fc = divmod(k, 2)
                                lo = fc * HD + cc * P
                                ins = mm(ps[:, 6 + cc, par_ * NF:(par_ + 1) * NF], spec[:, ri, lo:lo + P],
                                         TI[:, par_, k, :], start=(k == 0), stop=(k == 3))
                    ins.then_inc(S["hc_mm"], 1)

                def stat(k, chunks, weights, first_sq):
                    pe.wait_ge(S["nsq"], lay * 8 + first_sq + len(chunks))
                    pe.wait_ge(S["const_in"], 16 * 4)
                    if k:
                        pe.wait_ge(S["nstd"], lay * 7 + k)
                    for n, s_ in enumerate(chunks):
                        ins = mm(ps[:, 2, :], weights[:], sq[:, s_, :], start=(n == 0), stop=(n == len(chunks) - 1))
                    ins.then_inc(S["nstat"], 1)

                def permute(k, src):
                    pe.wait_ge(S["nrm"], lay * 7 + k + 1)
                    if k:
                        pe.wait_ge(S["roped"], lay * 6 + k)
                    mm(ps[:, 3, :], perm_g[:], src, start=True, stop=True).then_inc(S["nperm"], 1)

                item(0)
                for t in range(1, WIN + 2):
                    if t in (1, 2):
                        filt_taps(2 * (t - 1))
                        filt_taps(2 * (t - 1) + 1)
                    if t in (3, 4):
                        filt_spec(2 * (t - 3))
                        filt_spec(2 * (t - 3) + 1)
                    if t == 5:
                        h_turn(0)
                    if t == 6:
                        h_forward(0)
                    if t == 8:
                        h_inverse(0)
                    if t == 9:
                        h_turn(1)
                    if t == 10:
                        h_forward(1)
                    if t == 14:
                        h_inverse(1)
                    if t < WIN:
                        item(t)
                    if C_Q <= t - 1 <= C_K:
                        stat(t - 1 - C_Q, [(t - 1 - C_Q) % 2], b64, t - 1 - C_Q)
                    if C_Q <= t - 2 < C_K:
                        permute(t - 2 - C_Q, qf[:, t - 2 - C_Q, :])
                    if t - 2 == C_K:
                        permute(4, cv[:, 0, :])
                    if t == C_V + 2:
                        pe.wait_ge(S["evac"], lay * WIN + C_V + 1)
                        pe.wait_ge(S["roped"], lay * 6 + 5)
                        for s_ in range(TC):
                            ins = nc.tensor.transpose(ps[:, 3, s_ * P:(s_ + 1) * P], cv[:, 1, s_ * P:(s_ + 1) * P], ident[:])
                        ins.then_inc(S["vtr"], 1)
                    if t == C_MQ + 2:
                        stat(5, [1, 0], ones, 5)
                    if t == C_MKV + 1:
                        stat(6, [1], ones, 7)
                    if t == WIN:
                        pe.wait_ge(S["evac"], lay * WIN + WIN)
                        pe.wait_ge(S["vcopy"], lay + 1)
                        pe.wait_ge(S["h_done"], lay * 2 + 2)
                        mm(ps[0:MD, 7, :], perm_m[:], kr[0:MD, :], start=True, stop=True).then_inc(S["nperm"], 1)

                def group(g):
                    n = GROUPS[g][2]
                    if g:
                        pe.wait_ge(S["gstd"], lay * 3 + g)
                    else:
                        pe.wait_ge(S["b7_free"], lay * len(B7) + len(B7))
                    pe.wait_ge(S["gsq_used"], lay * DC + GROUPS[g][3] + n)
                    mm(ps[:, 7, :], ones[:], acc[:], start=True, stop=True).then_inc(S["gstat"], 1)

                def scores(h):
                    for qc in range(TC):
                        cols = slice(qc * P, (qc + 1) * P)
                        if h == 0:
                            if qc == 0:
                                pe.wait_ge(S["evac"], lay * WIN + WIN)
                            if qc == 2:
                                pe.wait_ge(S["nstd"], lay * 7 + 7)
                            if qc == 3:
                                pe.wait_ge(S["vcopy"], lay + 1)
                        else:
                            pe.wait_ge(S["p_ready"], (lay * HEADS + h - 1) * 4 + qc + 1)
                        if h < GH:
                            if qc == 0:
                                pe.wait_ge(S["q2hi"], lay * GH + h + 1)
                                pe.wait_ge(S["q2lo"], lay * GH + h + 1)
                                if h == 0:
                                    pe.wait_ge(S["khi"], lay * 4 + 4)
                                    pe.wait_ge(S["klo"], lay * 4 + 4)
                            mm(ps[:, qc, :], q2[:, h % 2, cols], ka[:, h // 4, :], start=True, stop=False)
                            mm(ps[:, qc, :], q2[:, h % 2, cols], kb[:, h // 4, :], start=False, stop=True) \
                                .then_inc(S["s_tile"], 1)
                        else:
                            if h == GH and qc == 0:
                                pe.wait_ge(S["b7_free"], lay * len(B7) + 3 * MH)
                                pe.wait_ge(S["kr_copy"], lay * MH + MH)
                            mm(ps[:, qc, :], mqf[0:MD, h - GH, cols], mkf[0:MD, h - GH, :], start=True, stop=True) \
                                .then_inc(S["s_tile"], 1)

                def bank7(k):
                    kind, i = B7[k]
                    if k:
                        pe.wait_ge(S["b7_free"], lay * len(B7) + k)
                    else:
                        pe.wait_ge(S["roped"], lay * 6 + 6)
                        pe.wait_ge(S["mhi"], lay * 4 + 4)
                        pe.wait_ge(S["mlo"], lay * 4 + 4)
                    if kind == "q":
                        n, last = 0, 5
                        for c in range(2):
                            for w, x in ((uqh, cqh), (uqh, cql), (uql, cqh)):
                                ins = mm(ps[0:MD, 7, :], w[:, c, i * MD:(i + 1) * MD], x[:, c, :], start=(n == 0), stop=(n == last))
                                n += 1
                    elif kind == "perm":
                        ins = mm(ps[0:MD, 7, :], perm_m[:], mqf[0:MD, i, :], start=True, stop=True)
                    elif kind == "k":
                        for n, (w, x) in enumerate(((ukh, ckh), (ukh, ckl), (ukl, ckh))):
                            ins = mm(ps[0:MN, 7, :], w[:, i * P:i * P + MN], x[:], start=(n == 0), stop=(n == 2))
                    else:
                        cols = slice(i * P, (i + 1) * P)
                        for n, (w, x) in enumerate(((ckh, ukh), (ckh, ukl), (ckl, ukh))):
                            ins = mm(ps[:, 7, :], w[:, cols], x[:], start=(n == 0), stop=(n == 2))
                    ins.then_inc(S["b7_full"], 1)

                def turn(h, tiles_):
                    pe.wait_ge(S["p_ready"], (lay * HEADS + h) * 4 + 4)
                    for sc in tiles_:
                        if sc >= 2 or h:
                            k = (lay * HEADS + h) * 2 + sc // 2
                            pe.wait_ge(S["pt_act" if sc % 2 == 0 else "pt_dve"], k)
                        for qc in range(TC):
                            ins = nc.tensor.transpose(ps[:, 4 + sc % 2, qc * P:(qc + 1) * P],
                                                      prob[:, h % 2, qc, sc * P:(sc + 1) * P], ident[:])
                        ins.then_inc(S["pt_tile"], 1)

                def values(h):
                    if h:
                        pe.wait_ge(S["y_head"], lay * HEADS + h)
                    if h == 0:
                        pe.wait_ge(S["vcopy"], lay + 1)
                    if h == GH:
                        pe.wait_ge(S["b7_free"], lay * len(B7) + len(B7))
                    pe.wait_ge(S["pt_act"], (lay * HEADS + h) * 2 + 2)
                    pe.wait_ge(S["pt_dve"], (lay * HEADS + h) * 2 + 2)
                    for sc in range(TC):
                        if h < GH:
                            v = vg[:, sc, (h // 4) * GD:(h // 4) * GD + P]
                        else:
                            i = h - GH
                            v = mv[:, sc, i // 2, (i % 2) * MV:(i % 2) * MV + P]
                        ins = mm(ps[:, 6, :], v, probT[h % 2][:, sc, :], start=(sc == 0), stop=(sc == TC - 1))
                    ins.then_inc(S["pv"], 1)

                scores(0)
                for h in range(HEADS):
                    if h + 1 < HEADS:
                        scores(h + 1)
                    if h < GH:
                        bank7(2 * h)
                    turn(h, (0, 1))
                    if h:
                        values(h - 1)
                    turn(h, (2, 3))
                    if h < GH:
                        bank7(2 * h + 1)
                    if h in (GH, GH + 1):
                        group(h - GH)
                values(HEADS - 1)

                def gate_out(k):
                    pe.wait_ge(S["ygh"], lay * DC + k + 1)
                    pe.wait_ge(S["ygl"], lay * DC + k + 1)

                pe.wait_ge(S["p_ready"], (lay * HEADS + HEADS) * 4)
                ready = GROUPS[2][3]
                for m in range(2):
                    tiles(lay, I_OUT + m, m, m, DC, yh, yl, 0, True, True, gate=gate_out, ks=range(ready))
                    if m == 0:
                        group(2)
                for m in range(2):
                    tiles(lay, I_OUT + m, m, m, DC, yh, yl, 0, True, True, gate=gate_out, ks=range(ready, DC))
                pe.wait_ge(S["y_head"], lay * HEADS + HEADS)
                pe.wait_ge(S["gstd"], lay * 3 + 3)
                for m in range(2, DC):
                    tiles(lay, I_OUT + m, m % 2, m, DC, yh, yl, 0, True, True)
                stat_post(lay, 0)

                def gate_up(k):
                    if k == 0:
                        pe.wait_ge(S["t_ready"], lay * 2 * DC + 3)
                    square_sum(lay * 2 + 1, k)
                    pe.wait_ge(S["gh_ready"], (lay * 2 + 1) * DC + k + 1)
                    pe.wait_ge(S["gl_ready"], (lay * 2 + 1) * DC + k + 1)

                def up(j, gate=None):
                    for k in range(2):
                        pe.wait_ge(S["f_evac"], (lay * FC + j) * 2 + k + 1)
                        tiles(lay, j * 2 + (I_UP + k), k, 2 + k, DC, gh, gl, 0, True, True,
                              gate=gate if k == 0 else None)

                up(0, gate_up)
                mark(pe, "pe_marks")
                with pe.Fori(1, FC) as j:
                    up(j)

                pe.wait_ge(S["rbc_ready"], lay * 2 + 2)
                for m in range(DC):
                    if m == 2:
                        pe.wait_ge(S["f_evac"], lay * 2 * FC + 2 * FC + 2)
                    for i, (k0, n) in enumerate(DOWN_PARTS):
                        last = i == len(DOWN_PARTS) - 1

                        def gate_down(k, k0=k0):
                            if m == 0:
                                pe.wait_ge(S["f_hi"], lay * FC + k0 + k + 1)
                                pe.wait_ge(S["f_lo"], lay * FC + k0 + k + 1)

                        tiles(lay, I_DOWN + 3 * m + i, (3 * m + i) % 2, m, n, fh, fl, k0, i == 0, last, gate=gate_down)
                stat_post(lay, 1)

            for c in range(DC):
                pe.wait_ge(S["x_new"], 2 * DEPTH * DC + c + 1)
                if c >= 4:
                    pe.wait_ge(S["o_copy"], c - 3)
                else:
                    pe.wait_ge(S["t_ready"], 2 * DEPTH * DC)
                for t in range(TC):
                    ins = nc.tensor.transpose(ps[:, 4 + c % 4, t * P:(t + 1) * P], xT[:, c, t * P:(t + 1) * P], ident[:])
                ins.then_inc(S["o_tr"], 1)

        @block.vector
        def _(dve):
            V = Chain(dve, dve_self)
            tt, ts, stt = nc.vector.tensor_tensor, nc.vector.tensor_scalar, nc.vector.scalar_tensor_tensor
            copy = nc.vector.tensor_copy

            def operand_lo(q, off, c):
                dve.wait_ge(S["gh_ready"], q * DC + c + 1)
                stt(out=gl[:, c, :], in0=xT[:, c, :], scalar=pm[:, bass.ds(off + c, 1)], in1=gh[:, c, :].bitcast(F32),
                    op0=ALU.mult, op1=ALU.subtract).then_inc(S["gl_ready"], 1)

            def ysum(lay, b, m):
                dve.wait_ge(S["ysq"], (lay * 2 + b) * DC + m + 1)
                if m == 0:
                    copy(acc[:], sq[:, 0, :]).then_inc(S["ysq_used"], 1)
                else:
                    dve.wait_ge(S["ysq_used"], (lay * 2 + b) * (DC - 1) + m)
                    tt(acc[:], acc[:], sq[:, m % 2, :], ALU.add).then_inc(S["ysq_used"], 1)

            def step(lay, b, gain, c):
                y = yt[:, c, :] if c < 2 else ps[:, c, :]
                stt(out=tb[:, c, :], in0=y, scalar=pm[:, bass.ds(lay * PML + (gain + c), 1)], in1=rr[:, 0, :],
                    op0=ALU.mult, op1=ALU.mult).then_inc(S["t_ready"], 1)

            def sine_arg(k):
                dve.wait_ge(S["f_mm"], k + 1)
                x, n = arg[:, 0, :], arg[:, 1, :]
                V.do(ts(x, ps[:, 6, :], fbf[:, 2 * k:2 * k + 1], fbf[:, 2 * k + 1:2 * k + 2], ALU.add, ALU.mult))
                V.join()
                V.do(ts(n, x, 1.0 / (2 * np.pi), MAGIC, ALU.mult, ALU.add))
                V.join()
                V.do(ts(n, n, -MAGIC, None, ALU.add))
                V.join()
                for part in PI2:
                    V.do(stt(out=x, in0=n, scalar=-part, in1=x, op0=ALU.mult, op1=ALU.add))
                    V.join()
                ts(x, x, PI, -PI, ALU.min, ALU.max).then_inc(S["f_arg"], 1)

            dve.wait_ge(S["fst_tr"], 1)
            V.do(copy(fbf[:], ps[:, 5, 0:4]))
            V.join()
            for k in range(2):
                sine_arg(k)
            dve.wait_ge(S["x_first"], DC)
            dve.wait_ge(S["par_ok"], 3 * DEPTH)
            dve.wait_ge(S["const_ok"], 1)
            dve.wait_ge(S["f_sin"], 2)
            dve.sem_inc(S["f_evac"], 2)

            with dve.Fori(0, DEPTH) as lay:
                V.restart()
                col = lay * PML

                def par(name, i=0, rows=slice(0, P)):
                    return pm[rows, bass.ds(col + (PM[name] + i), 1)]

                def evac(t, dst, rows=P):
                    dve.wait_ge(S["pe_item"], lay * ITEMS + t + 3)
                    if 2 <= t < C_Q:
                        dve.wait_ge(S["conv_done"], lay * 6 + t - 1)
                    tt(dst, ps[0:rows, t % 2, :], rbc[0:rows, :], ALU.mult).then_inc(S["evac"], 1)

                def conv(i):
                    dve.wait_ge(S["conv1"], lay * 6 + i + 1)
                    u = uc[:, i, :]
                    V.do(stt(out=u, in0=pad[:, i % 2, 0:T], scalar=par("hy_w", i), in1=u, op0=ALU.mult, op1=ALU.add))
                    V.join()
                    stt(out=u, in0=pad[:, i % 2, 2:T + 2], scalar=par("hy_w", 12 + i), in1=u, op0=ALU.mult,
                        op1=ALU.add).then_inc(S["conv_done"], 1)

                def taps(j):
                    dve.wait_ge(S["fc_mm"], lay * 4 + j + 1)
                    if j:
                        dve.wait_ge(S["fc_done"], lay * 4 + j)
                    b = 4 + 2 * (j % 2)
                    for d in range(2):
                        w = win[:, d, j, :].unsqueeze(1).to_broadcast([P, 2, HD])
                        V.do(tt(yt[:, d, :].rearrange("p (o n) -> p o n", o=2),
                                ps[:, b + d, :].rearrange("p (o n) -> p o n", o=2), w, ALU.mult))
                    V.join()
                    V.do(tt(hsum[:, j, :], yt[:, 0, :], yt[:, 1, :], ALU.add))
                    tt(hdif[:, j, :], yt[:, 0, :], yt[:, 1, :], ALU.subtract).then_inc(S["fc_done"], 1)
                    V.join()

                def spectrum(k):
                    dve.wait_ge(S["fd_copy"], lay * 4 + k + 1)
                    dve.wait_ge(S["fd_mm"], lay * 8 + 2 * k + 2)
                    ri, fc = divmod(k, 2)
                    o_ = ps[:, 5 + 2 * (k % 2), :].rearrange("p (o n) -> p o n", o=2)
                    e_ = yt[:, 0, :].rearrange("p (o n) -> p o n", o=2)
                    V.do(tt(KP[:, ri, :, fc * HD:(fc + 1) * HD], e_, o_, ALU.add))
                    tt(KM[:, ri, :, fc * HD:(fc + 1) * HD], e_, o_, ALU.subtract).then_inc(S["fd_done"], 1)

                def times(x, kk, o, dst):
                    kre = kk[:, 0:1, o, :].to_broadcast([P, 2, T])
                    kim = kk[:, 1:2, o, :].to_broadcast([P, 2, T])
                    V.do(tt(p1[:], x[:], kre, ALU.mult))
                    V.do(tt(p2[:], x[:], kim, ALU.mult))
                    V.join()
                    V.do(tt(dst[:, 0, :], p1[:, 0, :], p2[:, 1, :], ALU.subtract))
                    V.do(tt(dst[:, 1, :], p1[:, 1, :], p2[:, 0, :], ALU.add))
                    V.join()

                def h_first(o):
                    dve.wait_ge(S["he_copy"], lay * 2 + o + 1)
                    dve.wait_ge(S["ho_mm"], lay * 2 + o + 1)
                    V.do(tt(fa[:], ebuf[:], ps[:, 4:6, :], ALU.add))
                    V.do(tt(fb[:], ebuf[:], ps[:, 4:6, :], ALU.subtract))
                    V.join()
                    times(fa, KP, o, ya)

                def h_second(o):
                    times(fb, KM, o, ebuf)
                    V.do(tt(fa[:], ya[:], ebuf[:], ALU.add))
                    tt(fb[:], ya[:], ebuf[:], ALU.subtract).then_inc(S["h_prod"], 1)
                    V.join()

                def h_gate(o):
                    dve.wait_ge(S["hc_mm"], lay * 2 + o + 1)
                    dve.wait_ge(S["conv_done"], lay * 6 + 4 + 2 * o)
                    for cc in range(2):
                        u = uc[:, cc, :].rearrange("p (n two) -> p two n", two=2)
                        y = ps[:, 6 + cc, :].rearrange("p (two n) -> p two n", two=2)
                        V.do(stt(out=u, in0=u, scalar=par("skip", 2 * o + cc), in1=y, op0=ALU.mult, op1=ALU.add))
                    V.join()
                    V.do(tt(uc[:, 0, :], uc[:, 0, :], uc[:, 2 + 2 * o, :], ALU.mult))
                    V.join()
                    tt(uc[:, 1, :], uc[:, 1, :], uc[:, 3 + 2 * o, :], ALU.mult).then_inc(S["h_done"], 1)
                    dve.wait_ge(S["h_done"], lay * 2 + o + 1)

                def norm(k, parts):
                    dve.wait_ge(S["nstd"], lay * 7 + k + 1)
                    for n, (x, g) in enumerate(parts):
                        ins = stt(out=x, in0=x, scalar=g, in1=rr[:, 0, :], op0=ALU.mult, op1=ALU.mult)
                        if n == len(parts) - 1:
                            ins.then_inc(S["nrm"], 1)
                        else:
                            V.do(ins)
                            V.join()
                    dve.wait_ge(S["nrm"], lay * 7 + k + 1)

                def rotate(k, x, rows, table, bank=3):
                    dve.wait_ge(S["nperm"], lay * 6 + k + 1)
                    dve.wait_ge(S["const_in"], 16 * 4)
                    V.do(tt(yt[rows, 0, :], x, rope[rows, table, :], ALU.mult))
                    V.do(tt(yt[rows, 1, :], ps[rows, bank, :], rope[rows, table + 1, :], ALU.mult))
                    V.join()
                    tt(x, yt[rows, 0, :], yt[rows, 1, :], ALU.add).then_inc(S["roped"], 1)

                def klo():
                    for kv in range(GKV):
                        rows = slice(kv * GD, (kv + 1) * GD)
                        for half in range(2):
                            dve.wait_ge(S["khi"], lay * 4 + 2 * kv + 2)
                            tt(kb[half * GD:(half + 1) * GD, kv, :], cv[rows, 0, :], ka[rows, kv, :].bitcast(F32),
                               ALU.subtract).then_inc(S["klo"], 1)

                def mla_lo(k):
                    dst, src, hi_ = ((uql, uqr, uqh), (ukl, ukr, ukh), (cql, cq, cqh), (ckl, ckv, ckh))[k]
                    dve.wait_ge(S["mhi"], lay * 4 + k + 1)
                    tt(dst[:], src[:], hi_[:].bitcast(F32), ALU.subtract).then_inc(S["mlo"], 1)

                everything = slice(0, P)
                for c in range(DC):
                    operand_lo(lay * 2, col + PM["mix_pre"], c)
                V.do(nc.vector.memset(kr[0:MN, :], 0.0))
                V.do(nc.vector.memset(vg[:, :, GD:2 * GD], 1.0))
                dve.wait_ge(S["rbc_ready"], lay * 2 + 1)
                for t in range(WIN + 2):
                    if t == 0:
                        evac(0, pad[:, 0, 1:T + 1])
                    elif t < C_Q:
                        evac(t, pad[:, t % 2, 1:T + 1])
                    elif t < C_K:
                        evac(t, qf[:, t - C_Q, :])
                    elif t == C_K:
                        evac(t, cv[:, 0, :])
                    elif t == C_V:
                        evac(t, cv[:, 1, :])
                    elif t < C_MKV:
                        evac(t, cq[:, t - C_MQ, :])
                    elif t == C_MKV:
                        evac(t, ckv[:])
                    elif t == C_MKR:
                        V.join()
                        evac(t, kr[MN:MD, :], MR)
                    if 0 <= t - 1 < 4:
                        conv(t - 1)
                    if C_Q <= t - 1 < C_K:
                        norm(t - 1 - C_Q, [(qf[:, t - 1 - C_Q, :], par("gq"))])
                    if t - 1 == C_K:
                        norm(4, [(cv[:, 0, :], par("gk"))])
                    if C_Q <= t - 2 < C_K:
                        rotate(t - 2 - C_Q, qf[:, t - 2 - C_Q, :], everything, 0)
                    if t - 2 == C_K:
                        rotate(4, cv[:, 0, :], everything, 0)
                    if t == C_V + 2:
                        dve.wait_ge(S["vtr"], lay + 1)
                        v = ps[:, 3, :].rearrange("p (s n) -> p s n", s=TC)
                        V.do(copy(vg[:, :, 0:GD], v[:, :, 0:GD]))
                        copy(vg[:, :, 2 * GD:3 * GD], v[:, :, GD:2 * GD]).then_inc(S["vcopy"], 1)
                    if t in (0, 1):
                        taps(2 * t)
                        taps(2 * t + 1)
                    if t in (2, 3):
                        spectrum(2 * (t - 2))
                        spectrum(2 * (t - 2) + 1)
                    if t == 5:
                        h_first(0)
                    if t == 6:
                        h_second(0)
                        conv(4)
                        conv(5)
                    if t == 7:
                        h_gate(0)
                    if t == 9:
                        h_first(1)
                    if t == 11:
                        h_second(1)
                    if t == 13:
                        h_gate(1)
                        klo()
                    if t == 14:
                        mla_lo(0)
                        mla_lo(1)
                    if t == C_MQ + 2:
                        norm(5, [(cq[:, 0, :], par("mqa", 0)), (cq[:, 1, :], par("mqa", 1))])
                    if t == C_MKV + 1:
                        norm(6, [(ckv[:], par("mkva"))])
                gsq_n = [0]

                def group_sum(g):
                    for c in range(GROUPS[g][2]):
                        k = gsq_n[0]
                        gsq_n[0] += 1
                        dve.wait_ge(S["gsq"], lay * DC + k + 1)
                        if c == 0:
                            if g:
                                dve.wait_ge(S["gstat"], lay * 3 + g)
                            copy(acc[:], sq[:, k % 2, :]).then_inc(S["gsq_used"], 1)
                        else:
                            dve.wait_ge(S["gsq_used"], lay * DC + k)
                            tt(acc[:], acc[:], sq[:, k % 2, :], ALU.add).then_inc(S["gsq_used"], 1)

                def group_norm(g):
                    src, _, n, c0 = GROUPS[g]
                    dve.wait_ge(S["gstd"], lay * 3 + g + 1)
                    for c in range(n):
                        stt(out=src[:, c, :], in0=src[:, c, :], scalar=par("g_out", c0 + c), in1=groot[g], op0=ALU.mult,
                            op1=ALU.mult).then_inc(S["y_norm"], 1)

                def group_lo(g):
                    src, _, n, c0 = GROUPS[g]
                    for c in range(n):
                        dve.wait_ge(S["ygh"], lay * DC + c0 + c + 1)
                        tt(yl[:, c0 + c, :], src[:, c, :], yh[:, c0 + c, :].bitcast(F32), ALU.subtract).then_inc(S["ygl"], 1)

                V.do(nc.vector.memset(mv[:, :, :, MV:2 * MV], 1.0))
                def maxima(h):
                    scale = GD ** -0.5 if h < GH else MD ** -0.5
                    for qc in range(TC):
                        dve.wait_ge(S["s_tile"], (lay * HEADS + h) * 4 + qc + 1)
                        V.do(nc.vector.reduce_max(nm[:, h % 2, qc:qc + 1], ps[:, qc, :], AX.X))
                    V.join()
                    ts(ns[:, h % 2, :], nm[:, h % 2, :], -scale, None, ALU.mult).then_inc(S["nmax"], 1)

                def pt_copy(h, sc):
                    dve.wait_ge(S["pt_tile"], (lay * HEADS + h) * 4 + sc + 1)
                    if h >= 2 and sc == 1:
                        dve.wait_ge(S["pv"], lay * HEADS + h - 1)
                    copy(probT[h % 2][:, sc, :], ps[:, 5, :]).then_inc(S["pt_dve"], 1)

                def bank7(k):
                    kind, i = B7[k]
                    dve.wait_ge(S["b7_full"], lay * len(B7) + k + 1)
                    if kind == "q":
                        copy(mqf[0:MD, i, :], ps[0:MD, 7, :]).then_inc(S["b7_free"], 1)
                        dve.wait_ge(S["b7_free"], lay * len(B7) + k + 1)
                    elif kind == "perm":
                        V.do(tt(yt[0:MD, 0, :], mqf[0:MD, i, :], rope[0:MD, 2, :], ALU.mult))
                        V.do(tt(yt[0:MD, 1, :], ps[0:MD, 7, :], rope[0:MD, 3, :], ALU.mult))
                        V.join()
                        tt(mqf[0:MD, i, :], yt[0:MD, 0, :], yt[0:MD, 1, :], ALU.add).then_inc(S["b7_free"], 1)
                    elif kind == "k":
                        copy(mkf[0:MN, i, :], ps[0:MN, 7, :]).then_inc(S["b7_free"], 1)
                    else:
                        v = ps[:, 7, :].rearrange("p (a b n) -> p a b n", a=2, b=2)
                        V.do(copy(mv[:, i, :, 0:MV], v[:, :, 0, MN:MN + MV]))
                        copy(mv[:, i, :, 2 * MV:3 * MV], v[:, :, 1, MN:MN + MV]).then_inc(S["b7_free"], 1)

                def head_out(h):
                    swapped = (h // 4) % 2 if h < GH else h % 2
                    o_rows = slice(GD, 2 * GD) if swapped else slice(0, GD)
                    rows = slice((h % 2) * GD, (h % 2 + 1) * GD)
                    dst = qf[rows, h // 2, :] if h < GH else cq[rows, (h - GH) // 2, :]
                    if h < GH:
                        dve.wait_ge(S["q2lo"], lay * GH + h + 1)
                    dve.wait_ge(S["head_inv"], lay * HEADS + h + 1)
                    tt(dst, ps[o_rows, 6, :], rr[o_rows, h % 2, :], ALU.mult).then_inc(S["y_head"], 1)

                maxima(0)
                mla_lo(2)
                mla_lo(3)
                rotate(5, kr[MN:MD, :], slice(MN, MD), 2, bank=7)
                for h in range(HEADS):
                    if h + 1 < HEADS:
                        maxima(h + 1)
                    pt_copy(h, 1)
                    if h < GH:
                        bank7(2 * h)
                    if h == GH + 3:
                        dve.wait_ge(S["y_head"], lay * HEADS + GH)
                        group_norm(1)
                    if h:
                        head_out(h - 1)
                    pt_copy(h, 3)
                    if h < GH:
                        bank7(2 * h + 1)
                    if h == GH - 1:
                        group_sum(0)
                    if h == GH:
                        group_sum(1)
                    if h == GH + 2:
                        group_norm(0)
                    if h == GH + 3:
                        group_lo(0)
                        group_lo(1)
                head_out(HEADS - 1)
                dve.wait_ge(S["y_head"], lay * HEADS + HEADS)
                group_sum(2)
                group_norm(2)
                group_lo(2)

                for m in range(DC - 1):
                    ysum(lay, 0, m)
                dve.wait_ge(S["rms_post"], lay * 2 + 1)
                for c in range(DC + 2):
                    if c < DC:
                        step(lay, 0, PM["mix_post"], c)
                    if c >= 2:
                        operand_lo(lay * 2 + 1, col + PM["ffn_pre"], c - 2)
                dve.wait_ge(S["rbc_ready"], lay * 2 + 2)

                V.join()
                mark(dve, "dve_marks")
                with dve.Fori(0, FC) as j:
                    V.restart()
                    r = lay * FC + j

                    def f_evac(k):
                        dve.wait_ge(S["pe_item"], lay * ITEMS + j * 2 + (I_UP + k + 3))
                        tt(pad[:, k, 1:T + 1], ps[:, 2 + k, :], rbc[:], ALU.mult).then_inc(S["f_evac"], 1)

                    def f_conv(k):
                        dve.wait_ge(S["f_conv1"], r * 2 + k + 1)
                        c = cv[:, k, :]
                        V.do(stt(out=c, in0=pad[:, k, 0:T], scalar=pm[:, bass.ds(col + j + (PM["ffn_w0"] + k * FC), 1)],
                                 in1=c, op0=ALU.mult, op1=ALU.add))
                        V.join()
                        stt(out=c, in0=pad[:, k, 2:T + 2], scalar=pm[:, bass.ds(col + j + (PM["ffn_w2"] + k * FC), 1)],
                            in1=c, op0=ALU.mult, op1=ALU.add).then_inc(S["f_conv"], 1)

                    f_evac(0)
                    f_conv(0)
                    f_evac(1)
                    f_conv(1)
                    dve.wait_ge(S["f_gelu"], r + 1)
                    dve.wait_ge(S["f_conv"], r * 2 + 2)
                    tt(fprod[:], gact[:], cv[:, 1, :], ALU.mult).then_inc(S["f_prod"], 1)
                    dve.wait_ge(S["f_hi"], r + 1)
                    tt(fl[:, bass.ds(j, 1), :], fprod[:].rearrange("p (o t) -> p o t", o=1),
                       fh[:, bass.ds(j, 1), :].bitcast(F32), ALU.subtract).then_inc(S["f_lo"], 1)
                    V.join()
                    mark(dve, "dve_marks")

                V.restart()
                for m in range(DC - 1):
                    ysum(lay, 1, m)
                dve.wait_ge(S["rms_post"], lay * 2 + 2)
                for c in range(DC):
                    step(lay, 1, PM["ffn_post"], c)
                V.join()
                mark(dve, "dve_marks")


def constants():
    c = {}
    c["c_ident"] = np.eye(P, dtype=np.float32)
    c["c_b64"] = np.kron(np.eye(2), np.ones((GD, GD))).astype(np.float32)

    def swap(n, at, total):
        m = np.zeros((total, total), np.float32)
        for i in range(n):
            m[at + n + i, at + i] = -1.0
            m[at + i, at + n + i] = 1.0
        return m

    c["c_perm_g"] = swap(GD // 2, 0, P) + swap(GD // 2, GD, P)
    c["c_perm_m"] = swap(MR // 2, MN, MD)
    rows, cols = np.divmod(np.arange(T), GRID_W)

    def angles(rot):
        n = rot // 4
        inv = (np.float32(10000.0) ** (-np.arange(n, dtype=np.float32) / np.float32(n))).astype(np.float32)
        ang = np.concatenate([rows[:, None].astype(np.float32) * inv, cols[:, None].astype(np.float32) * inv], -1)
        return ang.astype(np.float64)

    rope = np.zeros((P, 4, T), np.float32)
    g, m = angles(GD), angles(MR)
    for i in range(4):
        rope[i * GD // 2:(i + 1) * GD // 2, 0] = np.cos(g).T
        rope[i * GD // 2:(i + 1) * GD // 2, 1] = np.sin(g).T
    rope[:MN, 2] = 1.0
    for i in range(2):
        at = MN + i * MR // 2
        rope[at:at + MR // 2, 2] = np.cos(m).T
        rope[at:at + MR // 2, 3] = np.sin(m).T
    c["c_rope"] = rope
    bands = (HEMB - 1) // 2
    t = np.linspace(0.0, 1.0, T, dtype=np.float32)[:, None]
    w = (np.float32(2.0 * np.pi) * np.arange(T, dtype=np.float32)[:, None] / np.float32(T)).astype(np.float32)
    f = np.linspace(1e-4, bands - 1, bands, dtype=np.float32)[None, :]
    fw = (f * w).astype(np.float32).astype(np.float64)
    c["c_z"] = np.ascontiguousarray(np.concatenate([t, np.cos(fw), -np.sin(fw)], -1).astype(np.float32).T)
    lo, hi = np.log(1e-2) / 1.5, np.log(1e-2) / 0.3
    deltas = np.linspace(lo, hi, HD, dtype=np.float32)
    window = np.exp((-t * np.abs(deltas)[None, :]).astype(np.float64)).astype(np.float32)
    late = np.concatenate([np.zeros((1, HD), np.float32), window[:-1]])
    tiles = lambda x: x.reshape(2, P, 2, HD).transpose(1, 2, 0, 3).reshape(P, 4, HD)
    c["c_win"] = np.ascontiguousarray(np.stack([tiles(window), tiles(late)], 1))
    theta = np.pi * (2 * np.arange(NF) + 1) / (2 * T)
    tf = np.zeros((P, 2, 2, T), np.float32)
    ti = np.zeros((P, 2, 4, NF), np.float32)
    for par in range(2):
        ang = np.outer(2 * np.arange(NF) + par, theta)
        fwd = np.concatenate([np.cos(ang), -np.sin(ang)], 1)
        for k in range(2):
            tf[:, par, k] = fwd[k * P:(k + 1) * P]
        inv = np.stack([np.cos(ang).T, -np.sin(ang).T]) / T
        ti[:, par] = inv.reshape(2, 2, P, NF).transpose(2, 0, 1, 3).reshape(P, 4, NF)
    c["c_tf"], c["c_ti"] = tf, ti
    return c


NAMES = ['x', 'mix_pre_norm', 'w_in', 'hy_conv_w', 'hy_conv_b', 'hy_filt_w1', 'hy_filt_b1', 'hy_filt_freq1',
         'hy_filt_w2', 'hy_filt_b2', 'hy_filt_freq2', 'hy_filt_w3', 'hy_skip', 'gqa_q_norm', 'gqa_k_norm',
         'mla_q_a_norm', 'mla_w_uq', 'mla_kv_a_norm', 'mla_w_ukv', 'hy_out_norm', 'gqa_out_norm', 'mla_out_norm',
         'w_out', 'mix_post_norm', 'ffn_pre_norm', 'w_up', 'ffn_conv_w', 'ffn_conv_b', 'w_down', 'ffn_post_norm']


def kernel(**inputs):
    import concourse.bacc as bacc
    from concourse.bass_utils import run_bass_kernel_spmd

    nc = bacc.Bacc("TRN2", target_bir_lowering=False, num_devices=1, dynamic_dma_scratch_size=1024)
    arrays = {n: np.ascontiguousarray(inputs[n]) for n in NAMES}
    arrays.update(constants())
    aps = {n: nc.dram_tensor(n, v.shape, F32, kind="ExternalInput").ap() for n, v in arrays.items()}
    out = nc.dram_tensor("out", (1, T, DM), F32, kind="ExternalOutput").ap()
    build(nc, aps, out)
    r = run_bass_kernel_spmd(nc, [arrays], core_ids=[0])
    return r.results[0]["out"]
```
